# Optimizing a Trainium2 kernel written in Bass

```python
import math
import jax, jax.numpy as jnp
from jax import lax
import numpy as np

D_MODEL = 1024
BATCH = 1
SEQ = 512
DEPTH = 2

CHUNK = 64
D_MIX = 2 * D_MODEL
D_BRANCH = D_MIX // 4
EPS = 1e-6

SWA_HEADS = 8
SWA_KV_HEADS = 2
SWA_HEAD_DIM = D_BRANCH // SWA_HEADS
WINDOW = 128
WINDOW_CHUNKS = WINDOW // CHUNK
ROPE_THETA = 500000.0
ROPE_DIM = SWA_HEAD_DIM // 4

GLA_HEADS = 4
GLA_KEY_DIM = D_BRANCH // 2 // GLA_HEADS
GLA_VAL_DIM = D_BRANCH // GLA_HEADS
GLA_GATE_RANK = 16
GLA_GATE_TAU = 16.0

SSD_HEADS = 8
SSD_HEAD_DIM = D_BRANCH // SSD_HEADS
SSD_GROUPS = 2
SSD_STATE = 128
SSD_CONV = 4
SSD_CONV_CH = D_BRANCH + 2 * SSD_GROUPS * SSD_STATE

MLSTM_HEADS = 4
MLSTM_HEAD_DIM = D_BRANCH // MLSTM_HEADS
MLSTM_CONV = 4

SWA_COLS = [D_BRANCH, SWA_KV_HEADS * SWA_HEAD_DIM, SWA_KV_HEADS * SWA_HEAD_DIM, D_BRANCH]
GLA_COLS = [GLA_HEADS * GLA_KEY_DIM, GLA_HEADS * GLA_KEY_DIM, D_BRANCH, D_BRANCH, GLA_GATE_RANK]
SSD_COLS = [SSD_CONV_CH, SSD_HEADS, D_BRANCH]
MLSTM_COLS = [D_BRANCH, D_BRANCH, D_BRANCH, MLSTM_HEADS, MLSTM_HEADS, D_BRANCH, D_BRANCH]
IN_SPLITS = SWA_COLS + GLA_COLS + SSD_COLS + MLSTM_COLS
N_IN = sum(IN_SPLITS)

kernel_name = "hybrid_parallel_group_streaming_encoder"

def _split(u, sizes):
    idx = [int(i) for i in np.cumsum(sizes)[:-1]]
    return jnp.split(u, idx, axis=-1)

def rms_norm(x, g):
    x32 = x.astype(jnp.float32)
    y = x32 * lax.rsqrt(jnp.mean(x32 * x32, axis=-1, keepdims=True) + EPS)
    return (y * g.astype(jnp.float32)).astype(x.dtype)

def causal_conv(u, w, b):
    k = w.shape[0]
    out = lax.conv_general_dilated(
        u, w[:, None, :].astype(u.dtype), window_strides=(1,), padding=[(k - 1, 0)],
        dimension_numbers=('NWC', 'WIO', 'NWC'), feature_group_count=u.shape[-1])
    return out + b.astype(u.dtype)

def partial_rope(x, cos, sin):
    half = ROPE_DIM // 2
    x1, x2, rest = x[..., :half], x[..., half:ROPE_DIM], x[..., ROPE_DIM:]
    return jnp.concatenate([x1 * cos - x2 * sin, x2 * cos + x1 * sin, rest], axis=-1)

def _to_chunks(t):
    bsz, seq, nh = t.shape[:3]
    t = t.reshape((bsz, seq // CHUNK, CHUNK, nh) + t.shape[3:])
    return jnp.swapaxes(jnp.moveaxis(t, 1, 0), 2, 3)

def _from_chunks(o):
    nc, bsz, nh, _, d = o.shape
    return jnp.moveaxis(jnp.swapaxes(o, 2, 3), 0, 1).reshape(bsz, nc * CHUNK, nh, d)

def sink_window_attention(q, k, v, sinks):
    bsz, seq = q.shape[:2]
    nc = seq // CHUNK
    grp = SWA_HEADS // SWA_KV_HEADS
    qc = q.reshape(bsz, nc, CHUNK, SWA_KV_HEADS, grp, SWA_HEAD_DIM)
    kc = k.reshape(bsz, nc, CHUNK, SWA_KV_HEADS, SWA_HEAD_DIM)
    vc = v.reshape(bsz, nc, CHUNK, SWA_KV_HEADS, SWA_HEAD_DIM)

    def band(t):
        pad = jnp.pad(t, ((0, 0), (WINDOW_CHUNKS - 1, 0)) + ((0, 0),) * (t.ndim - 2))
        return jnp.concatenate([pad[:, i:i + nc] for i in range(WINDOW_CHUNKS)], axis=2)

    kb, vb = band(kc), band(vc)
    key_chunk = (jnp.arange(nc)[:, None] - (WINDOW_CHUNKS - 1)
                 + jnp.arange(WINDOW_CHUNKS)[None, :])
    valid = jnp.repeat(key_chunk >= 0, CHUNK, axis=1)
    s = jnp.einsum('bcqhgd,bckhd->bchgqk', qc, kb).astype(jnp.float32) * (SWA_HEAD_DIM ** -0.5)
    s = jnp.where(valid[None, :, None, None, None, :], s, -jnp.inf)
    sink = sinks.astype(jnp.float32).reshape(SWA_KV_HEADS, grp)[None, None, :, :, None, None]
    m = jnp.maximum(jnp.max(s, axis=-1, keepdims=True), sink)
    p = jnp.exp(s - m)
    p = p / (jnp.sum(p, axis=-1, keepdims=True) + jnp.exp(sink - m))
    o = jnp.einsum('bchgqk,bckhd->bcqhgd', p.astype(v.dtype), vb)
    return o.reshape(bsz, seq, SWA_HEADS * SWA_HEAD_DIM)

def swa_branch(q, k, v, z, sinks, cos, sin):
    bsz, seq = q.shape[:2]
    q = partial_rope(q.reshape(bsz, seq, SWA_HEADS, SWA_HEAD_DIM), cos, sin)
    k = partial_rope(k.reshape(bsz, seq, SWA_KV_HEADS, SWA_HEAD_DIM), cos, sin)
    v = v.reshape(bsz, seq, SWA_KV_HEADS, SWA_HEAD_DIM)
    return sink_window_attention(q, k, v, sinks) * jax.nn.silu(z)

def gla_chunked(q, k, v, log_a):
    bsz, _, nh, dk = q.shape
    dv = v.shape[-1]
    tril = jnp.tril(jnp.ones((CHUNK, CHUNK), dtype=bool))

    def step(state, inp):
        qc, kc, vc, gc = inp
        b = jnp.cumsum(gc, axis=2)
        o_inter = jnp.einsum('bhlk,bhkv->bhlv', qc * jnp.exp(b), state)
        diff = jnp.where(tril[:, :, None], b[:, :, :, None, :] - b[:, :, None, :, :], -jnp.inf)
        att = jnp.einsum('bhlk,bhsk,bhlsk->bhls', qc, kc, jnp.exp(diff))
        o = o_inter + jnp.einsum('bhls,bhsv->bhlv', att, vc)
        b_last = b[:, :, -1:, :]
        new_state = (jnp.exp(b_last[:, :, 0, :])[..., None] * state
                     + jnp.einsum('bhsk,bhsv->bhkv', kc * jnp.exp(b_last - b), vc))
        return new_state, o

    s0 = jnp.zeros((bsz, nh, dk, dv), jnp.float32)
    _, o = lax.scan(step, s0, (_to_chunks(q), _to_chunks(k), _to_chunks(v), _to_chunks(log_a)))
    return _from_chunks(o)

def gla_branch(q, k, v, z, lr, w_gate, b_gate, norm_g):
    bsz, seq = q.shape[:2]
    f32 = jnp.float32
    log_a = jax.nn.log_sigmoid((lr @ w_gate + b_gate).astype(f32)) / GLA_GATE_TAU
    shp_k = (bsz, seq, GLA_HEADS, GLA_KEY_DIM)
    o = gla_chunked(q.reshape(shp_k).astype(f32) * (GLA_KEY_DIM ** -0.5),
                    k.reshape(shp_k).astype(f32),
                    v.reshape(bsz, seq, GLA_HEADS, GLA_VAL_DIM).astype(f32),
                    log_a.reshape(shp_k))
    o = rms_norm(o, norm_g).astype(z.dtype)
    return o.reshape(bsz, seq, D_BRANCH) * jax.nn.silu(z)

def ssd_chunked(xs, dt, a, bm, cm):
    bsz, seq = xs.shape[:2]
    nc = seq // CHUNK
    hpg = SSD_HEADS // SSD_GROUPS
    xdt = (xs * dt[..., None]).reshape(bsz, nc, CHUNK, SSD_GROUPS, hpg, SSD_HEAD_DIM)
    da = (dt * a).reshape(bsz, nc, CHUNK, SSD_GROUPS, hpg).transpose(0, 1, 3, 4, 2)
    acs = jnp.cumsum(da, axis=-1)
    bc = bm.reshape(bsz, nc, CHUNK, SSD_GROUPS, SSD_STATE)
    cc = cm.reshape(bsz, nc, CHUNK, SSD_GROUPS, SSD_STATE)
    tril = jnp.tril(jnp.ones((CHUNK, CHUNK), dtype=bool))
    lmat = jnp.exp(jnp.where(tril, acs[..., :, None] - acs[..., None, :], -jnp.inf))
    cb = jnp.einsum('bclgn,bcsgn->bcgls', cc, bc)
    y_diag = jnp.einsum('bcgls,bcgjls,bcsgjp->bclgjp', cb, lmat, xdt)
    decay_states = jnp.exp(acs[..., -1:] - acs)
    states = jnp.einsum('bcsgn,bcgjs,bcsgjp->bcgjpn', bc, decay_states, xdt)
    chunk_decay = jnp.exp(acs[..., -1])

    def step(h, inp):
        st, dec = inp
        return dec[..., None, None] * h + st, h

    h0 = jnp.zeros((bsz, SSD_GROUPS, hpg, SSD_HEAD_DIM, SSD_STATE), jnp.float32)
    _, prev = lax.scan(step, h0, (jnp.moveaxis(states, 1, 0), jnp.moveaxis(chunk_decay, 1, 0)))
    prev = jnp.moveaxis(prev, 0, 1)
    y_off = jnp.einsum('bclgn,bcgjpn,bcgjl->bclgjp', cc, prev, jnp.exp(acs))
    return (y_diag + y_off).reshape(bsz, seq, SSD_HEADS, SSD_HEAD_DIM)

def ssd_branch(xbc, dt_raw, z, conv_w, conv_b, dt_bias, a_log, d_skip, norm_g):
    bsz, seq = xbc.shape[:2]
    f32 = jnp.float32
    xbc = jax.nn.silu(causal_conv(xbc, conv_w, conv_b))
    xs, bm, cm = _split(xbc, [D_BRANCH, SSD_GROUPS * SSD_STATE, SSD_GROUPS * SSD_STATE])
    xs = xs.reshape(bsz, seq, SSD_HEADS, SSD_HEAD_DIM).astype(f32)
    dt = jax.nn.softplus(dt_raw.astype(f32) + dt_bias.astype(f32))
    a = -jnp.exp(a_log.astype(f32))
    y = ssd_chunked(xs, dt, a,
                    bm.reshape(bsz, seq, SSD_GROUPS, SSD_STATE).astype(f32),
                    cm.reshape(bsz, seq, SSD_GROUPS, SSD_STATE).astype(f32))
    y = y + d_skip.astype(f32)[:, None] * xs
    y = y.reshape(bsz, seq, D_BRANCH).astype(z.dtype) * jax.nn.silu(z)
    y = rms_norm(y.reshape(bsz, seq, SSD_GROUPS, D_BRANCH // SSD_GROUPS),
                 norm_g.reshape(SSD_GROUPS, D_BRANCH // SSD_GROUPS))
    return y.reshape(bsz, seq, D_BRANCH)

def mlstm_chunked(q, k, v, ig, lf):
    bsz, _, nh, dk = q.shape
    dv = v.shape[-1]
    tril = jnp.tril(jnp.ones((CHUNK, CHUNK), dtype=bool))

    def step(carry, inp):
        cmat, nvec, m = carry
        qc, kc, vc, ic, fc = inp
        b = jnp.cumsum(fc, axis=-1)
        log_d = jnp.where(tril, b[..., :, None] - b[..., None, :] + ic[..., None, :], -jnp.inf)
        log_inter = b + m[..., None]
        m_t = jnp.maximum(jnp.max(log_d, axis=-1), log_inter)
        w_intra = jnp.exp(log_d - m_t[..., None])
        w_inter = jnp.exp(log_inter - m_t)
        p = jnp.einsum('bhld,bhsd->bhls', qc, kc) * w_intra
        num = (jnp.einsum('bhls,bhsv->bhlv', p, vc)
               + w_inter[..., None] * jnp.einsum('bhld,bhdv->bhlv', qc, cmat))
        den = jnp.sum(p, axis=-1) + w_inter * jnp.einsum('bhld,bhd->bhl', qc, nvec)
        h = num / jnp.maximum(jnp.abs(den), jnp.exp(-m_t))[..., None]
        b_last = b[..., -1]
        log_end = b_last[..., None] - b + ic
        m_new = jnp.maximum(b_last + m, jnp.max(log_end, axis=-1))
        w_end = jnp.exp(log_end - m_new[..., None])
        decay = jnp.exp(b_last + m - m_new)
        cmat = decay[..., None, None] * cmat + jnp.einsum('bhs,bhsd,bhsv->bhdv', w_end, kc, vc)
        nvec = decay[..., None] * nvec + jnp.einsum('bhs,bhsd->bhd', w_end, kc)
        return (cmat, nvec, m_new), h

    carry0 = (jnp.zeros((bsz, nh, dk, dv), jnp.float32),
              jnp.zeros((bsz, nh, dk), jnp.float32),
              jnp.zeros((bsz, nh), jnp.float32))
    _, h = lax.scan(step, carry0, (_to_chunks(q), _to_chunks(k), _to_chunks(v),
                                   _to_chunks(ig), _to_chunks(lf)))
    return _from_chunks(h)

def mlstm_branch(q, k, v, i_raw, f_raw, o_raw, z, conv_w, conv_b, i_bias, f_bias, norm_g):
    bsz, seq = q.shape[:2]
    f32 = jnp.float32
    qk = jax.nn.silu(causal_conv(jnp.concatenate([q, k], axis=-1), conv_w, conv_b))
    q, k = _split(qk, [D_BRANCH, D_BRANCH])
    shp = (bsz, seq, MLSTM_HEADS, MLSTM_HEAD_DIM)
    ig = i_raw.astype(f32) + i_bias.astype(f32)
    lf = jax.nn.log_sigmoid(f_raw.astype(f32) + f_bias.astype(f32))
    h = mlstm_chunked(q.reshape(shp).astype(f32),
                      k.reshape(shp).astype(f32) * (MLSTM_HEAD_DIM ** -0.5),
                      v.reshape(shp).astype(f32), ig, lf)
    h = jax.nn.sigmoid(o_raw.astype(f32)).reshape(shp) * h
    h = rms_norm(h, norm_g.reshape(MLSTM_HEADS, MLSTM_HEAD_DIM)).astype(z.dtype)
    return h.reshape(bsz, seq, D_BRANCH) * jax.nn.silu(z)

def setup_inputs(seed: int = 0) -> dict:
    key = jax.random.key(seed)
    ks = jax.random.split(key, 32)
    f32 = jnp.float32

    def nrm(k, shape, scale):
        return jax.random.normal(k, shape, f32) * scale

    x = nrm(ks[0], (BATCH, SEQ, D_MODEL), 1.0)
    c = nrm(ks[1], (BATCH, D_MODEL), 1.0)
    positions = (jax.random.randint(ks[2], (BATCH, 1), 0, SEQ, dtype=jnp.int32)
                 + jnp.arange(SEQ, dtype=jnp.int32)[None, :])
    norm_g = 1.0 + nrm(ks[3], (DEPTH, D_MODEL), 0.02)
    w_ada = nrm(ks[4], (DEPTH, D_MODEL, 3 * D_MODEL), 0.5 * D_MODEL ** -0.5)
    b_ada = nrm(ks[5], (DEPTH, 3 * D_MODEL), 0.02)
    w_in = nrm(ks[6], (DEPTH, D_MODEL, N_IN), D_MODEL ** -0.5)
    swa_sinks = nrm(ks[7], (DEPTH, SWA_HEADS), 0.5)
    gla_w_gate = nrm(ks[8], (DEPTH, GLA_GATE_RANK, GLA_HEADS * GLA_KEY_DIM), GLA_GATE_RANK ** -0.5)
    gla_b_gate = nrm(ks[9], (DEPTH, GLA_HEADS * GLA_KEY_DIM), 0.1)
    gla_norm_g = 1.0 + nrm(ks[10], (DEPTH, GLA_VAL_DIM), 0.02)
    ssd_conv_w = nrm(ks[11], (DEPTH, SSD_CONV, SSD_CONV_CH), SSD_CONV ** -0.5)
    ssd_conv_b = nrm(ks[12], (DEPTH, SSD_CONV_CH), 0.02)
    dt0 = jnp.exp(jax.random.uniform(ks[13], (DEPTH, SSD_HEADS), f32, math.log(1e-3), math.log(1e-1)))
    ssd_dt_bias = dt0 + jnp.log(-jnp.expm1(-dt0))
    ssd_a_log = jnp.log(jax.random.uniform(ks[14], (DEPTH, SSD_HEADS), f32, 1.0, 16.0))
    ssd_d = 1.0 + nrm(ks[15], (DEPTH, SSD_HEADS), 0.1)
    ssd_norm_g = 1.0 + nrm(ks[16], (DEPTH, D_BRANCH), 0.02)
    mlstm_conv_w = nrm(ks[17], (DEPTH, MLSTM_CONV, 2 * D_BRANCH), MLSTM_CONV ** -0.5)
    mlstm_conv_b = nrm(ks[18], (DEPTH, 2 * D_BRANCH), 0.02)
    mlstm_i_bias = nrm(ks[19], (DEPTH, MLSTM_HEADS), 0.1)
    mlstm_f_bias = (jnp.linspace(3.0, 6.0, MLSTM_HEADS, dtype=f32)[None, :]
                    + nrm(ks[20], (DEPTH, MLSTM_HEADS), 0.1))
    mlstm_norm_g = 1.0 + nrm(ks[21], (DEPTH, D_BRANCH), 0.02)
    w_out = nrm(ks[22], (DEPTH, D_MIX, D_MODEL), D_MIX ** -0.5)
    final_g = 1.0 + nrm(ks[23], (D_MODEL,), 0.02)
    return {"x": x, "c": c, "positions": positions, "norm_g": norm_g, "w_ada": w_ada,
            "b_ada": b_ada, "w_in": w_in, "swa_sinks": swa_sinks, "gla_w_gate": gla_w_gate,
            "gla_b_gate": gla_b_gate, "gla_norm_g": gla_norm_g, "ssd_conv_w": ssd_conv_w,
            "ssd_conv_b": ssd_conv_b, "ssd_dt_bias": ssd_dt_bias, "ssd_a_log": ssd_a_log,
            "ssd_d": ssd_d, "ssd_norm_g": ssd_norm_g, "mlstm_conv_w": mlstm_conv_w,
            "mlstm_conv_b": mlstm_conv_b, "mlstm_i_bias": mlstm_i_bias,
            "mlstm_f_bias": mlstm_f_bias, "mlstm_norm_g": mlstm_norm_g, "w_out": w_out,
            "final_g": final_g}

def reference(x, c, positions, norm_g, w_ada, b_ada, w_in, swa_sinks, gla_w_gate, gla_b_gate,
              gla_norm_g, ssd_conv_w, ssd_conv_b, ssd_dt_bias, ssd_a_log, ssd_d, ssd_norm_g,
              mlstm_conv_w, mlstm_conv_b, mlstm_i_bias, mlstm_f_bias, mlstm_norm_g, w_out,
              final_g):
    inv_freq = ROPE_THETA ** (-jnp.arange(0, ROPE_DIM, 2, dtype=jnp.float32) / ROPE_DIM)
    ang = positions.astype(jnp.float32)[..., None] * inv_freq
    cos = jnp.cos(ang)[:, :, None, :].astype(x.dtype)
    sin = jnp.sin(ang)[:, :, None, :].astype(x.dtype)
    c_act = jax.nn.silu(c)

    for l in range(DEPTH):
        mod = c_act @ w_ada[l] + b_ada[l]
        shift, scale, gate = jnp.split(mod, 3, axis=-1)
        h = rms_norm(x, norm_g[l]) * (1.0 + scale[:, None, :]) + shift[:, None, :]
        u = h @ w_in[l]
        (sq, sk, sv, sz, gq, gk, gv, gz, glr, sxbc, sdt, ssz,
         mq, mk, mv, mi, mf, mo, mz) = _split(u, IN_SPLITS)
        y_a = swa_branch(sq, sk, sv, sz, swa_sinks[l], cos, sin)
        y_b = gla_branch(gq, gk, gv, gz, glr, gla_w_gate[l], gla_b_gate[l], gla_norm_g[l])
        y_c = ssd_branch(sxbc, sdt, ssz, ssd_conv_w[l], ssd_conv_b[l], ssd_dt_bias[l],
                         ssd_a_log[l], ssd_d[l], ssd_norm_g[l])
        y_d = mlstm_branch(mq, mk, mv, mi, mf, mo, mz, mlstm_conv_w[l], mlstm_conv_b[l],
                           mlstm_i_bias[l], mlstm_f_bias[l], mlstm_norm_g[l])
        y = jnp.concatenate([y_a, y_b, y_c, y_d], axis=-1)
        x = x + gate[:, None, :] * (y @ w_out[l])
    return rms_norm(x, final_g)


_drawn_inputs = setup_inputs


def setup_inputs(seed=0):
    import zlib

    import numpy as np

    out = dict(_drawn_inputs(seed))
    spreads = {}
    factors = {'norm_g': 6.358,
     'swa_sinks': 8.0,
     'gla_b_gate': 8.0,
     'gla_norm_g': 8.0,
     'ssd_conv_b': 34.075,
     'ssd_d': 200.0,
     'ssd_norm_g': 50.478,
     'mlstm_conv_b': 64.0,
     'mlstm_i_bias': 200.0,
     'mlstm_norm_g': 8.0,
     'final_g': 26.706}
    for name, (base, spread) in spreads.items():
        noise = np.random.default_rng([zlib.crc32(name.encode()), seed]).standard_normal(out[name].shape)
        drawn = base * np.exp(spread * noise) if base else spread * noise
        out[name] = __import__('jax').numpy.asarray(drawn.astype(out[name].dtype))
    for name, factor in factors.items():
        out[name] = (out[name] * factor).astype(out[name].dtype)
    return out
```

```python
from contextlib import ExitStack

import numpy as np

import concourse.bass as bass
from concourse import mybir

F32 = mybir.dt.float32
F32R = mybir.dt.float32r
I32 = mybir.dt.int32
U8 = mybir.dt.uint8
ALU = mybir.AluOpType
ACT = mybir.ActivationFunctionType
AX_X = mybir.AxisListType.X

P = 128
D_MODEL = 1024
SEQ = 512
DEPTH = 2
EPS = 1e-6
KT_IN = D_MODEL // P
C = 128
NC = SEQ // C
D_BRANCH = 512
BT = D_BRANCH // P
NB = 8
WIN = 64
ROPE_THETA = 500000.0
ROPE_DIM = 16
LEVELS = [64, 32, 16, 8, 4, 2, 1]

IN_SPLITS = [512, 128, 128, 512, 256, 256, 512, 512, 16, 1024, 8, 512, 512, 512, 512, 4, 4, 512, 512]
IN_NAMES = ["aq", "ak", "av", "az", "gq", "gk", "gv", "gz", "lr", "xbc", "dt", "cz",
            "mq", "mk", "mv", "mi", "mf", "mo", "mz"]
IN_OFF = dict(zip(IN_NAMES, np.cumsum([0] + IN_SPLITS[:-1]).tolist()))

ORDER = ["m", "c", "g", "a"]
Y_TILE = {"m": 0, "c": 4, "g": 8, "a": 12}
Y_ROW = {"a": 0, "g": 512, "c": 1024, "m": 1536}
N_EARLY = 12

R_DT, R_I, R_LR, R_F = 0, 32, 64, 96
T_C, T_R, T_R2, T_ACS = 0, 32, 64, 96

COL = {}
_n = 0
for _name, _w in [("norm_g", 8), ("b_ada", 24), ("gla_b", 2), ("gla_g", 1), ("ssd_g", 4), ("m_g", 4),
                  ("conv_b", 16), ("conv_w", 64), ("ssd_d", 4), ("gate_b", 1), ("a_log", 1), ("sinks", 8)]:
    COL[_name] = _n
    _n += _w
N_COLS = _n

TILE_W = 1024
RING = 4
SPLIT_RING = 3
ADA_EARLY = 8
ADA_SLOTS = 6
ADA_SLOT = [0, 1, 2, 3, 4, 5, 0, 1, 4, 5, 4, 5]


def between(steps, fill):
    out, n = [], 0
    for i, s in enumerate(steps):
        out.append(s)
        want = (i + 1) * len(fill) // len(steps)
        out += fill[n:want]
        n = want
    return out


def make_schedule():
    def proj(name, n=4):
        return [("proj", name, t) for t in range(n)]

    s = [("norm",)] + [("ada", j) for j in range(8)] + [("modulate",), ("proj", "gate", 0), ("rows",), ("proj", "ak", 0), ("rope", "ak", 0),
         ("proj", "av", 0), ("av",)]
    s += between(proj("mq") + proj("mk"), [("ada", j) for j in range(ADA_EARLY, 12)]) + [("vtok", "mv")]
    m = [("tok",), ("mk_tok",)]
    m += [("m_qk", 0), ("m_state", 0), ("m_decay", 0), ("m_state", 1), ("m_qk", 1), ("m_state", 2), ("m_decay", 1),
          ("m_num", 0), ("m_qk", 2), ("m_decay", 2), ("m_num", 1), ("m_qk", 3), ("m_decay", 3), ("m_num", 2),
          ("m_num", 3), ("m_norm",)]
    s += between(m, proj("mo") + proj("mz") + proj("xs") + proj("bc") + proj("cz"))
    c = [("c_cb", 0), ("c_cb", 1), ("c_x", 0), ("c_x", 1), ("c_x", 2), ("c_x", 3), ("c_b", 0), ("c_b", 1),
         ("c_state", 0), ("c_state", 1), ("c_state", 2)]
    for t in range(4):
        c += [("c_decay", 2 * t), ("c_decay", 2 * t + 1)]
        if t:
            c += [("c_y", t - 1)]
    c += [("c_y", 3), ("c_norm", 0), ("c_norm", 1)]
    s += between(c, proj("gq", 2) + proj("gk", 2) + [("vtok", "gv")])
    g = [("g_gate",), ("g_decay",), ("g_ktok",), ("g_diag",)]
    g += [("g_state", p) for p in range(3)]
    for i in range(len(LEVELS)):
        g += [("g_level", i)] + ([("g_merge", i - 1)] if i else [])
    g += [("g_merge", len(LEVELS) - 1)]
    g += [("g_out", h) for h in range(4)] + [("y_split", 0), ("g_norm",), ("y_split", 1)]
    s += between(g, proj("gz") + [x for t in range(4) for x in (("proj", "aq", t), ("rope", "aq", t))] + proj("az"))
    a = [("a_s", 0), ("a_s", 1), ("a_pt", 0), ("a_s", 2), ("a_pv", 0), ("a_pt", 1), ("a_s", 3), ("a_pv", 1),
         ("a_pt", 2), ("a_pv", 2), ("a_pt", 3), ("a_pv", 3)]
    s += between(a, [("out1", j) for j in range(8)])
    s += [("out2", j) for j in range(8)]
    return s


SCHEDULE = make_schedule()


def tiles_of(step):
    kind = step[0]
    one = {"norm": 1, "ada": 1, "proj": 1, "av": 1, "rope": 1, "m_qk": 2, "m_decay": 2, "m_state": 2, "m_num": 2,
           "c_cb": 1, "c_x": 1, "c_b": 1, "c_state": 1, "c_decay": 1, "c_norm": 1, "g_ktok": 2, "g_gate": 2,
           "g_state": 1, "g_level": 2, "g_out": 1, "a_s": 2, "a_pt": 2, "a_pv": 1, "out1": 1, "out2": 1,
           "tok": 3, "mk_tok": 3, "vtok": 4, "m_norm": 4, "g_norm": 4, "g_diag": 4, "c_y": 3,
           "modulate": 0, "rows": 0, "y_split": 0, "g_decay": 0, "g_merge": 0}
    return [step + (i,) for i in range(one[kind])]


TILE = {}
for _step in SCHEDULE:
    for _key in tiles_of(_step):
        TILE[_key] = (len(TILE) % NB, len(TILE) // NB)

def weights_of(step):
    kind, arg = step[0], step[1:]
    if kind == "proj":
        return [arg]
    if kind == "vtok":
        return [(arg[0], q) for q in range(4)]
    if kind == "out1":
        return [("o1", arg[0], i) for i in range(2)]
    if kind == "out2" and arg[0] % 2 == 0:
        return [("o2", arg[0] // 2)]
    return []


SPLITS = [w for s in SCHEDULE for w in weights_of(s)]
SPLIT_NO = {w: i for i, w in enumerate(SPLITS)}
WIDTH = {("o1", j, 1): 512 for j in range(8)}

USED_BY = {}
_n = 0
for _w in SPLITS:
    if _w[0] in ("mv", "gv") and _w[1] < 3 or _w[0] == "o1" and _w[2] == 0:
        _n += 1
        USED_BY[_w] = _n
    else:
        USED_BY[_w] = {"mv": ("vtok", _w[0], 3), "gv": ("vtok", _w[0], 3), "o1": ("out1", _w[1], 0),
                       "o2": ("out2", 2 * _w[1] + 1, 0)}.get(_w[0], ("proj",) + _w + (0,))


def releases(step):
    if step[0] == "out2":
        return [("o2", step[1] // 2)] if step[1] % 2 else []
    return weights_of(step)


def next_splits(step):
    n = [SPLIT_NO[w] + SPLIT_RING for w in releases(step)]
    n = [i if i < len(SPLITS) else None for i in n]
    return [i for i in n[:-1] if i is not None], [i for i in n[-1:] if i is not None]


ADA_BEFORE = {6: 8, 7: 9, 9: 10, 11: 11}
LAST_PROJ = max(i for i, w in enumerate(SPLITS) if w[0] not in ("o1", "o2"))
Y_SLOT = [10, 11, 12, 13, 14, 15, 4, 5, 6, 7, 8, 9, 0, 1, 2, 3]


def order_of(kinds):
    seen = [s[1:] for s in SCHEDULE if s[0] == "proj" and s[1] in kinds]
    return {k: i for i, k in enumerate(seen)}


CONV_NAMES = ("mq", "mk", "xs", "bc")
SILUS = order_of(CONV_NAMES + ("mz", "cz", "gz", "az"))
CONVS = order_of(CONV_NAMES)
CONV_TILE = {("xs", t): t for t in range(4)} | {("bc", t): 4 + t for t in range(4)} \
    | {("mq", t): 8 + t for t in range(4)} | {("mk", t): 12 + t for t in range(4)}
Z_OF = {"mz": "m", "cz": "c", "gz": "g", "az": "a"}
ROPES = {("ak", 0): 0} | {("aq", t): 1 + t for t in range(4)}

TWO_PI = 2.0 * np.pi
PI_HI = 6.28125
PI_MID = float(np.float32(np.floor((TWO_PI - PI_HI) * 2 ** 21) / 2 ** 21))
PI_LO = float(np.float32(TWO_PI - PI_HI - PI_MID))
ROUND = 12582912.0
PI_CLIP = 3.1415925


def bcast(ap, n):
    shape = list(ap.shape)
    return ap.unsqueeze(len(shape)).broadcast_to(shape + [n])


def mid_bcast(ap, n):
    p, a = ap.shape
    return ap.unsqueeze(1).broadcast_to([p, n, a])


def build(nc, xT_in, c_in, pos_in, cols_in, wgate_in, final_in, ada_in, weights, consts_in, masks_in, x_kept, out):
    ctx = ExitStack()
    with ctx:
        def sb(name, shape, dt=F32):
            return ctx.enter_context(nc.sbuf_tensor(name, shape, dt))

        at_x, at_h, at_y, at_r1, arena_size = 0, 4096, 8192, 16384, 30464
        arena_at = -(-nc.sbuf_base // 32) * 32
        sb("arena", [P, arena_size])
        assert nc.sbuf_base >= arena_at + 4 * arena_size

        def placed(name, at, shape, dt=F32):
            return nc.alloc_sbuf_tensor_at(name, shape, dt, offset=arena_at + 4 * at)

        xT = placed("xT", at_x, [P, KT_IN, SEQ])
        hT_hi = placed("hT_hi", at_x, [P, KT_IN, SEQ], F32R)
        hT = placed("hT", at_h, [P, KT_IN, SEQ])
        hT_lo = placed("hT_lo", at_h, [P, KT_IN, SEQ], F32R)
        yT = placed("yT", at_y, [P, 16, SEQ])
        y_lo = placed("y_lo", at_y, [P, 16, SEQ], F32R)
        r1 = placed("r1", at_r1, [P, 14080])
        y_hi = placed("y_hi", at_r1 + 4096, [P, 16, SEQ], F32R)
        ring = sb("ring", [P, RING, TILE_W])
        w_hi = sb("w_hi", [P, SPLIT_RING, TILE_W], F32R)
        w_lo = sb("w_lo", [P, SPLIT_RING, TILE_W], F32R)
        ident = sb("ident", [P, P])
        ones = sb("ones", [P, P])
        causal = sb("causal", [P, P])
        rot = sb("rot", [P, P])
        reset = sb("reset", [P, SEQ])
        invf = sb("invf", [P, 2])
        eps = sb("eps", [P, 1])
        levelmask = sb("levelmask", [P, len(LEVELS), 256], U8)
        cos = sb("cos", [P, SEQ])
        sin = sb("sin", [P, SEQ])
        neg = sb("neg", [1, WIN])
        cols = sb("cols", [P, N_COLS])
        ccol = sb("ccol", [P, KT_IN])
        mod = sb("mod", [P, 24])
        factor = sb("factor", [P, KT_IN])
        small = sb("small", [P, 64])
        half_b = small[:, 0:16]
        half_mg = small[:, 16:20]
        neg_sinks = small[:, 20:28]
        a_col = small[0:8, 28:29]
        final_g = small[:, 32:40]
        scr_in = sb("scr_in", [P, 2, SEQ + 4])
        scr_acc = sb("scr_acc", [P, 2, SEQ])
        scr_t = sb("scr_t", [P, 2, SEQ])
        gate_x = sb("gate_x", [P, SEQ])
        rows = sb("rows", [P, SEQ])
        dtm = sb("dtm", [P, SEQ])
        tok = sb("tok", [P, NC, P])
        dt_tok = sb("dt_tok", [P, NC, 8])
        edge = sb("edge", [P, NC, 24])
        edge_e = sb("edge_e", [P, NC, 24])
        kdup = sb("kdup", [P, 2, WIN + SEQ])
        v_al = sb("v_al", [P, NC, P])
        v_off = sb("v_off", [P, NC, P])
        wgate = dtm[R_LR:R_LR + 16, 0:256]
        pairsel = dtm[T_ACS:T_ACS + 8, :].rearrange("p (a b) -> p a b", a=4)
        r2 = sb("r2", [P, 4, SEQ])

        def cut(at, *shape):
            n = int(np.prod(shape))
            v = r1[:, at:at + n]
            if len(shape) == 2:
                v = v.rearrange("p (a b) -> p a b", a=shape[0])
            if len(shape) == 3:
                v = v.rearrange("p (a b c) -> p a b c", a=shape[0], b=shape[1])
            return v

        m_q, m_k, m_v = cut(0, 4, SEQ), cut(2048, 4, SEQ), cut(4096, NC, 512)
        m_kw, m_cs = cut(6144, 3, 512), cut(7680, 3, 512)
        m_w, m_pt, m_qw = cut(9216, 2, SEQ), cut(10240, 2, SEQ), cut(11264, 2, SEQ)
        m_em, m_ad, m_ns = cut(12288, 2, SEQ), cut(13312, SEQ), cut(13824, 3, 4)
        m_max = dtm[32:36, :]
        av_t = cut(12288, SEQ)
        ada_w = cut(0, ADA_SLOTS, 2048)
        m_o = yT[:, 12:16, :]
        g_q, g_k, g_v = cut(0, 2, SEQ), cut(1024, 2, SEQ), cut(2048, NC, 512)
        g_o = cut(0, 4, SEQ)
        c_x = yT[:, 8:12, :]
        c_b, c_c = r2[:, 0:2, :], r2[:, 2:4, :]
        c_xdt, c_xdd = cut(4096, NC, 512), cut(6144, 3, 512)
        c_bt, c_cb = cut(7680, 2, 384), cut(8448, 2, SEQ)
        c_ss, c_l = cut(9472, 3, 512), cut(11008, 4, SEQ)
        c_e2, c_tmp = cut(13056, SEQ), cut(13568, SEQ)
        g_att, g_b = cut(4096, 4, SEQ), cut(6144, 1024)
        g_g, g_d = cut(7168, 2, 1024), cut(9216, 1024)
        g_kt, g_s = cut(10240, 2, 384), cut(11008, 3, 512)
        g_qb, g_dec = cut(12544, 1024), cut(13568, 2, NC)
        g_sqs = cut(7168, 4, SEQ)
        a_q = r2
        a_p, a_pt, a_st = cut(0, 2, 1024), cut(2048, 2, 1024), cut(13600, 2, 40)

        banks = [ctx.enter_context(nc.psum_tensor(f"bank{i}", [P, 512], F32)) for i in range(NB)]

        masks_f = cut(2048, len(LEVELS), 256)

        layer = []

        def sem(name):
            s = ctx.enter_context(nc.semaphore(name))
            layer.append(s)
            return s

        bank_full = [sem(f"bank_full{i}") for i in range(NB)]
        bank_read = [sem(f"bank_read{i}") for i in range(NB)]
        w_in = [sem(f"w_in{i}") for i in range(RING)]
        ada_w_in = [sem(f"ada_w_in{i}") for i in range(ADA_SLOTS)]
        w_hi_ready, w_lo_ready, w_used = sem("w_hi_ready"), sem("w_lo_ready"), sem("w_used")
        x_spilled, x_back = sem("x_spilled"), sem("x_back")
        y_hi_ready, y_ready = sem("y_hi_ready"), sem("y_ready")
        layer_in = sem("layer_in")
        vec_order, act_order, pool_order = sem("vec_order"), sem("act_order"), sem("pool_order")
        squares, x_scaled, h_ready = sem("squares"), sem("x_scaled"), sem("h_ready")
        h_mod, h_hi_ready, a_log_exp = sem("h_mod"), sem("h_hi_ready"), sem("a_log_exp")
        conv_acc, conv_tanh, silu_out = sem("conv_acc"), sem("conv_tanh"), sem("silu_out")
        rope_cos, rope_out = sem("rope_cos"), sem("rope_out")
        gate_ln, rows_ready, edge_exp = sem("gate_ln"), sem("rows_ready"), sem("edge_exp")
        m_exp_in, m_exp, m_masked = sem("m_exp_in"), sem("m_exp"), sem("m_masked")
        m_query, m_decayed, m_h, m_sq, m_done = sem("m_query"), sem("m_decayed"), sem("m_h"), sem("m_sq"), sem("m_done")
        c_xdd_s, c_decayed, c_exp_in, c_exp = sem("c_xdd_s"), sem("c_decayed"), sem("c_exp_in"), sem("c_exp")
        c_l_s, c_gated, c_sq, c_done = sem("c_l_s"), sem("c_gated"), sem("c_sq"), sem("c_done")
        g_ln, g_diff, g_exp, g_kd = sem("g_ln"), sem("g_diff"), sem("g_exp"), sem("g_kd")
        g_key, g_query, g_sq, g_done = sem("g_key"), sem("g_query"), sem("g_sq"), sem("g_done")
        a_max, a_exp, a_rden, a_prob = sem("a_max"), sem("a_exp"), sem("a_rden"), sem("a_prob")
        once = ctx.enter_context(nc.semaphore("once"))
        once_v = ctx.enter_context(nc.semaphore("once_v"))
        once_a = ctx.enter_context(nc.semaphore("once_a"))
        out_done = ctx.enter_context(nc.semaphore("out_done"))

        def bank(key):
            return banks[TILE[key][0]]

        def full(eng, key):
            b, n = TILE[key]
            eng.wait_ge(bank_full[b], n + 1)

        def was_read(eng, key):
            b, n = TILE[key]
            eng.wait_ge(bank_read[b], n + 1)

        def used(eng, w):
            by = USED_BY[w]
            if isinstance(by, tuple):
                full(eng, by)
            else:
                eng.wait_ge(w_used, by)

        def silu_done(eng, name, t):
            eng.wait_ge(silu_out, SILUS[(name, t)] + 1)

        def merged(eng):
            for par in range(2):
                was_read(eng, ("g_level", len(LEVELS) - 1, par))

        def vacant(eng, key):
            b, n = TILE[key]
            if n:
                eng.wait_ge(bank_read[b], n)

        class Line:

            def __init__(self, eng, own):
                self.eng, self.own, self.count, self.last = eng, own, {}, None

            def did(self, ins, signal=None):
                s = self.own if signal is None else signal
                ins.then_inc(s, 1)
                self.count[s.name] = self.count.get(s.name, 0) + 1
                self.last = (s, self.count[s.name])

            def read(self, ins, key):
                b, n = TILE[key]
                ins.then_inc(bank_read[b], 1)
                self.last = (bank_read[b], n + 1)

            def settle(self):
                if self.last:
                    self.eng.wait_ge(*self.last)

        with nc.Block() as block:
            @block.sync
            def _(sp):
                loads = [(xT[:, :, :], xT_in), (ccol[:, :], c_in), (final_g, final_in),
                         (ident[:, :], consts_in[:, 0:128]), (causal[:, :], consts_in[:, 128:256]),
                         (rot[:, :], consts_in[:, 256:384]), (reset[:, :], consts_in[:, 384:896]),
                         (invf[:, :], consts_in[:, 896:898]),
                         (dtm[T_ACS:T_ACS + 8, :], consts_in[T_ACS:T_ACS + 8, 898:1410]),
                         (masks_f, masks_in), (scr_t[:, 1, :].bitcast(I32), pos_in)]
                for dst, src in loads:
                    sp.dma_start(dst, src).then_inc(once, 16)
                sp.wait_ge(once, 16 * len(loads))
                sp.sem_inc(once_v, 1)

            @block.gpsimd
            def _(pool):
                pool.memset(ones[:, :], 1.0)
                pool.memset(eps[:, :], EPS)
                pool.memset(neg[:, :], -1.0e30)
                pool.memset(scr_in[:, :, :], 0.0)
                pool.memset(rows[:, :], 0.0)
                pool.memset(kdup[:, :, :], 0.0)
                pool.memset(v_off[:, :, :], 0.0)

            @block.vector
            def _(dve):
                v = Line(dve, once_v)
                v.count["once_v"] = 1
                dve.wait_ge(once_v, 1)
                ang, k, r = scr_acc[:, 0, :], scr_acc[:, 1, :], scr_t[:, 0, :]
                v.did(dve.tensor_copy(levelmask[:, :, :], masks_f))
                v.did(dve.tensor_copy(r, scr_t[:, 1, :].bitcast(I32)))
                v.settle()
                v.did(dve.tensor_scalar(ang, r, invf[:, 0:1], None, ALU.mult))
                v.settle()
                for quarter, dst in ((0.0, r1[:, 0:512]), (0.25, r1[:, 512:1024])):
                    v.did(dve.tensor_scalar(k, ang, 1.0 / TWO_PI, quarter, ALU.mult, ALU.add))
                    v.settle()
                    v.did(dve.tensor_scalar(k, k, ROUND, None, ALU.add))
                    v.settle()
                    v.did(dve.tensor_scalar(k, k, -ROUND, None, ALU.add))
                    v.settle()
                    v.did(dve.scalar_tensor_tensor(dst, k, -PI_HI, ang, ALU.mult, ALU.add))
                    v.settle()
                    v.did(dve.scalar_tensor_tensor(dst, k, -PI_MID, dst, ALU.mult, ALU.add))
                    v.settle()
                    v.did(dve.scalar_tensor_tensor(dst, k, -PI_LO, dst, ALU.mult, ALU.add))
                    v.settle()
                    v.did(dve.tensor_scalar(dst, dst, quarter * TWO_PI, PI_CLIP, ALU.add, ALU.min))
                    v.settle()
                    v.did(dve.tensor_scalar(dst, dst, -PI_CLIP, None, ALU.max))
                    v.settle()
                dve.memset(small[:, 60:61], 0.0).then_inc(once_a, 1)

            @block.scalar
            def _(act):
                act.wait_ge(once_a, 1)
                act.activation(sin[:, :], r1[:, 0:512], ACT.Sin)
                act.activation(cos[:, :], r1[:, 512:1024], ACT.Sin)
                act.activation(scr_acc[:, 0, 0:8], ccol[:, :], ACT.Tanh, scale=0.5).then_inc(once_a, 1)
                act.wait_ge(once_a, 2)
                act.activation(scr_acc[:, 0, 0:8], scr_acc[:, 0, 0:8], ACT.Copy, bias=1.0).then_inc(once_a, 1)
                act.wait_ge(once_a, 3)
                for t in range(KT_IN):
                    act.activation(ccol[:, t:t + 1], ccol[:, t:t + 1], ACT.Copy, scale=scr_acc[:, 0, t:t + 1])\
                        .then_inc(once_a, 1)
                act.wait_ge(once_a, 3 + KT_IN)
                act.activation(ccol[:, :], ccol[:, :], ACT.Copy, scale=0.5)

        with nc.Fori(0, DEPTH) as l:
            with nc.Block() as block:
                @block.sync
                def _(sp):
                    sp.dma_start(cols[:, :], cols_in[bass.ds(l, 1)].rearrange("a p n -> (a p) n"))\
                        .then_inc(layer_in, 16)
                    sp.dma_start(wgate, wgate_in[bass.ds(l, 1)].rearrange("a p n -> (a p) n"))\
                        .then_inc(layer_in, 16)

                    def load_ada(j):
                        at = ADA_SLOT[j]
                        if at in ADA_SLOT[:j]:
                            old = max(i for i in range(j) if ADA_SLOT[i] == at)
                            full(sp, ("ada", old, 0))
                        sp.dma_start(ada_w[:, at, :], ada_in[bass.ds(l, 1), j].rearrange("a p n -> (a p) n"))\
                            .then_inc(ada_w_in[at], 16)

                    for j in range(ADA_SLOTS):
                        load_ada(j)
                    sp.dma_start(x_kept, xT[:, :, :]).then_inc(x_spilled, 16)
                    for j in range(ADA_SLOTS, ADA_EARLY):
                        load_ada(j)
                    for i, w in enumerate(SPLITS):
                        if i in ADA_BEFORE:
                            load_ada(ADA_BEFORE[i])
                        if i == LAST_PROJ + SPLIT_RING + RING:
                            sp.wait_ge(x_spilled, 16)
                            used(sp, SPLITS[LAST_PROJ])
                            sp.dma_start(xT[:, :, :], x_kept).then_inc(x_back, 16)
                        if i >= RING:
                            sp.wait_ge(w_lo_ready, i - RING + 1)
                        n = WIDTH.get(w, TILE_W)
                        src = weights[bass.ds(l, 1), i, :, 0:n].rearrange("a p n -> (a p) n")
                        sp.dma_start(ring[:, i % RING, 0:n], src).then_inc(w_in[i % RING], 16)
                    sp.wait_ge(x_spilled, 16)

                @block.tensor
                def _(pe):
                    def end(mm, key):
                        mm.then_inc(bank_full[TILE[key][0]], 1)

                    def split_tile(w):
                        i = SPLIT_NO[w]
                        pe.wait_ge(w_lo_ready, i + 1)
                        return [t[:, i % SPLIT_RING, :] for t in (w_hi, w_lo)]

                    def product(o, a, b, start, stop):
                        pe.matmul(o, a[0], b[0], start=start, stop=False)
                        pe.matmul(o, a[0], b[1], start=False, stop=False)
                        return pe.matmul(o, a[1], b[0], start=False, stop=stop)

                    for step in SCHEDULE:
                        kind, arg = step[0], step[1:]
                        keys = tiles_of(step)
                        for key in keys[:1]:
                            vacant(pe, key)
                        o = bank(keys[0]) if keys else None
                        if kind == "norm":
                            for t in range(KT_IN):
                                pe.wait_ge(squares, t + 1)
                                mm = pe.matmul(o[:, :], ones[:, :], hT[:, t, :],
                                               start=(t == 0), stop=(t == KT_IN - 1))
                            end(mm, keys[0])
                        elif kind == "ada":
                            j = arg[0]
                            pe.wait_ge(ada_w_in[ADA_SLOT[j]], 16 * ADA_SLOT[:j + 1].count(ADA_SLOT[j]))
                            for t in range(2):
                                w = ada_w[:, ADA_SLOT[j], t * TILE_W:(t + 1) * TILE_W]
                                for k in range(KT_IN):
                                    mm = pe.matmul(o[:, t:t + 1], w[:, k * P:(k + 1) * P], ccol[:, k:k + 1],
                                                   start=(k == 0), stop=(k == KT_IN - 1))
                            end(mm, keys[0])
                        elif kind == "proj":
                            w = split_tile(arg)
                            for k in range(KT_IN):
                                if arg[0] == "gate":
                                    pe.wait_ge(h_ready, k + 1)
                                mm = product(o[:, :], [x[:, k * P:(k + 1) * P] for x in w],
                                             [x[:, k, :] for x in (hT_hi, hT_lo)], k == 0, k == KT_IN - 1)
                            end(mm, keys[0])
                        elif kind == "rope":
                            i = ROPES[arg]
                            was_read(pe, ("proj",) + arg + (0,))
                            end(pe.matmul(o[:, :], rot[:, :], scr_in[:, i % 2, 3:3 + SEQ], start=True, stop=True), keys[0])
                        elif kind == "av":
                            was_read(pe, ("proj", "av", 0, 0))
                            for p in range(NC):
                                mm = pe.transpose(o[:, p * P:(p + 1) * P], av_t[:, p * P:(p + 1) * P], ident[:, :])
                            end(mm, keys[0])
                        elif kind == "vtok":
                            for q in range(4):
                                w = split_tile((arg[0], q))
                                for p in range(NC):
                                    if q == 0 and p:
                                        vacant(pe, keys[p])
                                    for k in range(2):
                                        mm = product(bank(keys[p])[:, :],
                                                     [x[:, 2 * q + k, p * P:(p + 1) * P] for x in (hT_hi, hT_lo)],
                                                     [x[:, k * 512:(k + 1) * 512] for x in w],
                                                     q == 0 and k == 0, q == 3 and k == 1)
                                    if q == 3:
                                        end(mm, keys[p])
                                if q < 3:
                                    mm.then_inc(w_used, 1)
                        elif kind == "tok":
                            pe.wait_ge(rows_ready, 1)
                            for p in range(NC):
                                mm = pe.transpose(o[:, p * P:(p + 1) * P], rows[:, p * P:(p + 1) * P], ident[:, :])
                            end(mm, keys[0])
                            vacant(pe, keys[1])
                            for p in range(NC):
                                mm = pe.transpose(bank(keys[1])[:, p * 8:(p + 1) * 8], dtm[0:8, p * P:(p + 1) * P],
                                                  ident[0:8, 0:8])
                            end(mm, keys[1])
                            vacant(pe, keys[2])
                            was_read(pe, keys[0])
                            end(pe.matmul(bank(keys[2])[:, :], ident[:, P - 1:P].broadcast_to([P, P]),
                                          tok[:, :, :].rearrange("p a b -> p (a b)"), start=True, stop=True), keys[2])
                        elif kind == "mk_tok":
                            silu_done(pe, "mk", 3)
                            for p in range(3):
                                if p:
                                    vacant(pe, keys[p])
                                for h in range(4):
                                    mm = pe.transpose(bank(keys[p])[:, h * P:(h + 1) * P],
                                                      m_k[:, h, p * P:(p + 1) * P], ident[:, :])
                                end(mm, keys[p])
                        elif kind == "m_qk":
                            h = arg[0]
                            silu_done(pe, "mk", 3)
                            for p in range(NC):
                                tk = slice(p * P, (p + 1) * P)
                                mm = pe.matmul(o[:, tk], m_k[:, h, tk], m_q[:, h, tk], start=True, stop=True)
                            end(mm, keys[0])
                            vacant(pe, keys[1])
                            end(pe.matmul(bank(keys[1])[:, :], ident[T_R:T_R + 4, T_R + h:T_R + h + 1]
                                          .broadcast_to([4, P]), rows[T_R:T_R + 4, :], start=True, stop=True), keys[1])
                        elif kind == "m_decay":
                            h = arg[0]
                            end(pe.matmul(o[:, :], ident[T_R2:T_R2 + 4, T_R2 + h:T_R2 + h + 1].broadcast_to([4, P]),
                                          rows[T_R2:T_R2 + 4, :], start=True, stop=True), keys[0])
                            vacant(pe, keys[1])
                            end(pe.matmul(bank(keys[1])[:, :], ident[32:36, 32 + h:33 + h].broadcast_to([4, P]),
                                          m_max, start=True, stop=True), keys[1])
                        elif kind == "m_state":
                            p = arg[0]
                            was_read(pe, ("mk_tok", p))
                            was_read(pe, ("vtok", "mv", p))
                            for h in range(4):
                                hd = slice(h * P, (h + 1) * P)
                                mm = pe.matmul(o[:, hd], m_kw[:, p, hd], m_v[:, p, hd], start=True, stop=True)
                            end(mm, keys[0])
                            vacant(pe, keys[1])
                            for h in range(4):
                                hd = slice(h * P, (h + 1) * P)
                                mm = pe.matmul(bank(keys[1])[:, h:h + 1], m_kw[:, p, hd], ones[:, 0:1],
                                               start=True, stop=True)
                            end(mm, keys[1])
                        elif kind == "m_num":
                            h = arg[0]
                            hd = slice(h * P, (h + 1) * P)
                            was_read(pe, ("m_qk", h, 0))
                            pe.wait_ge(m_query, h + 1)
                            was_read(pe, ("m_state", 2, 0))
                            was_read(pe, ("m_state", 2, 1))
                            was_read(pe, ("vtok", "mv", 3))
                            for p in range(NC):
                                tk = slice(p * P, (p + 1) * P)
                                mm = pe.matmul(o[:, tk], m_v[:, p, hd], m_pt[:, h % 2, tk], start=True, stop=(p == 0))
                                if p:
                                    mm = pe.matmul(o[:, tk], m_cs[:, p - 1, hd], m_qw[:, h % 2, tk],
                                                   start=False, stop=True)
                            end(mm, keys[0])
                            vacant(pe, keys[1])
                            d = bank(keys[1])
                            pe.matmul(d[:, :], ones[:, :], m_pt[:, h % 2, :], start=True, stop=False)
                            for p in range(1, NC):
                                tk = slice(p * P, (p + 1) * P)
                                mm = pe.matmul(d[:, tk], m_ns[:, p - 1, h:h + 1].broadcast_to([P, P]), m_qw[:, h % 2, tk],
                                               start=False, stop=(p == NC - 1))
                            end(mm, keys[1])
                        elif kind == "m_norm":
                            for h in range(4):
                                if h:
                                    vacant(pe, keys[h])
                                pe.wait_ge(m_sq, h + 1)
                                end(pe.matmul(bank(keys[h])[:, :], ones[:, :], m_k[:, h, :], start=True, stop=True),
                                    keys[h])
                        elif kind == "c_cb":
                            g = arg[0]
                            silu_done(pe, "bc", 3)
                            for p in range(NC):
                                tk = slice(p * P, (p + 1) * P)
                                mm = pe.matmul(o[:, tk], c_b[:, g, tk], c_c[:, g, tk], start=True, stop=True)
                            end(mm, keys[0])
                        elif kind == "c_x":
                            p = arg[0]
                            for t in range(4):
                                mm = pe.transpose(o[:, t * P:(t + 1) * P], c_x[:, t, p * P:(p + 1) * P], ident[:, :])
                            end(mm, keys[0])
                        elif kind == "c_b":
                            g = arg[0]
                            for p in range(3):
                                mm = pe.transpose(o[:, p * P:(p + 1) * P], c_b[:, g, p * P:(p + 1) * P], ident[:, :])
                            end(mm, keys[0])
                        elif kind == "c_state":
                            p = arg[0]
                            pe.wait_ge(c_xdd_s, p + 1)
                            was_read(pe, ("c_b", 1, 0))
                            was_read(pe, ("c_b", 0, 0))
                            for g in range(2):
                                mm = pe.matmul(o[:, g * 256:(g + 1) * 256], c_bt[:, g, p * P:(p + 1) * P],
                                               c_xdd[:, p, g * 256:(g + 1) * 256], start=True, stop=True)
                            end(mm, keys[0])
                        elif kind == "c_decay":
                            h = arg[0]
                            end(pe.matmul(o[:, :], ident[T_ACS:T_ACS + 8, T_ACS + h:T_ACS + h + 1].broadcast_to([8, P]),
                                          rows[T_ACS:T_ACS + 8, :], start=True, stop=True), keys[0])
                        elif kind == "c_y":
                            t = arg[0]
                            g = t // 2
                            for h in (2 * t, 2 * t + 1):
                                pe.wait_ge(c_l_s, h + 1)
                                lo = WIN * (h % 2)
                                for p in range(NC):
                                    if h == 0:
                                        was_read(pe, ("c_x", p, 0))
                                    tk = slice(p * P, (p + 1) * P)
                                    mm = pe.matmul(o[lo:lo + WIN, tk], c_xdt[:, p, h * 64:(h + 1) * 64],
                                                   c_l[:, h % 4, tk], start=True, stop=True)
                            end(mm, keys[0])
                            vacant(pe, keys[1])
                            was_read(pe, ("c_state", 2, 0))
                            for p in range(1, NC):
                                tk = slice(p * P, (p + 1) * P)
                                mm = pe.matmul(bank(keys[1])[:, tk], c_ss[:, p - 1, t * P:(t + 1) * P],
                                               c_c[:, g, tk], start=True, stop=True)
                            end(mm, keys[1])
                            vacant(pe, keys[2])
                            end(pe.matmul(bank(keys[2])[:, :], pairsel[:, t, :],
                                          rows[T_ACS:T_ACS + 8, :], start=True, stop=True), keys[2])
                        elif kind == "c_norm":
                            for j in range(2):
                                pe.wait_ge(c_sq, 2 * arg[0] + j + 1)
                                mm = pe.matmul(o[:, :], ones[:, :], c_l[:, 2 * arg[0] + j, :],
                                               start=(j == 0), stop=(j == 1))
                            end(mm, keys[0])
                        elif kind == "g_gate":
                            for t in range(2):
                                if t:
                                    vacant(pe, keys[t])
                                pe.wait_ge(layer_in, 32)
                                end(pe.matmul(bank(keys[t])[:, :], wgate[:, t * P:(t + 1) * P],
                                              gate_x[R_LR:R_LR + 16, :], start=True, stop=True), keys[t])
                        elif kind == "g_ktok":
                            pe.wait_ge(g_kd, 2)
                            for t in range(2):
                                if t:
                                    vacant(pe, keys[t])
                                for p in range(3):
                                    mm = pe.transpose(bank(keys[t])[:, p * P:(p + 1) * P],
                                                      g_g[:, 0, t * SEQ + p * P:t * SEQ + (p + 1) * P], ident[:, :])
                                end(mm, keys[t])
                        elif kind == "g_state":
                            p = arg[0]
                            for t in range(2):
                                was_read(pe, ("g_ktok", t))
                            for q in range(4):
                                was_read(pe, ("vtok", "gv", q))
                            for h in range(4):
                                mm = pe.matmul(o[:, h * P:(h + 1) * P], g_kt[:, h // 2, p * P:(p + 1) * P],
                                               g_v[:, p, h * P:(h + 1) * P], start=True, stop=True)
                            end(mm, keys[0])
                        elif kind == "g_diag":
                            for t in range(2):
                                was_read(pe, ("proj", "gq", t, 0))
                                was_read(pe, ("proj", "gk", t, 0))
                            for h in range(4):
                                if h:
                                    vacant(pe, keys[h])
                                lo = 64 * (h % 2)
                                for p in range(NC):
                                    tk = slice(p * P, (p + 1) * P)
                                    mm = pe.matmul(bank(keys[h])[:, tk], g_k[lo:lo + 64, h // 2, tk],
                                                   g_q[lo:lo + 64, h // 2, tk], start=True, stop=True)
                                end(mm, keys[h])
                        elif kind == "g_level":
                            i = arg[0]
                            b = LEVELS[i]
                            pe.wait_ge(g_key, i + 1)
                            pe.wait_ge(g_query, i + 1)
                            for par in range(2):
                                if par:
                                    vacant(pe, keys[par])
                                lo = 64 * par
                                for t in range(2):
                                    for p in range(NC):
                                        at = t * SEQ + p * P
                                        src = g_g[lo:lo + 64, i % 2, at:at + P]
                                        second = src.rearrange("p (n b) -> p n b", b=2 * b)[:, :, b:2 * b]
                                        mm = pe.matmul(bank(keys[par])[:, (t * NC + p) * 64:(t * NC + p + 1) * 64],
                                                       src, second, start=True, stop=True)
                                end(mm, keys[par])
                        elif kind == "g_out":
                            h = arg[0]
                            hd = slice(h * P, (h + 1) * P)
                            merged(pe)
                            was_read(pe, ("g_state", 2, 0))
                            pe.wait_ge(g_kd, 3)
                            for p in range(NC):
                                tk = slice(p * P, (p + 1) * P)
                                mm = pe.matmul(o[:, tk], g_v[:, p, hd], g_att[:, h, tk], start=True, stop=(p == 0))
                                if p:
                                    mm = pe.matmul(o[:, tk], g_s[:, p - 1, hd], g_qb[:, (h // 2) * SEQ + p * P:(h // 2) * SEQ + (p + 1) * P],
                                                   start=False, stop=True)
                            end(mm, keys[0])
                        elif kind == "g_norm":
                            for h in range(4):
                                if h:
                                    vacant(pe, keys[h])
                                pe.wait_ge(g_sq, h + 1)
                                end(pe.matmul(bank(keys[h])[:, :], ones[:, :], g_sqs[:, h, :], start=True, stop=True),
                                    keys[h])
                        elif kind == "a_s":
                            p = arg[0]
                            pe.wait_ge(rope_out, 5)
                            for par in range(2):
                                if par:
                                    vacant(pe, keys[par])
                                s = bank(keys[par])
                                lo = 64 * par
                                for e in range(2):
                                    q0 = (2 * p + e) * WIN
                                    for t in range(4):
                                        mm = pe.matmul(s[64 * e:64 * e + 64, t * P:(t + 1) * P],
                                                       a_q[lo:lo + 64, t, q0:q0 + WIN],
                                                       kdup[lo:lo + 64, t // 2, q0:q0 + 2 * WIN],
                                                       start=True, stop=not (p == 0 and e == 0))
                                        if p == 0 and e == 0:
                                            mm = pe.matmul(s[0:64, t * P:t * P + WIN], ones[0:1, 0:64],
                                                           neg[0:1, 0:WIN], start=False, stop=True)
                                end(mm, keys[par])
                        elif kind == "a_pt":
                            p = arg[0]
                            pe.wait_ge(a_prob, p + 1)
                            for g in range(2):
                                if g:
                                    vacant(pe, keys[g])
                                for j in range(4):
                                    h = 4 * g + j
                                    mm = pe.transpose(bank(keys[g])[:, j * P:(j + 1) * P],
                                                      a_p[:, p % 2, h * P:(h + 1) * P], ident[:, :])
                                end(mm, keys[g])
                        elif kind == "a_pv":
                            p = arg[0]
                            for g in range(2):
                                was_read(pe, ("a_pt", p, g))
                            was_read(pe, ("av", 0))
                            for hp in range(2):
                                for g in range(2):
                                    for e in range(2):
                                        v = (v_al if e else v_off)[:, p, g * 64:(g + 1) * 64]
                                        pr = a_pt[:, p % 2, :].rearrange("p (h q) -> p h q", h=8)
                                        for j in range(2):
                                            t = 2 * g + j
                                            mm = pe.matmul(o[64 * hp:64 * hp + 64, t * P + 64 * e:t * P + 64 * e + 64],
                                                           v, pr[:, 2 * t + hp, 64 * e:64 * e + 64],
                                                           start=True, stop=True)
                            end(mm, keys[0])
                        elif kind == "out1":
                            j = arg[0]
                            for i in range(2):
                                w = split_tile(("o1", j, i))
                                for k in range(8 * i, 8 if i == 0 else N_EARLY):
                                    if j == 0:
                                        pe.wait_ge(y_ready, k + 1)
                                    at = (k - 8 * i) * P
                                    mm = product(o[:, :], [x[:, at:at + P] for x in w],
                                                 [y_hi[:, Y_SLOT[k], :], y_lo[:, k, :]], k == 0, k == N_EARLY - 1)
                                if i == 0:
                                    mm.then_inc(w_used, 1)
                            end(mm, keys[0])
                        elif kind == "out2":
                            j = arg[0]
                            pe.wait_ge(y_ready, N_EARLY + NC)
                            w = split_tile(("o2", j // 2))
                            for k in range(4):
                                at = ((j % 2) * 4 + k) * P
                                mm = product(o[:, :], [x[:, at:at + P] for x in w],
                                             [y_hi[:, Y_SLOT[N_EARLY + k], :], y_lo[:, N_EARLY + k, :]], k == 0, k == 3)
                            end(mm, keys[0])

                @block.scalar
                def _(act):
                    a = Line(act, act_order)

                    def apply(out, in_, func, **kw):
                        return act.activation(out, in_, func, **kw)

                    def split(i):
                        n = WIDTH.get(SPLITS[i], TILE_W)
                        act.wait_ge(w_in[i % RING], 16 * (i // RING + 1))
                        if i >= SPLIT_RING:
                            used(act, SPLITS[i - SPLIT_RING])
                        a.did(apply(w_hi[:, i % SPLIT_RING, 0:n], ring[:, i % RING, 0:n], ACT.Copy), w_hi_ready)

                    act.wait_ge(layer_in, 32)
                    a.did(apply(small[0:8, 29:30], cols[0:8, COL["a_log"]:COL["a_log"] + 1], ACT.Exp), a_log_exp)
                    for step in SCHEDULE:
                        kind, arg = step[0], step[1:]
                        keys = tiles_of(step)
                        within, after = next_splits(step)
                        for i in within:
                            split(i)
                        a.settle()
                        if kind == "norm":
                            for t in range(KT_IN):
                                a.did(apply(hT[:, t, :], xT[:, t, :], ACT.Square), squares)
                            full(act, keys[0])
                            a.read(apply(scr_t[:, 0, :], bank(keys[0])[:, :], ACT.Sqrt, bias=eps[:, 0:1],
                                         scale=1.0 / D_MODEL), keys[0])
                        elif kind == "modulate":
                            for i in range(SPLIT_RING):
                                split(i)
                            act.wait_ge(x_spilled, 16)
                            for t in range(KT_IN):
                                act.wait_ge(h_mod, t + 1)
                                a.did(apply(hT_hi[:, t, :], hT[:, t, :], ACT.Copy), h_hi_ready)
                        elif kind == "proj":
                            name, t = arg
                            o, key = bank(keys[0]), keys[0]
                            if name != "gate":
                                full(act, key)
                            if name == "gate":
                                pass
                            elif name == "av":
                                a.read(apply(av_t, o[:, :], ACT.Copy), key)
                            elif name in ("ak", "aq"):
                                i = ROPES[arg]
                                if i == 1:
                                    silu_done(act, "bc", 3)
                                if i >= 2:
                                    act.wait_ge(rope_out, i - 1)
                                a.read(apply(scr_in[:, i % 2, 3:3 + SEQ], o[:, :], ACT.Copy), key)
                            elif arg in CONVS:
                                i, u = CONVS[arg], SILUS[arg]
                                if i == 0:
                                    act.wait_ge(rope_out, 1)
                                if i >= 2:
                                    act.wait_ge(conv_acc, i - 1)
                                a.read(apply(scr_in[:, i % 2, 3:3 + SEQ], o[:, :], ACT.Copy, scale=0.5), key)
                                for n in after:
                                    split(n)
                                after = []
                                act.wait_ge(conv_acc, i + 1)
                                if u >= 2:
                                    act.wait_ge(silu_out, u - 1)
                                a.did(apply(scr_t[:, u % 2, :], scr_acc[:, u % 2, :], ACT.Tanh), conv_tanh)
                            elif arg in SILUS:
                                u = SILUS[arg]
                                act.wait_ge(silu_out, u - 1)
                                a.did(apply(scr_acc[:, u % 2, :], o[:, :], ACT.Copy, scale=0.5))
                                a.read(apply(scr_t[:, u % 2, :], o[:, :], ACT.Tanh, scale=0.5), key)
                            elif name == "mo":
                                a.read(apply(m_o[:, t, :], o[:, :], ACT.Tanh, scale=0.5), key)
                            else:
                                act.wait_ge(m_done, 4)
                                dst, scale = {"gq": (g_q, 0.125), "gk": (g_k, 1.0)}[name]
                                a.read(apply(dst[:, t, :], o[:, :], ACT.Copy, scale=scale), key)
                        elif kind == "rows":
                            was_read(act, ("proj", "gate", 0, 0))
                            w = scr_t[:, 1, :]
                            act.wait_ge(x_scaled, KT_IN)
                            a.did(apply(w, gate_x[:, :], ACT.Abs))
                            a.settle()
                            a.did(apply(w, w, ACT.Exp, scale=-1.0))
                            a.settle()
                            a.did(apply(w, w, ACT.Ln, bias=1.0), gate_ln)
                        elif kind == "av":
                            full(act, keys[0])
                            o = bank(keys[0])
                            a.did(apply(v_al[:, :, :], o[:, :].rearrange("p (a b) -> p a b", a=NC), ACT.Copy))
                            a.did(apply(v_off[64:128, :, :], o[0:64, :].rearrange("p (a b) -> p a b", a=NC), ACT.Copy))
                            a.read(apply(v_off[0:64, 1:NC, :], o[64:128, 0:384].rearrange("p (a b) -> p a b", a=3),
                                         ACT.Copy), keys[0])
                        elif kind == "vtok":
                            if arg[0] == "gv":
                                act.wait_ge(m_done, 4)
                            for p in range(NC):
                                full(act, keys[p])
                                dst = m_v if arg[0] == "mv" else g_v
                                a.read(apply(dst[:, p, :], bank(keys[p])[:, :], ACT.Copy), keys[p])
                        elif kind == "tok":
                            full(act, keys[0])
                            a.read(apply(tok[:, :, :].rearrange("p a b -> p (a b)"), bank(keys[0])[:, :], ACT.Copy),
                                   keys[0])
                            full(act, keys[1])
                            a.read(apply(dt_tok[:, :, :].rearrange("p a b -> p (a b)"), bank(keys[1])[:, 0:32],
                                         ACT.Copy), keys[1])
                            was_read(act, keys[2])
                            a.did(apply(edge_e[:, :, :], edge[:, :, :], ACT.Exp), edge_exp)
                        elif kind == "m_qk":
                            h = arg[0]
                            act.wait_ge(m_exp_in, h + 1)
                            a.did(apply(m_w[:, h % 2, :], m_w[:, h % 2, :], ACT.Exp), m_exp)
                        elif kind == "m_decay":
                            h = arg[0]
                            if h >= 2:
                                full(act, ("m_num", h - 2, 1))
                                act.wait_ge(m_h, h - 1)
                            full(act, keys[0])
                            a.read(apply(m_qw[:, h % 2, :], bank(keys[0])[:, :], ACT.Exp), keys[0])
                            full(act, keys[1])
                            a.read(apply(m_em[:, h % 2, :], bank(keys[1])[:, :], ACT.Exp, scale=-1.0), keys[1])
                        elif kind == "m_num":
                            h = arg[0]
                            if h:
                                act.wait_ge(m_h, h)
                            full(act, keys[1])
                            a.read(apply(m_ad[:, :], bank(keys[1])[:, :], ACT.Abs), keys[1])
                        elif kind == "m_norm":
                            act.wait_ge(m_h, 4)
                            for h in range(4):
                                a.did(apply(m_k[:, h, :], m_q[:, h, :], ACT.Square), m_sq)
                            for h in range(4):
                                full(act, keys[h])
                                a.read(apply(m_v[:, h, :], bank(keys[h])[:, :], ACT.Sqrt, bias=eps[:, 0:1],
                                             scale=0.25 / P), keys[h])
                        elif kind == "c_b":
                            full(act, keys[0])
                            act.wait_ge(m_done, 4)
                            a.read(apply(c_bt[:, arg[0], :], bank(keys[0])[:, 0:384], ACT.Copy), keys[0])
                        elif kind == "c_decay":
                            h = arg[0]
                            act.wait_ge(c_exp_in, h + 1)
                            a.did(apply(c_l[:, h % 4, :], c_l[:, h % 4, :], ACT.Exp), c_exp)
                        elif kind == "c_y":
                            t = arg[0]
                            if t:
                                act.wait_ge(c_gated, t)
                            full(act, keys[2])
                            a.read(apply(c_e2[:, :], bank(keys[2])[:, :], ACT.Exp), keys[2])
                        elif kind == "c_norm":
                            j = arg[0]
                            act.wait_ge(c_gated, 4)
                            for t in (2 * j, 2 * j + 1):
                                a.did(apply(c_l[:, t, :], yT[:, 4 + t, :], ACT.Square), c_sq)
                            full(act, keys[0])
                            a.read(apply((c_e2, c_tmp)[j][:, :], bank(keys[0])[:, :], ACT.Sqrt, bias=eps[:, 0:1],
                                         scale=1.0 / 256), keys[0])
                        elif kind == "g_gate":
                            for t in range(2):
                                was_read(act, keys[t])
                            a.did(apply(g_d[:, :], g_b[:, :], ACT.Abs))
                            a.settle()
                            a.did(apply(g_d[:, :], g_d[:, :], ACT.Exp, scale=-1.0))
                            a.settle()
                            a.did(apply(g_d[:, :], g_d[:, :], ACT.Ln, bias=1.0), g_ln)
                        elif kind == "g_decay":
                            last = g_b[:, :].rearrange("p (n b) -> p n b", b=P)[:, :, P - 1]
                            act.wait_ge(g_diff, 1)
                            a.did(apply(g_d[:, :], g_d[:, :], ACT.Exp, scale=1.0 / 16), g_exp)
                            a.did(apply(g_dec[:, :, :].rearrange("p a b -> p (a b)"), last, ACT.Exp,
                                        scale=1.0 / 16), g_exp)
                            a.did(apply(g_qb[:, :], g_b[:, :], ACT.Exp, scale=1.0 / 16), g_exp)
                        elif kind == "g_ktok":
                            for t in range(2):
                                full(act, keys[t])
                                a.read(apply(g_kt[:, t, :], bank(keys[t])[:, 0:384], ACT.Copy), keys[t])
                        elif kind == "g_level":
                            act.wait_ge(g_diff, arg[0] + 2)
                            a.did(apply(g_d[:, :], g_d[:, :], ACT.Exp, scale=1.0 / 16), g_exp)
                        elif kind == "g_out":
                            h = arg[0]
                            full(act, keys[0])
                            merged(act)
                            a.read(apply(g_o[:, h, :], bank(keys[0])[:, :], ACT.Copy), keys[0])
                            a.settle()
                            a.did(apply(g_sqs[:, h, :], g_o[:, h, :], ACT.Square), g_sq)
                        elif kind == "g_norm":
                            for h in range(4):
                                full(act, keys[h])
                                a.read(apply(g_att[:, h, :], bank(keys[h])[:, :], ACT.Sqrt, bias=eps[:, 0:1],
                                             scale=1.0 / P), keys[h])
                        elif kind == "a_s":
                            p = arg[0]
                            st = a_st[:, p % 2, :]
                            act.wait_ge(a_max, p + 1)
                            act.wait_ge(g_done, 4)
                            if p >= 2:
                                full(act, ("a_pt", p - 2, 1))
                            for par in range(2):
                                for t in range(4):
                                    h = 2 * t + par
                                    ins = apply(a_p[:, p % 2, h * P:(h + 1) * P], bank(keys[par])[:, t * P:(t + 1) * P],
                                                ACT.Exp, bias=st[:, 8 + h:9 + h], scale=0.125,
                                                accum_out=st[:, 24 + h:25 + h])
                                a.read(ins, keys[par])
                            a.did(apply(st[:, 16:24], st[:, 16:24], ACT.Exp), a_exp)
                        elif kind == "a_pt":
                            p = arg[0]
                            if p >= 2:
                                full(act, ("a_pv", p - 2, 0))
                            full(act, keys[0])
                            a.read(apply(a_pt[:, p % 2, 0:512], bank(keys[0])[:, :], ACT.Copy), keys[0])
                        elif kind == "y_split":
                            act.wait_ge(m_done, 4)
                            act.wait_ge(c_done, 4)
                            full(act, ("g_out", 3, 0))
                            for k in (range(8) if arg[0] == 0 else range(8, N_EARLY)):
                                if k >= 8:
                                    act.wait_ge(g_done, k - 7)
                                a.did(apply(y_hi[:, Y_SLOT[k], :], yT[:, k, :], ACT.Copy), y_hi_ready)
                        elif kind == "a_pv":
                            p = arg[0]
                            was_read(act, keys[0])
                            tk = slice(p * P, (p + 1) * P)
                            a.did(apply(y_hi[:, 0:4, tk], yT[:, 12:16, tk], ACT.Copy), y_hi_ready)
                        for i in after:
                            split(i)

                @block.gpsimd
                def _(pool):
                    q = Line(pool, pool_order)

                    def split(i):
                        n = WIDTH.get(SPLITS[i], TILE_W)
                        pool.wait_ge(w_hi_ready, i + 1)
                        at = i % SPLIT_RING
                        q.did(pool.tensor_tensor(w_lo[:, at, 0:n], ring[:, i % RING, 0:n],
                                                 w_hi[:, at, 0:n].bitcast(F32), ALU.subtract), w_lo_ready)

                    for step in SCHEDULE:
                        kind, arg = step[0], step[1:]
                        keys = tiles_of(step)
                        q.settle()
                        for i in next_splits(step)[0] + (list(range(SPLIT_RING)) if kind == "modulate" else []):
                            split(i)
                        if kind == "rope":
                            i = ROPES[arg]
                            full(pool, keys[0])
                            w = scr_in[:, i % 2, 3:3 + SEQ]
                            q.did(pool.tensor_tensor(w, w, cos[:, :], ALU.mult), rope_cos)
                        elif kind == "m_qk":
                            h = arg[0]
                            pool.wait_ge(m_exp, h + 1)
                            w = m_w[:, h % 2, :].rearrange("p (a b) -> p a b", a=NC)
                            q.did(pool.tensor_tensor(w, w, mid_bcast(causal[:, :], NC), ALU.mult), m_masked)
                        elif kind == "m_state" and arg[0]:
                            p = arg[0]
                            carry = edge_e[:, p, 4:8]
                            was_read(pool, ("m_state", p - 1, 0))
                            was_read(pool, ("m_state", p - 1, 1))
                            q.did(pool.tensor_tensor(m_cs[:, p, :].rearrange("p (a b) -> p a b", a=4),
                                                     m_cs[:, p - 1, :].rearrange("p (a b) -> p a b", a=4),
                                                     bcast(carry, P), ALU.mult), m_decayed)
                            q.did(pool.tensor_tensor(m_ns[:, p, :], m_ns[:, p - 1, :], carry, ALU.mult), m_decayed)
                        elif kind == "c_x" and arg[0] < 3:
                            p = arg[0]
                            was_read(pool, keys[0])
                            q.did(pool.tensor_tensor(c_xdd[:, p, :].rearrange("p (a b) -> p a b", a=8),
                                                     c_xdt[:, p, :].rearrange("p (a b) -> p a b", a=8),
                                                     bcast(edge_e[:, p, 16:24], 64), ALU.mult), c_xdd_s)
                        elif kind == "c_state" and arg[0]:
                            p = arg[0]
                            was_read(pool, ("c_state", p - 1, 0))
                            q.did(pool.tensor_tensor(c_ss[:, p, :].rearrange("p (a b) -> p a b", a=8),
                                                     c_ss[:, p - 1, :].rearrange("p (a b) -> p a b", a=8),
                                                     bcast(edge_e[:, p, 8:16], 64), ALU.mult), c_decayed)
                        elif kind == "c_decay":
                            h = arg[0]
                            pool.wait_ge(c_exp, h + 1)
                            was_read(pool, ("c_cb", h // 4, 0))
                            q.did(pool.tensor_tensor(c_l[:, h % 4, :], c_l[:, h % 4, :], c_cb[:, h // 4, :], ALU.mult),
                                  c_l_s)
                        elif kind == "g_decay":
                            pool.wait_ge(c_done, 4)
                            q.did(pool.memset(g_s[:, :, :], 0.0), g_kd)
                            pool.wait_ge(g_exp, 3)
                            was_read(pool, ("proj", "gk", 1, 0))
                            kk = g_k[:, :, :].rearrange("p a b -> p (a b)")
                            qq = g_q[:, :, :].rearrange("p a b -> p (a b)")
                            q.did(pool.tensor_tensor(g_g[:, 0, :], kk, g_d[:, :], ALU.mult), g_kd)
                            q.did(pool.tensor_tensor(g_qb[:, :], qq, g_qb[:, :], ALU.mult), g_kd)
                        elif kind == "g_level":
                            i = arg[0]
                            b = LEVELS[i]
                            pool.wait_ge(g_exp, 4 + i)
                            full(pool, ("g_level", i - 2, 1) if i >= 2 else ("g_ktok", 1))

                            def first(v):
                                return v.rearrange("p (n b) -> p n b", b=2 * b)[:, :, 0:b]

                            kk = g_k[:, :, :].rearrange("p a b -> p (a b)")
                            q.did(pool.tensor_tensor(first(g_g[:, i % 2, :]), first(kk), first(g_d[:, :]), ALU.mult),
                                  g_key)
                        elif kind == "a_s":
                            p = arg[0]
                            pool.wait_ge(a_rden, p + 1)
                            w = a_p[:, p % 2, :].rearrange("p (a b) -> p a b", a=8)
                            q.did(pool.tensor_tensor(w, w, bcast(a_st[:, p % 2, 32:40], P), ALU.mult), a_prob)
                        elif kind == "y_split":
                            for k in (range(8) if arg[0] == 0 else range(8, N_EARLY)):
                                pool.wait_ge(y_hi_ready, k + 1)
                                q.did(pool.tensor_tensor(y_lo[:, k, :], yT[:, k, :], y_hi[:, Y_SLOT[k], :].bitcast(F32),
                                                         ALU.subtract), y_ready)
                        elif kind == "a_pv":
                            p = arg[0]
                            tk = slice(p * P, (p + 1) * P)
                            pool.wait_ge(y_hi_ready, N_EARLY + p + 1)
                            q.did(pool.tensor_tensor(y_lo[:, 12:16, tk], yT[:, 12:16, tk],
                                                     y_hi[:, 0:4, tk].bitcast(F32), ALU.subtract), y_ready)
                        for i in next_splits(step)[1]:
                            split(i)

                @block.vector
                def _(dve):
                    v = Line(dve, vec_order)

                    def col(name, i=0):
                        return cols[:, COL[name] + i:COL[name] + i + 1]

                    def chunks(ap):
                        return ap.rearrange("p (a b) -> p a b", a=NC)

                    dve.wait_ge(layer_in, 32)
                    v.did(dve.tensor_scalar(half_b, cols[:, COL["conv_b"]:COL["conv_b"] + 16], 0.5, None, ALU.mult))
                    v.did(dve.tensor_scalar(half_mg, cols[:, COL["m_g"]:COL["m_g"] + 4], 0.5, None, ALU.mult))
                    v.did(dve.tensor_scalar(neg_sinks, cols[:, COL["sinks"]:COL["sinks"] + 8], -1.0, None, ALU.mult))
                    dve.wait_ge(a_log_exp, 1)
                    v.did(dve.tensor_scalar(a_col, small[0:8, 29:30], -1.0, None, ALU.mult))
                    for step in SCHEDULE:
                        kind, arg = step[0], step[1:]
                        keys = tiles_of(step)
                        v.settle()
                        o = bank(keys[0]) if keys else None
                        if kind == "norm":
                            was_read(dve, keys[0])
                            v.did(dve.reciprocal(scr_t[:, 1, :], scr_t[:, 0, :]))
                            v.settle()
                            for t in range(KT_IN):
                                v.did(dve.tensor_tensor(hT[:, t, :], xT[:, t, :], scr_t[:, 1, :], ALU.mult), x_scaled)
                        elif kind == "ada":
                            j = arg[0]
                            full(dve, keys[0])
                            v.read(dve.tensor_tensor(mod[:, 2 * j:2 * j + 2], o[:, 0:2],
                                                     cols[:, COL["b_ada"] + 2 * j:COL["b_ada"] + 2 * j + 2], ALU.add),
                                   keys[0])
                        elif kind == "modulate":
                            v.settle()
                            v.did(dve.scalar_tensor_tensor(factor[:, :], mod[:, 8:16], 1.0,
                                                           cols[:, COL["norm_g"]:COL["norm_g"] + 8], ALU.add, ALU.mult))
                            v.settle()
                            for t in range(KT_IN + 1):
                                if t < KT_IN:
                                    v.did(dve.tensor_scalar(hT[:, t, :], hT[:, t, :], factor[:, t:t + 1],
                                                            mod[:, t:t + 1], ALU.mult, ALU.add), h_mod)
                                if t:
                                    dve.wait_ge(h_hi_ready, t)
                                    v.did(dve.tensor_tensor(hT_lo[:, t - 1, :], hT[:, t - 1, :],
                                                            hT_hi[:, t - 1, :].bitcast(F32), ALU.subtract), h_ready)
                        elif kind == "proj" and arg[0] == "gate":
                            full(dve, keys[0])
                            v.read(dve.tensor_scalar(gate_x[:, :], o[:, :], col("gate_b"), None, ALU.add), keys[0])
                            v.settle()
                        elif kind == "proj" and arg in SILUS:
                            name, t = arg
                            u = SILUS[arg]
                            was_read(dve, keys[0])
                            acc = scr_acc[:, u % 2, :]
                            if arg in CONVS:
                                i, ch = CONVS[arg], CONV_TILE[arg]
                                src = scr_in[:, i % 2, :]
                                v.did(dve.tensor_scalar(acc, src[:, 0:SEQ], col("conv_w", 4 * ch),
                                                        half_b[:, ch:ch + 1], ALU.mult, ALU.add))
                                for k in range(1, 4):
                                    v.settle()
                                    v.did(dve.scalar_tensor_tensor(acc, src[:, k:k + SEQ], col("conv_w", 4 * ch + k),
                                                                   acc, ALU.mult, ALU.add),
                                          conv_acc if k == 3 else None)
                                dst = {"mq": m_q[:, t, :], "mk": m_k[:, t, :], "xs": c_x[:, t, :],
                                       "bc": r2[:, t, :]}[name]
                                dve.wait_ge(conv_tanh, i + 1)
                            else:
                                dst = yT[:, Y_TILE[Z_OF[name]] + t, :]
                            v.did(dve.scalar_tensor_tensor(dst, scr_t[:, u % 2, :], 1.0, acc, ALU.add, ALU.mult),
                                  silu_out)
                        elif kind == "rows":
                            dve.wait_ge(gate_ln, 1)
                            ln = scr_t[:, 1, :]
                            lf, b, da = scr_acc[32:36, 0, :], scr_acc[32:36, 1, :], scr_acc[0:8, 1, :]
                            ig = gate_x[R_I:R_I + 4, :]
                            mprev = small[32:36, 48:52]
                            v.did(dve.scalar_tensor_tensor(dtm[0:8, :], gate_x[R_DT:R_DT + 8, :], 0.0, ln[0:8, :],
                                                           ALU.max, ALU.add))
                            v.did(dve.scalar_tensor_tensor(lf, gate_x[R_F:R_F + 4, :], 0.0, ln[R_F:R_F + 4, :],
                                                           ALU.min, ALU.subtract))
                            v.did(dve.memset(mprev[:, 0:1], 0.0))
                            v.settle()
                            v.did(dve.tensor_tensor_scan(m_max, lf, ig, 0.0, ALU.add, ALU.max))
                            v.did(dve.tensor_tensor_scan(b, reset[32:36, :], lf, 0.0, ALU.mult, ALU.add))
                            v.did(dve.tensor_scalar(da, dtm[0:8, :], a_col, None, ALU.mult))
                            v.settle()
                            v.did(dve.tensor_tensor_scan(rows[T_ACS:T_ACS + 8, :], reset[0:8, :], da, 0.0,
                                                         ALU.mult, ALU.add))
                            v.did(dve.tensor_tensor(rows[T_C:T_C + 4, :], ig, b, ALU.subtract))
                            v.did(dve.tensor_tensor(rows[T_R:T_R + 4, :], b, m_max, ALU.subtract))
                            v.did(dve.tensor_copy(mprev[:, 1:4], chunks(m_max)[:, 0:3, P - 1]))
                            v.settle()
                            v.did(dve.tensor_tensor(chunks(rows[T_R2:T_R2 + 4, :]), chunks(rows[T_R:T_R + 4, :]),
                                                    bcast(mprev, P), ALU.add), rows_ready)
                        elif kind == "rope":
                            i = ROPES[arg]
                            w = scr_in[:, i % 2, 3:3 + SEQ]
                            dst = scr_t[:, 0, :] if i == 0 else a_q[:, i - 1, :]
                            full(dve, keys[0])
                            v.read(dve.tensor_tensor(dst, o[:, :], sin[:, :], ALU.mult), keys[0])
                            dve.wait_ge(rope_cos, i + 1)
                            v.settle()
                            if i:
                                v.did(dve.tensor_tensor(dst, dst, w, ALU.add), rope_out)
                            else:
                                for g in range(2):
                                    half = slice(64 * g, 64 * g + 64)
                                    v.did(dve.tensor_tensor(kdup[half, g, WIN:], dst[half, :], w[half, :], ALU.add))
                                v.settle()
                                v.did(dve.tensor_copy(kdup[64:128, 0, WIN:], kdup[0:64, 0, WIN:]))
                                v.did(dve.tensor_copy(kdup[0:64, 1, WIN:], kdup[64:128, 1, WIN:]), rope_out)
                        elif kind == "tok":
                            full(dve, keys[2])
                            was_read(dve, keys[1])
                            was_read(dve, keys[0])
                            e = chunks(bank(keys[2])[:, :])
                            v.did(dve.tensor_tensor(edge[:, :, 0:4], e[:, :, T_R:T_R + 4], tok[:, :, T_C:T_C + 4],
                                                    ALU.add))
                            v.did(dve.tensor_copy(edge[:, :, 4:8], e[:, :, T_R2:T_R2 + 4]))
                            v.did(dve.tensor_copy(edge[:, :, 8:16], e[:, :, T_ACS:T_ACS + 8]))
                            v.read(dve.tensor_tensor(edge[:, :, 16:24], e[:, :, T_ACS:T_ACS + 8],
                                                     tok[:, :, T_ACS:T_ACS + 8], ALU.subtract), keys[2])
                        elif kind == "mk_tok":
                            dve.wait_ge(edge_exp, 1)
                            for p in range(3):
                                full(dve, keys[p])
                                v.read(dve.tensor_tensor(chunks(m_kw[:, p, :]), chunks(bank(keys[p])[:, :]),
                                                         bcast(edge_e[:, p, 0:4], P), ALU.mult), keys[p])
                        elif kind == "m_qk":
                            h = arg[0]
                            w = m_w[:, h % 2, :]
                            full(dve, keys[1])
                            v.read(dve.tensor_tensor(chunks(w), chunks(bank(keys[1])[:, :]),
                                                     bcast(tok[:, :, T_C + h], P), ALU.add), keys[1])
                            v.settle()
                            v.did(dve.tensor_scalar(w, w, 0.0, None, ALU.min), m_exp_in)
                        elif kind == "m_decay":
                            h = arg[0]
                            dve.wait_ge(m_masked, h + 1)
                            full(dve, ("m_qk", h, 0))
                            v.read(dve.scalar_tensor_tensor(m_pt[:, h % 2, :], bank(("m_qk", h, 0))[:, :], P ** -0.5,
                                                            m_w[:, h % 2, :], ALU.mult, ALU.mult), ("m_qk", h, 0))
                            was_read(dve, keys[0])
                            v.did(dve.scalar_tensor_tensor(m_qw[:, h % 2, :], m_q[:, h, :], P ** -0.5,
                                                           m_qw[:, h % 2, :], ALU.mult, ALU.mult), m_query)
                        elif kind == "m_state":
                            p = arg[0]
                            if p:
                                dve.wait_ge(m_decayed, 2 * p)
                            for dst, key, n in ((m_cs, keys[0], 512), (m_ns, keys[1], 4)):
                                full(dve, key)
                                src = bank(key)[:, 0:n]
                                v.read(dve.tensor_tensor(dst[:, p, :], src, dst[:, p, :], ALU.add) if p else
                                       dve.tensor_copy(dst[:, p, :], src), key)
                        elif kind == "m_num":
                            h = arg[0]
                            was_read(dve, keys[1])
                            was_read(dve, ("m_decay", h, 1))
                            v.did(dve.tensor_tensor(m_ad[:, :], m_ad[:, :], m_em[:, h % 2, :], ALU.max))
                            v.settle()
                            v.did(dve.reciprocal(m_ad[:, :], m_ad[:, :]))
                            v.settle()
                            full(dve, keys[0])
                            v.read(dve.tensor_tensor(m_q[:, h, :], o[:, :], m_ad[:, :], ALU.mult), keys[0])
                            v.settle()
                            was_read(dve, ("proj", "mo", h, 0))
                            v.did(dve.scalar_tensor_tensor(m_q[:, h, :], m_o[:, h, :], 1.0, m_q[:, h, :],
                                                           ALU.add, ALU.mult), m_h)
                        elif kind == "m_norm":
                            for h in range(4):
                                was_read(dve, keys[h])
                                v.did(dve.reciprocal(m_v[:, h, :], m_v[:, h, :]))
                                v.settle()
                                v.did(dve.scalar_tensor_tensor(m_q[:, h, :], m_q[:, h, :], half_mg[:, h:h + 1],
                                                               m_v[:, h, :], ALU.mult, ALU.mult))
                                v.settle()
                                silu_done(dve, "mz", h)
                                v.did(dve.tensor_tensor(yT[:, h, :], m_q[:, h, :], yT[:, h, :], ALU.mult), m_done)
                        elif kind == "c_cb":
                            full(dve, keys[0])
                            v.read(dve.tensor_tensor(chunks(c_cb[:, arg[0], :]), chunks(o[:, :]),
                                                     mid_bcast(causal[:, :], NC), ALU.mult), keys[0])
                        elif kind == "c_x":
                            p = arg[0]
                            full(dve, keys[0])
                            v.read(dve.tensor_tensor(c_xdt[:, p, :].rearrange("p (a b) -> p a b", a=8),
                                                     o[:, :].rearrange("p (a b) -> p a b", a=8),
                                                     bcast(dt_tok[:, p, :], 64), ALU.mult), keys[0])
                        elif kind == "c_state":
                            p = arg[0]
                            full(dve, keys[0])
                            if p:
                                dve.wait_ge(c_decayed, p)
                            v.read(dve.tensor_tensor(c_ss[:, p, :], o[:, :], c_ss[:, p, :], ALU.add) if p else
                                   dve.tensor_copy(c_ss[:, p, :], o[:, :]), keys[0])
                        elif kind == "c_decay":
                            h = arg[0]
                            if h >= 4:
                                full(dve, ("c_y", (h - 4) // 2, 0))
                            full(dve, keys[0])
                            w = c_l[:, h % 4, :]
                            v.read(dve.tensor_tensor(chunks(w), chunks(o[:, :]), bcast(tok[:, :, T_ACS + h], P),
                                                     ALU.subtract), keys[0])
                            v.settle()
                            v.did(dve.tensor_scalar(w, w, 0.0, None, ALU.min), c_exp_in)
                        elif kind == "c_y":
                            t = arg[0]
                            full(dve, keys[0])
                            v.read(dve.scalar_tensor_tensor(c_tmp[:, :], c_x[:, t, :], col("ssd_d", t), o[:, :],
                                                            ALU.mult, ALU.add), keys[0])
                            was_read(dve, keys[2])
                            full(dve, keys[1])
                            v.read(dve.tensor_tensor(c_e2[:, P:], c_e2[:, P:], bank(keys[1])[:, P:], ALU.mult), keys[1])
                            v.settle()
                            v.did(dve.tensor_tensor(c_tmp[:, P:], c_tmp[:, P:], c_e2[:, P:], ALU.add))
                            v.settle()
                            silu_done(dve, "cz", t)
                            v.did(dve.tensor_tensor(yT[:, 4 + t, :], yT[:, 4 + t, :], c_tmp[:, :], ALU.mult), c_gated)
                        elif kind == "c_norm":
                            j = arg[0]
                            was_read(dve, keys[0])
                            w = (c_e2, c_tmp)[j][:, :]
                            v.did(dve.reciprocal(w, w))
                            v.settle()
                            for t in (2 * j, 2 * j + 1):
                                v.did(dve.scalar_tensor_tensor(yT[:, 4 + t, :], yT[:, 4 + t, :], col("ssd_g", t), w,
                                                               ALU.mult, ALU.mult), c_done)
                        elif kind == "g_gate":
                            dve.wait_ge(c_done, 4)
                            for t in range(2):
                                full(dve, keys[t])
                                v.read(dve.tensor_scalar(g_b[:, t * SEQ:(t + 1) * SEQ], bank(keys[t])[:, :],
                                                         col("gla_b", t), None, ALU.add), keys[t])
                            dve.wait_ge(g_ln, 1)
                            v.did(dve.scalar_tensor_tensor(g_g[:, 0, :], g_b[:, :], 0.0, g_d[:, :],
                                                           ALU.min, ALU.subtract))
                            v.settle()
                            for t in range(2):
                                tk = slice(t * SEQ, (t + 1) * SEQ)
                                v.did(dve.tensor_tensor_scan(g_b[:, tk], reset[:, :], g_g[:, 0, tk], 0.0,
                                                             ALU.mult, ALU.add))
                            v.settle()
                        elif kind == "g_decay":
                            b = g_b[:, :].rearrange("p (n b) -> p n b", b=P)
                            v.did(dve.tensor_tensor(g_d[:, :].rearrange("p (n b) -> p n b", b=P),
                                                    bcast(b[:, :, P - 1], P), b, ALU.subtract), g_diff)
                        elif kind == "g_diag":
                            for h in range(4):
                                full(dve, keys[h])
                                v.read(dve.tensor_tensor(chunks(g_att[:, h, :]), chunks(bank(keys[h])[:, :]),
                                                         mid_bcast(ident[:, :], NC), ALU.mult), keys[h])
                        elif kind == "g_state":
                            p = arg[0]
                            full(dve, keys[0])
                            dve.wait_ge(g_kd, 1)
                            dve.wait_ge(g_exp, 2)
                            for h in range(4):
                                half, hd = slice(64 * (h % 2), 64 * (h % 2) + 64), slice(h * P, (h + 1) * P)
                                if p:
                                    ins = dve.scalar_tensor_tensor(g_s[half, p, hd], g_s[half, p - 1, hd],
                                                                   g_dec[half, h // 2, p:p + 1], o[half, hd],
                                                                   ALU.mult, ALU.add)
                                else:
                                    ins = dve.tensor_copy(g_s[half, p, hd], o[half, hd])
                                if h == 3:
                                    v.read(ins, keys[0])
                                else:
                                    v.did(ins)
                        elif kind == "g_level":
                            i = arg[0]
                            b = LEVELS[i]
                            dve.wait_ge(g_kd, 2) if i == 0 else dve.wait_ge(g_key, i)
                            bb = g_b[:, :].rearrange("p (n b) -> p n b", b=2 * b)
                            d = g_d[:, :].rearrange("p (n b) -> p n b", b=2 * b)
                            mid = bcast(bb[:, :, b - 1], b)
                            v.did(dve.tensor_tensor(d[:, :, 0:b], mid, bb[:, :, 0:b], ALU.subtract))
                            v.did(dve.tensor_tensor(d[:, :, b:2 * b], bb[:, :, b:2 * b], mid, ALU.subtract), g_diff)
                            dve.wait_ge(g_exp, 4 + i)
                            full(dve, ("g_level", i - 2, 1) if i >= 2 else ("g_ktok", 1))

                            def second(x):
                                return x.rearrange("p (n b) -> p n b", b=2 * b)[:, :, b:2 * b]

                            qq = g_q[:, :, :].rearrange("p a b -> p (a b)")
                            v.did(dve.tensor_tensor(second(g_g[:, i % 2, :]), second(qq), second(g_d[:, :]), ALU.mult),
                                  g_query)
                        elif kind == "g_merge":
                            i = arg[0]
                            b = LEVELS[i]
                            mask = levelmask[:, i, :].rearrange("p (m b) -> p m b", b=b)
                            mask = mask.unsqueeze(1).broadcast_to([P, 2, 256 // b, b])
                            for par in range(2):
                                key = ("g_level", i, par)
                                full(dve, key)
                                dst = g_att[:, :, :].rearrange("p (t e) n -> p t e n", e=2)[:, :, par, :]
                                dst = dst.rearrange("p t (m b) -> p t m b", b=2 * b)[:, :, :, b:2 * b]
                                src = bank(key)[:, :].rearrange("p (t m b) -> p t m b", t=2, b=b)
                                v.read(dve.copy_predicated(dst, mask, src), key)
                        elif kind == "g_norm":
                            for h in range(4):
                                was_read(dve, keys[h])
                                w = g_att[:, h, :]
                                v.did(dve.reciprocal(w, w))
                                v.settle()
                                v.did(dve.scalar_tensor_tensor(w, g_o[:, h, :], col("gla_g"), w, ALU.mult, ALU.mult))
                                v.settle()
                                silu_done(dve, "gz", h)
                                v.did(dve.tensor_tensor(yT[:, 8 + h, :], w, yT[:, 8 + h, :], ALU.mult), g_done)
                        elif kind == "a_s":
                            p = arg[0]
                            st = a_st[:, p % 2, :]
                            mx = st[:, 0:8].rearrange("p (t e) -> p t e", e=2)
                            for par in range(2):
                                full(dve, keys[par])
                                v.did(dve.tensor_reduce(mx[:, :, par], chunks(bank(keys[par])[:, :]), AX_X, ALU.max))
                            v.settle()
                            v.did(dve.scalar_tensor_tensor(st[:, 8:16], st[:, 0:8], -0.125, neg_sinks,
                                                           ALU.mult, ALU.min))
                            v.settle()
                            v.did(dve.tensor_tensor(st[:, 16:24], cols[:, COL["sinks"]:COL["sinks"] + 8],
                                                    st[:, 8:16], ALU.add), a_max)
                            dve.wait_ge(a_exp, p + 1)
                            v.did(dve.tensor_tensor(st[:, 32:40], st[:, 16:24], st[:, 24:32], ALU.add))
                            v.settle()
                            v.did(dve.reciprocal(st[:, 32:40], st[:, 32:40]), a_rden)
                        elif kind == "a_pt":
                            p = arg[0]
                            full(dve, keys[1])
                            if p >= 2:
                                full(dve, ("a_pv", p - 2, 0))
                            v.read(dve.tensor_copy(a_pt[:, p % 2, 512:1024], bank(keys[1])[:, :]), keys[1])
                        elif kind == "a_pv":
                            p = arg[0]
                            full(dve, keys[0])
                            z = yT[:, 12:16, p * P:(p + 1) * P]
                            v.read(dve.tensor_tensor(z, chunks(o[:, :]), z, ALU.mult), keys[0])
                        elif kind in ("out1", "out2"):
                            j = arg[0]
                            full(dve, keys[0])
                            dve.wait_ge(x_back, 16)
                            v.read(dve.scalar_tensor_tensor(xT[:, j, :], o[:, :], mod[:, 16 + j:17 + j], xT[:, j, :],
                                                            ALU.mult, ALU.add), keys[0])

            numbers = sorted(s.num for s in layer)
            assert numbers == list(range(numbers[0], numbers[-1] + 1))
            nc.gpsimd.sem_clear(range(numbers[0], numbers[-1] + 1))
            nc.all_engine_barrier()

        with nc.Block() as block:
            @block.scalar
            def _(act):
                for t in range(KT_IN):
                    act.activation(hT[:, t, :], xT[:, t, :], ACT.Square).then_inc(squares, 1)
                act.wait_ge(bank_full[0], 1)
                act.activation(scr_t[:, 0, :], banks[0][:, :], ACT.Sqrt, bias=eps[:, 0:1], scale=1.0 / D_MODEL)\
                    .then_inc(bank_read[0], 1)

            @block.tensor
            def _(pe):
                for t in range(KT_IN):
                    pe.wait_ge(squares, t + 1)
                    mm = pe.matmul(banks[0][:, :], ones[:, :], hT[:, t, :], start=(t == 0), stop=(t == KT_IN - 1))
                mm.then_inc(bank_full[0], 1)

            @block.vector
            def _(dve):
                dve.wait_ge(bank_read[0], 1)
                dve.reciprocal(scr_t[:, 1, :], scr_t[:, 0, :]).then_inc(vec_order, 1)
                dve.wait_ge(vec_order, 1)
                for t in range(KT_IN):
                    dve.scalar_tensor_tensor(xT[:, t, :], xT[:, t, :], final_g[:, t:t + 1], scr_t[:, 1, :],
                                             ALU.mult, ALU.mult).then_inc(x_scaled, 1)

            @block.sync
            def _(sp):
                for t in range(KT_IN):
                    sp.wait_ge(x_scaled, t + 1)
                    sp.dma_start(out[:, t, :], xT[:, t, :]).then_inc(out_done, 16)
                sp.wait_ge(out_done, 16 * KT_IN)



def constants():
    c = np.zeros((P, 1410), np.float32)
    c[:, 0:128] = np.eye(P)
    c[:, 128:256] = np.triu(np.ones((P, P)))
    for head in (0, 64):
        for d in range(ROPE_DIM // 2):
            c[head + d + ROPE_DIM // 2, 256 + head + d] = -1.0
            c[head + d, 256 + head + d + ROPE_DIM // 2] = 1.0
    c[:, 384:896] = (np.arange(SEQ) % C != 0).astype(np.float32)
    inv = np.float32(ROPE_THETA) ** (-np.arange(0, ROPE_DIM, 2, dtype=np.float32) / np.float32(ROPE_DIM))
    for head in (0, 64):
        for d in range(ROPE_DIM):
            c[head + d, 896] = inv[d % (ROPE_DIM // 2)]
    for h in range(8):
        c[T_ACS + h, 898 + (h // 2) * P + 64 * (h % 2):898 + (h // 2) * P + 64 * (h % 2) + 64] = 1.0
    masks = np.zeros((P, len(LEVELS), 256), np.float32)
    s = np.arange(P)
    for i, b in enumerate(LEVELS):
        n = np.arange(P // (2 * b))
        m = (s[:, None] // (2 * b) == n[None, :]) & (s[:, None] % (2 * b) < b)
        masks[:, i, :] = np.tile(np.repeat(m, b, axis=1), (1, NC))
    return c, masks


def feature_tiles(w):
    k, n = w.shape[0] // P, w.shape[1] // P
    return w.reshape(k, P, n, P).transpose(2, 1, 0, 3).reshape(n, P, k * P)


def pack_ada(w_ada):
    t = np.stack([feature_tiles(w) for w in w_ada]).reshape(DEPTH, 12, 2, P, TILE_W)
    return np.ascontiguousarray(t.transpose(0, 1, 3, 2, 4).reshape(DEPTH, 12, P, 2 * TILE_W))


def pack_weights(w_in, w_out):
    tiles = np.zeros((DEPTH, len(SPLITS), P, TILE_W), np.float32)
    names = {"xs": (IN_OFF["xbc"], 512), "bc": (IN_OFF["xbc"] + 512, 512)}
    for l in range(DEPTH):
        gates = np.zeros((D_MODEL, P), np.float32)
        for at, name, n in ((R_DT, "dt", 8), (R_I, "mi", 4), (R_F, "mf", 4), (R_LR, "lr", 16)):
            gates[:, at:at + n] = w_in[l, :, IN_OFF[name]:IN_OFF[name] + n]
        tiles[l, SPLIT_NO[("gate", 0)]] = feature_tiles(gates)[0]
        for name, n in (("ak", 1), ("av", 1), ("gq", 2), ("gk", 2), ("mq", 4), ("mk", 4), ("mo", 4), ("mz", 4),
                        ("xs", 4), ("bc", 4), ("cz", 4), ("gz", 4), ("aq", 4), ("az", 4)):
            at = names[name][0] if name in names else IN_OFF[name]
            for t, w in enumerate(feature_tiles(w_in[l, :, at:at + n * P])):
                tiles[l, SPLIT_NO[(name, t)]] = w
        for name in ("mv", "gv"):
            w = w_in[l, :, IN_OFF[name]:IN_OFF[name] + 512].reshape(4, 2, P, 512)
            for q in range(4):
                tiles[l, SPLIT_NO[(name, q)]] = w[q].transpose(1, 0, 2).reshape(P, TILE_W)
        order = np.concatenate([w_out[l, Y_ROW[b]:Y_ROW[b] + 512] for b in ORDER], axis=0)
        early = feature_tiles(order[0:N_EARLY * P])
        late = feature_tiles(order[N_EARLY * P:])
        for j in range(8):
            tiles[l, SPLIT_NO[("o1", j, 0)]] = early[j][:, 0:TILE_W]
            tiles[l, SPLIT_NO[("o1", j, 1)], :, 0:512] = early[j][:, TILE_W:]
        for j in range(4):
            tiles[l, SPLIT_NO[("o2", j)]] = late[2 * j:2 * j + 2].transpose(1, 0, 2).reshape(P, TILE_W)
    return tiles


def pack_columns(a):
    out = np.zeros((DEPTH, P, N_COLS), np.float32)

    def put(name, v):
        out[:, :, COL[name]:COL[name] + v.shape[2]] = v

    def per_feature(v):
        return v.reshape(DEPTH, -1, P).transpose(0, 2, 1)

    put("norm_g", per_feature(a["norm_g"]))
    put("b_ada", per_feature(a["b_ada"]))
    put("gla_b", per_feature(a["gla_b_gate"]))
    put("gla_g", per_feature(a["gla_norm_g"]))
    put("ssd_g", per_feature(a["ssd_norm_g"]))
    put("m_g", per_feature(a["mlstm_norm_g"]))
    put("conv_b", np.concatenate([per_feature(a["ssd_conv_b"]), per_feature(a["mlstm_conv_b"])], axis=2))
    for at, name in ((0, "ssd_conv_w"), (32, "mlstm_conv_w")):
        w = a[name].reshape(DEPTH, 4, 8, P).transpose(0, 3, 2, 1).reshape(DEPTH, P, 32)
        out[:, :, COL["conv_w"] + at:COL["conv_w"] + at + 32] = w
    put("ssd_d", per_feature(np.repeat(a["ssd_d"], 64, axis=1)))
    g = COL["gate_b"]
    out[:, R_DT:R_DT + 8, g] = a["ssd_dt_bias"]
    out[:, R_I:R_I + 4, g] = a["mlstm_i_bias"]
    out[:, R_F:R_F + 4, g] = a["mlstm_f_bias"]
    out[:, 0:8, COL["a_log"]] = a["ssd_a_log"]
    out[:, :, COL["sinks"]:COL["sinks"] + 8] = a["swa_sinks"][:, None, :]
    return out


def host_arrays(inputs):
    a = {k: np.asarray(v) for k, v in inputs.items()}
    consts, masks = constants()
    return {
        "xT": np.ascontiguousarray(a["x"][0].T.reshape(KT_IN, P, SEQ).transpose(1, 0, 2)),
        "c": np.ascontiguousarray(a["c"].reshape(KT_IN, P).T),
        "pos": np.ascontiguousarray(np.broadcast_to(a["positions"].astype(np.int32).reshape(1, SEQ), (P, SEQ))),
        "cols": pack_columns(a),
        "wgate": np.ascontiguousarray(a["gla_w_gate"]),
        "final": np.ascontiguousarray(a["final_g"].reshape(KT_IN, P).T),
        "ada": pack_ada(a["w_ada"]),
        "weights": pack_weights(a["w_in"], a["w_out"]),
        "consts": consts,
        "masks": masks,
    }


def program(nc, arrays):
    aps = [nc.dram_tensor(f"in_{k}", v.shape, mybir.dt.from_np(v.dtype), kind="ExternalInput").ap()
           for k, v in arrays.items()]
    out = nc.dram_tensor("out", (P, KT_IN, SEQ), F32, kind="ExternalOutput").ap()
    x_kept = nc.dram_tensor("x_kept", (P, KT_IN, SEQ), F32, kind="Internal").ap()
    build(nc, *aps, x_kept, out)


def kernel(**inputs):
    import concourse.bacc as bacc
    from concourse.bass_utils import run_bass_kernel_spmd

    arrays = host_arrays(inputs)
    nc = bacc.Bacc("TRN2", target_bir_lowering=False, num_devices=1)
    program(nc, arrays)
    r = run_bass_kernel_spmd(nc, [{f"in_{k}": v for k, v in arrays.items()}], core_ids=[0])
    y = r.results[0]["out"]
    return np.ascontiguousarray(y.transpose(1, 0, 2).reshape(D_MODEL, SEQ).T)[None]
```

```python
from contextlib import ExitStack

import numpy as np

import concourse.bass as bass
from concourse import mybir

F32 = mybir.dt.float32
F32R = mybir.dt.float32r
I32 = mybir.dt.int32
U8 = mybir.dt.uint8
ALU = mybir.AluOpType
ACT = mybir.ActivationFunctionType
AX_X = mybir.AxisListType.X

P = 128
D_MODEL = 1024
SEQ = 512
DEPTH = 2
EPS = 1e-6
KT_IN = D_MODEL // P
C = 128
NC = SEQ // C
D_BRANCH = 512
BT = D_BRANCH // P
NB = 8
WIN = 64
ROPE_THETA = 500000.0
ROPE_DIM = 16
LEVELS = [64, 32, 16, 8, 4, 2, 1]

IN_SPLITS = [512, 128, 128, 512, 256, 256, 512, 512, 16, 1024, 8, 512, 512, 512, 512, 4, 4, 512, 512]
IN_NAMES = ["aq", "ak", "av", "az", "gq", "gk", "gv", "gz", "lr", "xbc", "dt", "cz",
            "mq", "mk", "mv", "mi", "mf", "mo", "mz"]
IN_OFF = dict(zip(IN_NAMES, np.cumsum([0] + IN_SPLITS[:-1]).tolist()))

ORDER = ["m", "c", "g", "a"]
Y_TILE = {"m": 0, "c": 4, "g": 8, "a": 12}
Y_ROW = {"a": 0, "g": 512, "c": 1024, "m": 1536}
N_EARLY = 12

R_DT, R_I, R_LR, R_F = 0, 32, 64, 96
T_C, T_R, T_R2, T_ACS = 0, 32, 64, 96

COL = {}
_n = 0
for _name, _w in [("norm_g", 8), ("b_ada", 24), ("gla_b", 2), ("gla_g", 1), ("ssd_g", 4), ("m_g", 4),
                  ("conv_b", 16), ("conv_w", 64), ("ssd_d", 4), ("gate_b", 1), ("a_log", 1), ("sinks", 8)]:
    COL[_name] = _n
    _n += _w
N_COLS = _n

TILE_W = 1024
RING = 4
SPLIT_RING = 3
ADA_EARLY = 8
ADA_SLOTS = 6


def between(steps, fill):
    out, n = [], 0
    for i, s in enumerate(steps):
        out.append(s)
        want = (i + 1) * len(fill) // len(steps)
        out += fill[n:want]
        n = want
    return out


def make_schedule():
    def proj(name, n=4):
        return [("proj", name, t) for t in range(n)]

    s = [("norm",), ("ada", 0)]
    for j in range(1, ADA_EARLY):
        s += [("ada", j), ("ada_col", j - 1)]
    s += [("ada_col", ADA_EARLY - 1), ("modulate",), ("proj", "gate", 0), ("rows",), ("proj", "ak", 0),
         ("proj", "av", 0), ("rope", "ak", 0), ("proj", "mq", 0), ("av",)]
    s += proj("mq")[1:] + proj("mk") + [("ada", j) for j in range(ADA_EARLY, 12)] + [("vtok", "mv")]
    s += [("ada_col", j) for j in range(ADA_EARLY, 12)]
    mo, mz, xs, bc, cz = (proj(n) for n in ("mo", "mz", "xs", "bc", "cz"))
    s += [("tok",), mo[0], ("mk_tok",), ("m_qk", 0), mo[1], ("m_state", 0), ("m_decay", 0), xs[0], ("m_state", 1), mo[2],
          ("m_qk", 1), xs[1], ("m_state", 2), ("m_decay", 1), mo[3], ("m_num", 0), xs[2], ("m_qk", 2), mz[0],
          ("m_decay", 2), xs[3], ("m_num", 1), mz[1], ("m_qk", 3), bc[0], ("m_decay", 3), ("m_square", 0), mz[2],
          ("m_num", 2), ("m_square", 1), bc[1], ("m_norm", 0), mz[3], ("m_num", 3), ("m_square", 2), bc[2],
          ("m_norm", 1), cz[0], ("m_square", 3), bc[3], ("m_norm", 2), cz[1], ("m_norm", 3), cz[2], cz[3]]
    gq, gk, gz, aq, az = proj("gq", 2), proj("gk", 2), proj("gz"), proj("aq"), proj("az")
    s += [("c_cb", 0), ("c_cb", 1), ("c_x", 0), ("c_x", 1), ("c_x", 2), ("c_x", 3), gq[0], ("c_b", 0), ("c_b", 1),
          ("c_decay", 0), ("c_decay", 1), gq[1], ("c_state", 0), ("c_state", 1), ("c_state", 2),
          ("c_decay", 2), ("c_decay", 3), gk[0], ("c_y", 0), ("c_decay", 4), ("c_decay", 5), ("c_y", 1),
          ("c_decay", 6), ("c_decay", 7), gk[1], ("c_square", 0), ("c_y", 2), ("c_y", 3), ("c_norm", 0),
          ("c_square", 1), gz[0], ("c_norm", 1), ("g_gate",), ("g_scan",), ("vtok", "gv"), ("g_decay",), ("g_diag",),
          gz[1], ("g_ktok",), ("g_prep", 0), gz[2], ("g_state", 0), ("g_state", 1), ("g_state", 2)]
    fill = [[gz[3]], [aq[0]], [("rope", "aq", 0), aq[1]], [("rope", "aq", 1), aq[2]], [("rope", "aq", 2), aq[3]],
            [("rope", "aq", 3), az[0]], []]
    for i in range(len(LEVELS)):
        s += ([("g_prep", i + 1)] if i + 1 < len(LEVELS) else []) + [("g_level", i)] + fill[i] + [("g_merge", i)]
    s += [az[1], ("g_out", 0), ("g_out", 1), ("g_out", 2), ("g_out", 3), az[2], ("g_norm", 0), ("g_norm", 1),
          ("y_split", 0), az[3], ("g_norm", 2), ("g_norm", 3), ("y_split", 1)]
    o1 = [[("outa", j), ("out1", j)] for j in range(8)]
    s += [("outa", 0), ("outa", 1), ("a_s", 0), ("out1", 0), ("outa", 2), ("a_s", 1), ("out1", 1), ("a_pt", 0),
          ("out1", 2)]
    s += [("a_s", 2), ("a_pv", 0), ("a_pt", 1)] + o1[3] + [("a_s", 3), ("a_pv", 1)] + o1[4] + [("a_pt", 2)] + o1[5]
    s += [("a_pv", 2), ("a_pt", 3)] + o1[6] + [("a_pv", 3)] + o1[7]
    s += [("out2", j) for j in range(8)] + [("square",)]
    return s


SCHEDULE = make_schedule()


def tiles_of(step):
    kind = step[0]
    one = {"square": 1, "norm": 0, "ada": 0, "ada_col": 1, "proj": 1, "av": 1, "rope": 1, "m_qk": 2, "m_decay": 2, "m_state": 2, "m_num": 2,
           "c_cb": 1, "c_x": 1, "c_b": 1, "c_state": 1, "c_decay": 1, "c_norm": 1, "g_ktok": 2, "g_gate": 2,
           "g_state": 1, "g_level": 2, "g_out": 1, "a_s": 2, "a_pt": 2, "a_pv": 1, "out1": 0, "out2": 1,
           "tok": 3, "mk_tok": 3, "vtok": 4, "m_norm": 1, "g_norm": 1, "g_diag": 4, "c_y": 3,
           "modulate": 0, "rows": 0, "y_split": 0, "g_prep": 0, "g_scan": 0, "m_square": 0, "c_square": 0, "g_decay": 0, "g_merge": 0}
    if kind == "outa":
        return [("out1", step[1], 0)]
    return [step + (i,) for i in range(one[kind])]


TILE = {}
for _step in SCHEDULE:
    for _key in tiles_of(_step):
        TILE[_key] = (len(TILE) % NB, len(TILE) // NB)

def weights_of(step):
    kind, arg = step[0], step[1:]
    if kind == "proj":
        return [arg]
    if kind == "vtok":
        return [(arg[0], q) for q in range(4)]
    if kind in ("outa", "out1"):
        return [("o1", arg[0], int(kind == "out1"))]
    if kind == "out2" and arg[0] % 2 == 0:
        return [("o2", arg[0] // 2)]
    return []


SPLITS = [w for s in SCHEDULE for w in weights_of(s)]
SPLIT_NO = {w: i for i, w in enumerate(SPLITS)}
WIDTH = {("o1", j, 1): 512 for j in range(8)}

USED_BY = {}
_n = 0
for _w in SPLITS:
    if _w[0] in ("mv", "gv") and _w[1] < 3 or _w[0] == "o1" and _w[2] == 0:
        _n += 1
        USED_BY[_w] = _n
    else:
        USED_BY[_w] = {"mv": ("vtok", _w[0], 3), "gv": ("vtok", _w[0], 3), "o1": ("out1", _w[1], 0),
                       "o2": ("out2", 2 * _w[1] + 1, 0)}.get(_w[0], ("proj",) + _w + (0,))


def releases(step):
    if step[0] == "out2":
        return [("o2", step[1] // 2)] if step[1] % 2 else []
    return weights_of(step)


def next_splits(step):
    n = [SPLIT_NO[w] + SPLIT_RING for w in releases(step)]
    n = [i if i < len(SPLITS) else None for i in n]
    return [i for i in n[:-1] if i is not None], [i for i in n[-1:] if i is not None]


ADA_BEFORE = {5: 8, 7: 9, 9: 10, 11: 11}
LAST_PROJ = max(i for i, w in enumerate(SPLITS) if w[0] not in ("o1", "o2"))
Y_SLOT = [10, 11, 12, 13, 14, 15, 4, 5, 6, 7, 8, 9, 0, 1, 2, 3]


def order_of(kinds):
    seen = [s[1:] for s in SCHEDULE if s[0] == "proj" and s[1] in kinds]
    return {k: i for i, k in enumerate(seen)}


CONV_NAMES = ("mq", "mk", "xs", "bc")
SILUS = order_of(CONV_NAMES + ("mz", "cz", "gz", "az"))
CONVS = order_of(CONV_NAMES)
CONV_TILE = {("xs", t): t for t in range(4)} | {("bc", t): 4 + t for t in range(4)} \
    | {("mq", t): 8 + t for t in range(4)} | {("mk", t): 12 + t for t in range(4)}
Z_OF = {"mz": "m", "cz": "c", "gz": "g", "az": "a"}
ROPES = {("ak", 0): 0} | {("aq", t): 1 + t for t in range(4)}

TWO_PI = 2.0 * np.pi
PI_HI = 6.28125
PI_MID = float(np.float32(np.floor((TWO_PI - PI_HI) * 2 ** 21) / 2 ** 21))
PI_LO = float(np.float32(TWO_PI - PI_HI - PI_MID))
ROUND = 12582912.0
PI_CLIP = 3.1415925


def bcast(ap, n):
    shape = list(ap.shape)
    return ap.unsqueeze(len(shape)).broadcast_to(shape + [n])


def mid_bcast(ap, n):
    p, a = ap.shape
    return ap.unsqueeze(1).broadcast_to([p, n, a])


def build(nc, xT_in, c_in, pos_in, cols_in, wgate_in, final_in, ada_in, weights, consts_in, masks_in, x_kept, out):
    ctx = ExitStack()
    with ctx:
        def sb(name, shape, dt=F32):
            return ctx.enter_context(nc.sbuf_tensor(name, shape, dt))

        at_x, at_h, at_y, at_r1, arena_size = 0, 4096, 8192, 16384, 30464
        arena_at = -(-nc.sbuf_base // 32) * 32
        sb("arena", [P, arena_size])
        assert nc.sbuf_base >= arena_at + 4 * arena_size

        def placed(name, at, shape, dt=F32):
            return nc.alloc_sbuf_tensor_at(name, shape, dt, offset=arena_at + 4 * at)

        xT = placed("xT", at_x, [P, KT_IN, SEQ])
        hT_hi = placed("hT_hi", at_x, [P, KT_IN, SEQ], F32R)
        hT = placed("hT", at_h, [P, KT_IN, SEQ])
        hT_lo = placed("hT_lo", at_h, [P, KT_IN, SEQ], F32R)
        yT = placed("yT", at_y, [P, 16, SEQ])
        y_lo = placed("y_lo", at_y, [P, 16, SEQ], F32R)
        r1 = placed("r1", at_r1, [P, 14080])
        y_hi = placed("y_hi", at_r1 + 4096, [P, 16, SEQ], F32R)
        ring = sb("ring", [P, RING, TILE_W])
        w_hi = sb("w_hi", [P, SPLIT_RING, TILE_W], F32R)
        w_lo = sb("w_lo", [P, SPLIT_RING, TILE_W], F32R)
        ident = sb("ident", [P, P])
        ones = sb("ones", [P, P])
        causal = sb("causal", [P, P])
        rot = sb("rot", [P, P])
        reset = sb("reset", [P, SEQ])
        invf = sb("invf", [P, 2])
        eps = sb("eps", [P, 1])
        levelmask = sb("levelmask", [P, len(LEVELS), 256], U8)
        cos = sb("cos", [P, SEQ])
        sin = sb("sin", [P, SEQ])
        neg = sb("neg", [1, WIN])
        cols = sb("cols", [P, N_COLS])
        ccol = sb("ccol", [P, KT_IN])
        mod = sb("mod", [P, 24])
        factor = sb("factor", [P, KT_IN])
        small = sb("small", [P, 64])
        half_b = small[:, 0:16]
        half_mg = small[:, 16:20]
        neg_sinks = small[:, 20:28]
        a_col = small[0:8, 28:29]
        final_g = small[:, 32:40]
        scr_in = sb("scr_in", [P, 2, SEQ + 4])
        scr_acc = sb("scr_acc", [P, 2, SEQ])
        scr_t = sb("scr_t", [P, 2, SEQ])
        gate_x = sb("gate_x", [P, SEQ])
        rows = sb("rows", [P, SEQ])
        dtm = sb("dtm", [P, SEQ])
        tok = sb("tok", [P, NC, P])
        dt_tok = sb("dt_tok", [P, NC, 8])
        edge = sb("edge", [P, NC, 24])
        edge_e = sb("edge_e", [P, NC, 24])
        kdup = sb("kdup", [P, 2, WIN + SEQ])
        v_al = sb("v_al", [P, NC, P])
        v_off = sb("v_off", [P, NC, P])
        wgate = dtm[R_LR:R_LR + 16, 0:256]
        pairsel = dtm[T_ACS:T_ACS + 8, :].rearrange("p (a b) -> p a b", a=4)
        r2 = sb("r2", [P, 4, SEQ])

        def cut(at, *shape):
            n = int(np.prod(shape))
            v = r1[:, at:at + n]
            if len(shape) == 2:
                v = v.rearrange("p (a b) -> p a b", a=shape[0])
            if len(shape) == 3:
                v = v.rearrange("p (a b c) -> p a b c", a=shape[0], b=shape[1])
            return v

        banks = [ctx.enter_context(nc.psum_tensor(f"bank{i}", [P, 512], F32)) for i in range(NB)]

        m_q, m_k, m_v = cut(0, 4, SEQ), cut(2048, 4, SEQ), cut(4096, NC, 512)
        m_kw, m_cs = cut(6144, 3, 512), cut(7680, 3, 512)
        m_w, m_pt, m_qw = cut(9216, 2, SEQ), cut(10240, 2, SEQ), cut(11264, 2, SEQ)
        m_em, m_ad, m_ns = cut(12288, 2, SEQ), cut(13312, SEQ), cut(13824, 3, 4)
        m_max = dtm[32:36, :]
        av_t = cut(12288, SEQ)
        ada_w = cut(0, ADA_SLOTS, 2048)

        def ada_sums(j, half):
            return ada_w[:, j % ADA_SLOTS, half * TILE_W:half * TILE_W + 256]

        sum_bank = banks[TILE[("square", 0)][0]]
        m_o = yT[:, 12:16, :]
        g_q, g_k, g_v = cut(0, 2, SEQ), cut(1024, 2, SEQ), cut(2048, NC, 512)
        g_o = cut(0, 4, SEQ)
        c_x = yT[:, 8:12, :]
        c_b, c_c = r2[:, 0:2, :], r2[:, 2:4, :]
        c_xdt, c_xdd = cut(4096, NC, 512), cut(6144, 3, 512)
        c_bt, c_cb = cut(7680, 2, 384), cut(8448, 2, SEQ)
        c_sqs = cut(6144, 4, SEQ)
        c_ss, c_l = cut(9472, 3, 512), cut(11008, 4, SEQ)
        c_e2, c_tmp = cut(13056, SEQ), cut(13568, SEQ)
        g_att, g_b = cut(4096, 4, SEQ), cut(6144, 1024)
        g_g, g_d = cut(7168, 2, 1024), cut(9216, 1024)
        g_kt, g_s = cut(10240, 2, 384), cut(11008, 3, 512)
        g_qb, g_dec = cut(12544, 1024), cut(13568, 2, NC)
        g_sqs = cut(7168, 4, SEQ)
        a_q = r2
        a_p, a_pt, a_st = cut(0, 2, 1024), cut(2048, 2, 1024), cut(13600, 2, 40)

        masks_f = cut(2048, len(LEVELS), 64)

        layer = []

        def sem(name):
            s = ctx.enter_context(nc.semaphore(name))
            layer.append(s)
            return s

        bank_full = [sem(f"bank_full{i}") for i in range(NB)]
        bank_read = [sem(f"bank_read{i}") for i in range(NB)]
        w_in = [sem(f"w_in{i}") for i in range(RING)]
        ada_w_in = [sem(f"ada_w_in{i}") for i in range(ADA_SLOTS)]
        w_hi_ready, w_lo_ready, w_used = sem("w_hi_ready"), sem("w_lo_ready"), sem("w_used")
        x_back, ada_sum, root = sem("x_back"), sem("ada_sum"), sem("root")
        y_hi_ready, y_ready = sem("y_hi_ready"), sem("y_ready")
        layer_in = sem("layer_in")
        vec_order, act_order, pool_order = sem("vec_order"), sem("act_order"), sem("pool_order")
        squares_sum = sem("squares_sum")
        squares, x_scaled, h_ready = sem("squares"), sem("x_scaled"), sem("h_ready")
        h_mod, h_hi_ready, a_log_exp = sem("h_mod"), sem("h_hi_ready"), sem("a_log_exp")
        conv_acc, conv_tanh, silu_out = sem("conv_acc"), sem("conv_tanh"), sem("silu_out")
        rope_cos, rope_out = sem("rope_cos"), sem("rope_out")
        gate_ln, rows_ready, edge_exp = sem("gate_ln"), sem("rows_ready"), sem("edge_exp")
        m_exp_in, m_exp, m_masked = sem("m_exp_in"), sem("m_exp"), sem("m_masked")
        m_query, m_decayed, m_h, m_sq, m_done = sem("m_query"), sem("m_decayed"), sem("m_h"), sem("m_sq"), sem("m_done")
        c_xdd_s, c_decayed, c_exp_in, c_exp = sem("c_xdd_s"), sem("c_decayed"), sem("c_exp_in"), sem("c_exp")
        c_l_s, c_gated, c_sq, c_done = sem("c_l_s"), sem("c_gated"), sem("c_sq"), sem("c_done")
        g_ln, g_diff, g_exp, g_kd = sem("g_ln"), sem("g_diff"), sem("g_exp"), sem("g_kd")
        g_key, g_query, g_sq, g_done = sem("g_key"), sem("g_query"), sem("g_sq"), sem("g_done")
        a_max, a_exp, a_rden, a_prob = sem("a_max"), sem("a_exp"), sem("a_rden"), sem("a_prob")
        once = ctx.enter_context(nc.semaphore("once"))
        once_pos = ctx.enter_context(nc.semaphore("once_pos"))
        once_x, once_sq = ctx.enter_context(nc.semaphore("once_x")), ctx.enter_context(nc.semaphore("once_sq"))
        once_ones = ctx.enter_context(nc.semaphore("once_ones"))
        x_stored = ctx.enter_context(nc.semaphore("x_stored"))
        once_d = ctx.enter_context(nc.semaphore("once_d"))
        once_v = ctx.enter_context(nc.semaphore("once_v"))
        once_ang = ctx.enter_context(nc.semaphore("once_ang"))
        once_a = ctx.enter_context(nc.semaphore("once_a"))
        out_done = ctx.enter_context(nc.semaphore("out_done"))

        def bank(key):
            return banks[TILE[key][0]]

        def full(eng, key):
            b, n = TILE[key]
            eng.wait_ge(bank_full[b], n + 1)

        def was_read(eng, key):
            b, n = TILE[key]
            eng.wait_ge(bank_read[b], n + 1)

        def used(eng, w):
            by = USED_BY[w]
            if isinstance(by, tuple):
                full(eng, by)
            else:
                eng.wait_ge(w_used, by)

        def silu_done(eng, name, t):
            eng.wait_ge(silu_out, SILUS[(name, t)] + 1)

        def merged(eng):
            for par in range(2):
                was_read(eng, ("g_level", len(LEVELS) - 1, par))

        def vacant(eng, key):
            b, n = TILE[key]
            if n:
                eng.wait_ge(bank_read[b], n)

        class Line:

            def __init__(self, eng, own):
                self.eng, self.own, self.count, self.last = eng, own, {}, None

            def did(self, ins, signal=None):
                s = self.own if signal is None else signal
                ins.then_inc(s, 1)
                self.count[s.name] = self.count.get(s.name, 0) + 1
                self.last = (s, self.count[s.name])

            def read(self, ins, key):
                b, n = TILE[key]
                ins.then_inc(bank_read[b], 1)
                self.last = (bank_read[b], n + 1)

            def settle(self):
                if self.last:
                    self.eng.wait_ge(*self.last)

        with nc.Block() as block:
            @block.sync
            def _(sp):
                for dst, src in ((scr_t[:, 1, :].bitcast(I32), pos_in), (invf[:, :], consts_in[:, 896:898]),
                                 (ccol[:, :], c_in)):
                    sp.dma_start(dst, src).then_inc(once_pos, 16)
                sp.dma_start(xT[:, :, :], xT_in).then_inc(once_x, 16)
                loads = [(final_g, final_in),
                         (ident[:, :], consts_in[:, 0:128]), (causal[:, :], consts_in[:, 128:256]),
                         (rot[:, :], consts_in[:, 256:384]), (reset[:, :], consts_in[:, 384:896]),
                         (dtm[T_ACS:T_ACS + 8, :], consts_in[T_ACS:T_ACS + 8, 898:1410]), (masks_f, masks_in)]
                for dst, src in loads:
                    sp.dma_start(dst, src).then_inc(once, 16)
                sp.wait_ge(once_x, 16)
                for t in range(KT_IN):
                    sp.dma_start(x_kept[:, t, :], xT[:, t, :]).then_inc(x_stored, 16)
                sp.wait_ge(once, 16 * len(loads))
                sp.sem_inc(once_v, 1)

            @block.tensor
            def _(pe):
                pe.wait_ge(once_ones, 1)
                for t in range(KT_IN):
                    pe.wait_ge(once_sq, t + 1)
                    pe.matmul(sum_bank[:, :], ones[:, :], hT[:, t, :], start=(t == 0), stop=(t == KT_IN - 1))

            @block.gpsimd
            def _(pool):
                pool.memset(ones[:, :], 1.0).then_inc(once_ones, 1)
                pool.memset(eps[:, :], EPS)
                pool.memset(neg[:, :], -1.0e30)
                pool.memset(scr_in[:, :, :], 0.0)
                pool.memset(rows[:, :], 0.0)
                pool.memset(kdup[:, :, :], 0.0)
                pool.memset(v_off[:, :, :], 0.0)

            @block.vector
            def _(dve):
                v = Line(dve, once_d)
                dve.wait_ge(once_pos, 48)
                ang, r = scr_acc[:, 0, :], scr_t[:, 0, :]
                v.did(dve.tensor_copy(r, scr_t[:, 1, :].bitcast(I32)))
                v.settle()
                v.did(dve.tensor_scalar(ang, r, invf[:, 0:1], None, ALU.mult))
                v.settle()
                both = ((0.0, r1[:, 0:512], r1[:, 1024:1536]), (0.25, r1[:, 512:1024], r1[:, 1536:2048]))
                for quarter, dst, k in both:
                    v.did(dve.tensor_scalar(k, ang, 1.0 / TWO_PI, quarter, ALU.mult, ALU.add))
                for x in (ROUND, -ROUND):
                    v.settle()
                    for quarter, dst, k in both:
                        v.did(dve.tensor_scalar(k, k, x, None, ALU.add))
                for part in (PI_HI, PI_MID, PI_LO):
                    v.settle()
                    for quarter, dst, k in both:
                        v.did(dve.scalar_tensor_tensor(dst, k, -part, ang if part == PI_HI else dst,
                                                       ALU.mult, ALU.add))
                v.settle()
                for quarter, dst, k in both:
                    v.did(dve.tensor_scalar(dst, dst, quarter * TWO_PI, PI_CLIP, ALU.add, ALU.min))
                v.settle()
                for quarter, dst, k in both:
                    v.did(dve.tensor_scalar(dst, dst, -PI_CLIP, None, ALU.max))
                v.settle()
                dve.sem_inc(once_ang, 1)
                dve.wait_ge(once_v, 1)
                v.did(dve.tensor_copy(levelmask[:, :, :].rearrange("p i (c b) -> p i c b", c=NC),
                                      masks_f.unsqueeze(2).broadcast_to([P, len(LEVELS), NC, 64])))

            @block.scalar
            def _(act):
                act.wait_ge(once_pos, 48)
                th = small[:, 52:60]
                act.activation(th, ccol[:, :], ACT.Tanh, scale=0.5).then_inc(once_a, 1)
                act.wait_ge(once_a, 1)
                act.activation(th, th, ACT.Copy, bias=1.0).then_inc(once_a, 1)
                act.wait_ge(once_a, 2)
                for t in range(KT_IN):
                    act.activation(ccol[:, t:t + 1], ccol[:, t:t + 1], ACT.Copy, scale=th[:, t:t + 1])\
                        .then_inc(once_a, 1)
                act.wait_ge(once_a, 2 + KT_IN)
                act.activation(ccol[:, :], ccol[:, :], ACT.Copy, scale=0.5)
                act.wait_ge(once_x, 16)
                for t in range(KT_IN):
                    act.activation(hT[:, t, :], xT[:, t, :], ACT.Square).then_inc(once_sq, 1)
                act.wait_ge(once_ang, 1)
                act.activation(sin[:, :], r1[:, 0:512], ACT.Sin)
                act.activation(cos[:, :], r1[:, 512:1024], ACT.Sin)

        with nc.Fori(0, DEPTH) as l:
            with nc.Block() as block:
                @block.sync
                def _(sp):
                    sp.dma_start(cols[:, :], cols_in[bass.ds(l, 1)].rearrange("a p n -> (a p) n"))\
                        .then_inc(layer_in, 16)
                    sp.dma_start(wgate, wgate_in[bass.ds(l, 1)].rearrange("a p n -> (a p) n"))\
                        .then_inc(layer_in, 16)

                    def load_ada(j):
                        at = j % ADA_SLOTS
                        if j >= ADA_SLOTS:
                            full(sp, ("ada_col", j - ADA_SLOTS, 0))
                        sp.dma_start(ada_w[:, at, :], ada_in[bass.ds(l, 1), j].rearrange("a p n -> (a p) n"))\
                            .then_inc(ada_w_in[at], 16)

                    for j in range(ADA_EARLY):
                        load_ada(j)
                    for i, w in enumerate(SPLITS):
                        if i in ADA_BEFORE:
                            load_ada(ADA_BEFORE[i])
                        if i == LAST_PROJ + SPLIT_RING + RING:
                            sp.wait_ge(x_stored, 16 * KT_IN)
                            used(sp, SPLITS[LAST_PROJ])
                            sp.sem_clear(x_stored)
                            sp.dma_start(xT[:, :, :], x_kept).then_inc(x_back, 16)
                        if i >= RING:
                            sp.wait_ge(w_lo_ready, i - RING + 1)
                        n = WIDTH.get(w, TILE_W)
                        src = weights[bass.ds(l, 1), i, :, 0:n].rearrange("a p n -> (a p) n")
                        sp.dma_start(ring[:, i % RING, 0:n], src).then_inc(w_in[i % RING], 16)
                    for j in range(KT_IN):
                        was_read(sp, ("out2", j, 0))
                        sp.dma_start(x_kept[:, j, :], xT[:, j, :]).then_inc(x_stored, 16)

                @block.tensor
                def _(pe):
                    def end(mm, key):
                        mm.then_inc(bank_full[TILE[key][0]], 1)

                    def split_tile(w):
                        i = SPLIT_NO[w]
                        pe.wait_ge(w_lo_ready, i + 1)
                        return [t[:, i % SPLIT_RING, :] for t in (w_hi, w_lo)]

                    def product(o, a, b, start, stop):
                        pe.matmul(o, a[0], b[0], start=start, stop=False)
                        pe.matmul(o, a[0], b[1], start=False, stop=False)
                        return pe.matmul(o, a[1], b[0], start=False, stop=stop)

                    for step in SCHEDULE:
                        kind, arg = step[0], step[1:]
                        keys = tiles_of(step)
                        for key in keys[:1]:
                            vacant(pe, key)
                        o = bank(keys[0]) if keys else None
                        if kind == "norm":
                            pe.wait_ge(root, 1)
                        elif kind == "square":
                            pe.wait_ge(squares_sum, KT_IN - 2)
                            pe.matmul(sum_bank[:, :], ones[:, :], hT[:, 0, :], start=True, stop=False)
                            pe.wait_ge(squares, KT_IN)
                            pe.matmul(sum_bank[:, :], ones[:, :], hT[:, KT_IN - 1, :], start=False, stop=True)
                        elif kind == "ada_col":
                            pe.wait_ge(ada_sum, arg[0] + 1)
                            for t in range(2):
                                for half in range(2):
                                    mm = pe.matmul(o[:, t:t + 1], ada_sums(arg[0], half)[:, t * P:(t + 1) * P],
                                                   ones[:, 0:1], start=(half == 0), stop=(half == 1))
                            end(mm, keys[0])
                        elif kind == "proj":
                            w = split_tile(arg)
                            for k in range(KT_IN):
                                if arg[0] == "gate":
                                    pe.wait_ge(h_ready, k + 1)
                                mm = product(o[:, :], [x[:, k * P:(k + 1) * P] for x in w],
                                             [x[:, k, :] for x in (hT_hi, hT_lo)], k == 0, k == KT_IN - 1)
                            end(mm, keys[0])
                        elif kind == "rope":
                            i = ROPES[arg]
                            was_read(pe, ("proj",) + arg + (0,))
                            end(pe.matmul(o[:, :], rot[:, :], scr_in[:, i % 2, 3:3 + SEQ], start=True, stop=True), keys[0])
                        elif kind == "av":
                            was_read(pe, ("proj", "av", 0, 0))
                            for p in range(NC):
                                mm = pe.transpose(o[:, p * P:(p + 1) * P], av_t[:, p * P:(p + 1) * P], ident[:, :])
                            end(mm, keys[0])
                        elif kind == "vtok":
                            for q in range(4):
                                w = split_tile((arg[0], q))
                                for p in range(NC):
                                    if q == 0 and p:
                                        vacant(pe, keys[p])
                                    for k in range(2):
                                        mm = product(bank(keys[p])[:, :],
                                                     [x[:, 2 * q + k, p * P:(p + 1) * P] for x in (hT_hi, hT_lo)],
                                                     [x[:, k * 512:(k + 1) * 512] for x in w],
                                                     q == 0 and k == 0, q == 3 and k == 1)
                                    if q == 3:
                                        end(mm, keys[p])
                                if q < 3:
                                    mm.then_inc(w_used, 1)
                        elif kind == "tok":
                            pe.wait_ge(rows_ready, 1)
                            for p in range(NC):
                                mm = pe.transpose(o[:, p * P:(p + 1) * P], rows[:, p * P:(p + 1) * P], ident[:, :])
                            end(mm, keys[0])
                            vacant(pe, keys[1])
                            for p in range(NC):
                                mm = pe.transpose(bank(keys[1])[:, p * 8:(p + 1) * 8], dtm[0:8, p * P:(p + 1) * P],
                                                  ident[0:8, 0:8])
                            end(mm, keys[1])
                            vacant(pe, keys[2])
                            was_read(pe, keys[0])
                            end(pe.matmul(bank(keys[2])[:, :], ident[:, P - 1:P].broadcast_to([P, P]),
                                          tok[:, :, :].rearrange("p a b -> p (a b)"), start=True, stop=True), keys[2])
                        elif kind == "mk_tok":
                            silu_done(pe, "mk", 3)
                            for p in range(3):
                                if p:
                                    vacant(pe, keys[p])
                                for h in range(4):
                                    mm = pe.transpose(bank(keys[p])[:, h * P:(h + 1) * P],
                                                      m_k[:, h, p * P:(p + 1) * P], ident[:, :])
                                end(mm, keys[p])
                        elif kind == "m_qk":
                            h = arg[0]
                            silu_done(pe, "mk", 3)
                            for p in range(NC):
                                tk = slice(p * P, (p + 1) * P)
                                mm = pe.matmul(o[:, tk], m_k[:, h, tk], m_q[:, h, tk], start=True, stop=True)
                            end(mm, keys[0])
                            vacant(pe, keys[1])
                            end(pe.matmul(bank(keys[1])[:, :], ident[T_R:T_R + 4, T_R + h:T_R + h + 1]
                                          .broadcast_to([4, P]), rows[T_R:T_R + 4, :], start=True, stop=True), keys[1])
                        elif kind == "m_decay":
                            h = arg[0]
                            end(pe.matmul(o[:, :], ident[T_R2:T_R2 + 4, T_R2 + h:T_R2 + h + 1].broadcast_to([4, P]),
                                          rows[T_R2:T_R2 + 4, :], start=True, stop=True), keys[0])
                            vacant(pe, keys[1])
                            end(pe.matmul(bank(keys[1])[:, :], ident[32:36, 32 + h:33 + h].broadcast_to([4, P]),
                                          m_max, start=True, stop=True), keys[1])
                        elif kind == "m_state":
                            p = arg[0]
                            was_read(pe, ("mk_tok", p))
                            was_read(pe, ("vtok", "mv", p))
                            for h in range(4):
                                hd = slice(h * P, (h + 1) * P)
                                mm = pe.matmul(o[:, hd], m_kw[:, p, hd], m_v[:, p, hd], start=True, stop=True)
                            end(mm, keys[0])
                            vacant(pe, keys[1])
                            for h in range(4):
                                hd = slice(h * P, (h + 1) * P)
                                mm = pe.matmul(bank(keys[1])[:, h:h + 1], m_kw[:, p, hd], ones[:, 0:1],
                                               start=True, stop=True)
                            end(mm, keys[1])
                        elif kind == "m_num":
                            h = arg[0]
                            hd = slice(h * P, (h + 1) * P)
                            was_read(pe, ("m_qk", h, 0))
                            pe.wait_ge(m_query, h + 1)
                            was_read(pe, ("m_state", 2, 0))
                            was_read(pe, ("m_state", 2, 1))
                            was_read(pe, ("vtok", "mv", 3))
                            for p in range(NC):
                                tk = slice(p * P, (p + 1) * P)
                                mm = pe.matmul(o[:, tk], m_v[:, p, hd], m_pt[:, h % 2, tk], start=True, stop=(p == 0))
                                if p:
                                    mm = pe.matmul(o[:, tk], m_cs[:, p - 1, hd], m_qw[:, h % 2, tk],
                                                   start=False, stop=True)
                            end(mm, keys[0])
                            vacant(pe, keys[1])
                            d = bank(keys[1])
                            pe.matmul(d[:, :], ones[:, :], m_pt[:, h % 2, :], start=True, stop=False)
                            for p in range(1, NC):
                                tk = slice(p * P, (p + 1) * P)
                                mm = pe.matmul(d[:, tk], m_ns[:, p - 1, h:h + 1].broadcast_to([P, P]), m_qw[:, h % 2, tk],
                                               start=False, stop=(p == NC - 1))
                            end(mm, keys[1])
                        elif kind == "m_norm":
                            pe.wait_ge(m_sq, arg[0] + 1)
                            end(pe.matmul(o[:, :], ones[:, :], m_k[:, arg[0], :], start=True, stop=True), keys[0])
                        elif kind == "c_cb":
                            g = arg[0]
                            silu_done(pe, "bc", 3)
                            for p in range(NC):
                                tk = slice(p * P, (p + 1) * P)
                                mm = pe.matmul(o[:, tk], c_b[:, g, tk], c_c[:, g, tk], start=True, stop=True)
                            end(mm, keys[0])
                        elif kind == "c_x":
                            p = arg[0]
                            for t in range(4):
                                mm = pe.transpose(o[:, t * P:(t + 1) * P], c_x[:, t, p * P:(p + 1) * P], ident[:, :])
                            end(mm, keys[0])
                        elif kind == "c_b":
                            g = arg[0]
                            for p in range(3):
                                mm = pe.transpose(o[:, p * P:(p + 1) * P], c_b[:, g, p * P:(p + 1) * P], ident[:, :])
                            end(mm, keys[0])
                        elif kind == "c_state":
                            p = arg[0]
                            pe.wait_ge(c_xdd_s, p + 1)
                            was_read(pe, ("c_b", 1, 0))
                            was_read(pe, ("c_b", 0, 0))
                            for g in range(2):
                                mm = pe.matmul(o[:, g * 256:(g + 1) * 256], c_bt[:, g, p * P:(p + 1) * P],
                                               c_xdd[:, p, g * 256:(g + 1) * 256], start=True, stop=True)
                            end(mm, keys[0])
                        elif kind == "c_decay":
                            h = arg[0]
                            end(pe.matmul(o[:, :], ident[T_ACS:T_ACS + 8, T_ACS + h:T_ACS + h + 1].broadcast_to([8, P]),
                                          rows[T_ACS:T_ACS + 8, :], start=True, stop=True), keys[0])
                        elif kind == "c_y":
                            t = arg[0]
                            g = t // 2
                            for h in (2 * t, 2 * t + 1):
                                pe.wait_ge(c_l_s, h + 1)
                                lo = WIN * (h % 2)
                                for p in range(NC):
                                    if h == 0:
                                        was_read(pe, ("c_x", p, 0))
                                    tk = slice(p * P, (p + 1) * P)
                                    mm = pe.matmul(o[lo:lo + WIN, tk], c_xdt[:, p, h * 64:(h + 1) * 64],
                                                   c_l[:, h % 4, tk], start=True, stop=True)
                            end(mm, keys[0])
                            vacant(pe, keys[1])
                            was_read(pe, ("c_state", 2, 0))
                            for p in range(1, NC):
                                tk = slice(p * P, (p + 1) * P)
                                mm = pe.matmul(bank(keys[1])[:, tk], c_ss[:, p - 1, t * P:(t + 1) * P],
                                               c_c[:, g, tk], start=True, stop=True)
                            end(mm, keys[1])
                            vacant(pe, keys[2])
                            end(pe.matmul(bank(keys[2])[:, :], pairsel[:, t, :],
                                          rows[T_ACS:T_ACS + 8, :], start=True, stop=True), keys[2])
                        elif kind == "c_norm":
                            for j in range(2):
                                pe.wait_ge(c_sq, 2 * arg[0] + j + 1)
                                mm = pe.matmul(o[:, :], ones[:, :], c_sqs[:, 2 * arg[0] + j, :],
                                               start=(j == 0), stop=(j == 1))
                            end(mm, keys[0])
                        elif kind == "g_gate":
                            for t in range(2):
                                if t:
                                    vacant(pe, keys[t])
                                pe.wait_ge(layer_in, 32)
                                end(pe.matmul(bank(keys[t])[:, :], wgate[:, t * P:(t + 1) * P],
                                              gate_x[R_LR:R_LR + 16, :], start=True, stop=True), keys[t])
                        elif kind == "g_ktok":
                            pe.wait_ge(g_kd, 2)
                            for t in range(2):
                                if t:
                                    vacant(pe, keys[t])
                                for p in range(3):
                                    mm = pe.transpose(bank(keys[t])[:, p * P:(p + 1) * P],
                                                      g_g[:, 0, t * SEQ + p * P:t * SEQ + (p + 1) * P], ident[:, :])
                                end(mm, keys[t])
                        elif kind == "g_state":
                            p = arg[0]
                            for t in range(2):
                                was_read(pe, ("g_ktok", t))
                            for q in range(4):
                                was_read(pe, ("vtok", "gv", q))
                            for h in range(4):
                                mm = pe.matmul(o[:, h * P:(h + 1) * P], g_kt[:, h // 2, p * P:(p + 1) * P],
                                               g_v[:, p, h * P:(h + 1) * P], start=True, stop=True)
                            end(mm, keys[0])
                        elif kind == "g_diag":
                            for t in range(2):
                                was_read(pe, ("proj", "gq", t, 0))
                                was_read(pe, ("proj", "gk", t, 0))
                            for h in range(4):
                                if h:
                                    vacant(pe, keys[h])
                                lo = 64 * (h % 2)
                                for p in range(NC):
                                    tk = slice(p * P, (p + 1) * P)
                                    mm = pe.matmul(bank(keys[h])[:, tk], g_k[lo:lo + 64, h // 2, tk],
                                                   g_q[lo:lo + 64, h // 2, tk], start=True, stop=True)
                                end(mm, keys[h])
                        elif kind == "g_level":
                            i = arg[0]
                            b = LEVELS[i]
                            pe.wait_ge(g_key, i + 1)
                            pe.wait_ge(g_query, i + 1)
                            vacant(pe, keys[1])
                            for t in range(2):
                                for p in range(NC):
                                    at = t * SEQ + p * P
                                    for par in range(2):
                                        lo = 64 * par
                                        src = g_g[lo:lo + 64, i % 2, at:at + P]
                                        second = src.rearrange("p (n b) -> p n b", b=2 * b)[:, :, b:2 * b]
                                        mm = pe.matmul(bank(keys[par])[:, (t * NC + p) * 64:(t * NC + p + 1) * 64],
                                                       src, second, start=True, stop=True)
                                        if (t, p) == (1, NC - 1):
                                            end(mm, keys[par])
                        elif kind == "g_out":
                            h = arg[0]
                            hd = slice(h * P, (h + 1) * P)
                            merged(pe)
                            was_read(pe, ("g_state", 2, 0))
                            pe.wait_ge(g_kd, 3)
                            for p in range(NC):
                                tk = slice(p * P, (p + 1) * P)
                                mm = pe.matmul(o[:, tk], g_v[:, p, hd], g_att[:, h, tk], start=True, stop=(p == 0))
                                if p:
                                    mm = pe.matmul(o[:, tk], g_s[:, p - 1, hd], g_qb[:, (h // 2) * SEQ + p * P:(h // 2) * SEQ + (p + 1) * P],
                                                   start=False, stop=True)
                            end(mm, keys[0])
                        elif kind == "g_norm":
                            pe.wait_ge(g_sq, arg[0] + 1)
                            end(pe.matmul(o[:, :], ones[:, :], g_sqs[:, arg[0], :], start=True, stop=True), keys[0])
                        elif kind == "a_s":
                            p = arg[0]
                            pe.wait_ge(rope_out, 5)
                            for par in range(2):
                                if par:
                                    vacant(pe, keys[par])
                                s = bank(keys[par])
                                lo = 64 * par
                                for e in range(2):
                                    q0 = (2 * p + e) * WIN
                                    for t in range(4):
                                        mm = pe.matmul(s[64 * e:64 * e + 64, t * P:(t + 1) * P],
                                                       a_q[lo:lo + 64, t, q0:q0 + WIN],
                                                       kdup[lo:lo + 64, t // 2, q0:q0 + 2 * WIN],
                                                       start=True, stop=not (p == 0 and e == 0))
                                        if p == 0 and e == 0:
                                            mm = pe.matmul(s[0:64, t * P:t * P + WIN], ones[0:1, 0:64],
                                                           neg[0:1, 0:WIN], start=False, stop=True)
                                end(mm, keys[par])
                        elif kind == "a_pt":
                            p = arg[0]
                            pe.wait_ge(a_prob, p + 1)
                            for g in range(2):
                                if g:
                                    vacant(pe, keys[g])
                                for j in range(4):
                                    h = 4 * g + j
                                    mm = pe.transpose(bank(keys[g])[:, j * P:(j + 1) * P],
                                                      a_p[:, p % 2, h * P:(h + 1) * P], ident[:, :])
                                end(mm, keys[g])
                        elif kind == "a_pv":
                            p = arg[0]
                            for g in range(2):
                                was_read(pe, ("a_pt", p, g))
                            was_read(pe, ("av", 0))
                            for hp in range(2):
                                for g in range(2):
                                    for e in range(2):
                                        v = (v_al if e else v_off)[:, p, g * 64:(g + 1) * 64]
                                        pr = a_pt[:, p % 2, :].rearrange("p (h q) -> p h q", h=8)
                                        for j in range(2):
                                            t = 2 * g + j
                                            mm = pe.matmul(o[64 * hp:64 * hp + 64, t * P + 64 * e:t * P + 64 * e + 64],
                                                           v, pr[:, 2 * t + hp, 64 * e:64 * e + 64],
                                                           start=True, stop=True)
                            end(mm, keys[0])
                        elif kind in ("outa", "out1"):
                            j, i = arg[0], int(kind == "out1")
                            key = ("out1", j, 0)
                            w = split_tile(("o1", j, i))
                            for k in range(8 * i, 8 if i == 0 else N_EARLY):
                                if j == 0:
                                    pe.wait_ge(y_ready, k + 1)
                                at = (k - 8 * i) * P
                                mm = product(bank(key)[:, :], [x[:, at:at + P] for x in w],
                                             [y_hi[:, Y_SLOT[k], :], y_lo[:, k, :]], k == 0, k == N_EARLY - 1)
                            if i == 0:
                                mm.then_inc(w_used, 1)
                            else:
                                end(mm, key)
                        elif kind == "out2":
                            j = arg[0]
                            pe.wait_ge(y_ready, N_EARLY + NC)
                            w = split_tile(("o2", j // 2))
                            for k in range(4):
                                at = ((j % 2) * 4 + k) * P
                                mm = product(o[:, :], [x[:, at:at + P] for x in w],
                                             [y_hi[:, Y_SLOT[N_EARLY + k], :], y_lo[:, N_EARLY + k, :]], k == 0, k == 3)
                            end(mm, keys[0])

                @block.scalar
                def _(act):
                    a = Line(act, act_order)

                    def apply(out, in_, func, **kw):
                        return act.activation(out, in_, func, **kw)

                    def split(i):
                        n = WIDTH.get(SPLITS[i], TILE_W)
                        act.wait_ge(w_in[i % RING], 16 * (i // RING + 1))
                        if i >= SPLIT_RING:
                            used(act, SPLITS[i - SPLIT_RING])
                        a.did(apply(w_hi[:, i % SPLIT_RING, 0:n], ring[:, i % RING, 0:n], ACT.Copy), w_hi_ready)

                    act.wait_ge(layer_in, 32)
                    a.did(apply(small[0:8, 29:30], cols[0:8, COL["a_log"]:COL["a_log"] + 1], ACT.Exp), a_log_exp)
                    for step in SCHEDULE:
                        kind, arg = step[0], step[1:]
                        keys = tiles_of(step)
                        within, after = next_splits(step)
                        for i in within:
                            split(i)
                        a.settle()
                        if kind == "norm":
                            a.did(apply(scr_t[:, 0, :], sum_bank[:, :], ACT.Sqrt, bias=eps[:, 0:1],
                                        scale=1.0 / D_MODEL), root)
                        elif kind == "out2":
                            j = arg[0]
                            was_read(act, keys[0])
                            a.did(apply(hT[:, j, :], xT[:, j, :], ACT.Square), squares)
                        elif kind == "modulate":
                            for i in range(SPLIT_RING):
                                split(i)
                            act.wait_ge(x_stored, 16 * KT_IN)
                            for t in range(KT_IN):
                                act.wait_ge(h_mod, t + 1)
                                a.did(apply(hT_hi[:, t, :], hT[:, t, :], ACT.Copy), h_hi_ready)
                        elif kind == "proj":
                            name, t = arg
                            o, key = bank(keys[0]), keys[0]
                            if name != "gate":
                                full(act, key)
                            if name == "gate":
                                pass
                            elif name == "av":
                                a.read(apply(av_t, o[:, :], ACT.Copy), key)
                            elif name in ("ak", "aq"):
                                i = ROPES[arg]
                                if i == 1:
                                    silu_done(act, "bc", 3)
                                if i >= 2:
                                    act.wait_ge(rope_out, i - 1)
                                a.read(apply(scr_in[:, i % 2, 3:3 + SEQ], o[:, :], ACT.Copy), key)
                            elif arg in CONVS:
                                i, u = CONVS[arg], SILUS[arg]
                                if i == 0:
                                    act.wait_ge(rope_out, 1)
                                if i >= 2:
                                    act.wait_ge(conv_acc, i - 1)
                                a.read(apply(scr_in[:, i % 2, 3:3 + SEQ], o[:, :], ACT.Copy, scale=0.5), key)
                                for n in after:
                                    split(n)
                                after = []
                                act.wait_ge(conv_acc, i + 1)
                                if u >= 2:
                                    act.wait_ge(silu_out, u - 1)
                                a.did(apply(scr_t[:, u % 2, :], scr_acc[:, u % 2, :], ACT.Tanh), conv_tanh)
                            elif arg in SILUS:
                                u = SILUS[arg]
                                act.wait_ge(silu_out, u - 1)
                                a.did(apply(scr_acc[:, u % 2, :], o[:, :], ACT.Copy, scale=0.5))
                                a.read(apply(scr_t[:, u % 2, :], o[:, :], ACT.Tanh, scale=0.5), key)
                            elif name == "mo":
                                a.read(apply(m_o[:, t, :], o[:, :], ACT.Tanh, scale=0.5), key)
                            else:
                                act.wait_ge(m_done, 4)
                                dst, scale = {"gq": (g_q, 0.125), "gk": (g_k, 1.0)}[name]
                                a.read(apply(dst[:, t, :], o[:, :], ACT.Copy, scale=scale), key)
                        elif kind == "rows":
                            was_read(act, ("proj", "gate", 0, 0))
                            w = scr_t[:, 1, :]
                            act.wait_ge(x_scaled, KT_IN)
                            a.did(apply(w, gate_x[:, :], ACT.Abs))
                            a.settle()
                            a.did(apply(w, w, ACT.Exp, scale=-1.0))
                            a.settle()
                            a.did(apply(w, w, ACT.Ln, bias=1.0), gate_ln)
                        elif kind == "av":
                            full(act, keys[0])
                            o = bank(keys[0])
                            a.did(apply(v_al[:, :, :], o[:, :].rearrange("p (a b) -> p a b", a=NC), ACT.Copy))
                            a.did(apply(v_off[64:128, :, :], o[0:64, :].rearrange("p (a b) -> p a b", a=NC), ACT.Copy))
                            a.read(apply(v_off[0:64, 1:NC, :], o[64:128, 0:384].rearrange("p (a b) -> p a b", a=3),
                                         ACT.Copy), keys[0])
                        elif kind == "vtok":
                            if arg[0] == "gv":
                                act.wait_ge(m_done, 4)
                            else:
                                full(act, ("ada_col", 11, 0))
                            for p in range(NC):
                                full(act, keys[p])
                                dst = m_v if arg[0] == "mv" else g_v
                                a.read(apply(dst[:, p, :], bank(keys[p])[:, :], ACT.Copy), keys[p])
                        elif kind == "tok":
                            full(act, keys[0])
                            a.read(apply(tok[:, :, :].rearrange("p a b -> p (a b)"), bank(keys[0])[:, :], ACT.Copy),
                                   keys[0])
                            full(act, keys[1])
                            a.read(apply(dt_tok[:, :, :].rearrange("p a b -> p (a b)"), bank(keys[1])[:, 0:32],
                                         ACT.Copy), keys[1])
                            was_read(act, keys[2])
                            a.did(apply(edge_e[:, :, :], edge[:, :, :], ACT.Exp), edge_exp)
                        elif kind == "m_qk":
                            h = arg[0]
                            act.wait_ge(m_exp_in, h + 1)
                            a.did(apply(m_w[:, h % 2, :], m_w[:, h % 2, :], ACT.Exp), m_exp)
                        elif kind == "m_decay":
                            h = arg[0]
                            if h >= 2:
                                full(act, ("m_num", h - 2, 1))
                                act.wait_ge(m_h, h - 1)
                            full(act, keys[0])
                            a.read(apply(m_qw[:, h % 2, :], bank(keys[0])[:, :], ACT.Exp), keys[0])
                            full(act, keys[1])
                            a.read(apply(m_em[:, h % 2, :], bank(keys[1])[:, :], ACT.Exp, scale=-1.0), keys[1])
                        elif kind == "m_num":
                            h = arg[0]
                            if h:
                                act.wait_ge(m_h, h)
                            full(act, keys[1])
                            a.read(apply(m_ad[:, :], bank(keys[1])[:, :], ACT.Abs), keys[1])
                        elif kind == "m_square":
                            h = arg[0]
                            act.wait_ge(m_h, h + 1)
                            a.did(apply(m_k[:, h, :], m_q[:, h, :], ACT.Square), m_sq)
                        elif kind == "m_norm":
                            h = arg[0]
                            full(act, keys[0])
                            a.read(apply(m_k[:, h, :], bank(keys[0])[:, :], ACT.Sqrt, bias=eps[:, 0:1],
                                         scale=0.25 / P), keys[0])
                        elif kind == "c_b":
                            full(act, keys[0])
                            act.wait_ge(m_done, 4)
                            a.read(apply(c_bt[:, arg[0], :], bank(keys[0])[:, 0:384], ACT.Copy), keys[0])
                        elif kind == "c_decay":
                            h = arg[0]
                            act.wait_ge(c_exp_in, h + 1)
                            a.did(apply(c_l[:, h % 4, :], c_l[:, h % 4, :], ACT.Exp), c_exp)
                        elif kind == "c_y":
                            t = arg[0]
                            if t:
                                act.wait_ge(c_gated, t)
                            full(act, keys[2])
                            a.read(apply(c_e2[:, :], bank(keys[2])[:, :], ACT.Exp), keys[2])
                        elif kind == "c_square":
                            j = arg[0]
                            full(act, ("c_state", 2, 0))
                            for t in (2 * j, 2 * j + 1):
                                act.wait_ge(c_gated, t + 1)
                                a.did(apply(c_sqs[:, t, :], yT[:, 4 + t, :], ACT.Square), c_sq)
                        elif kind == "c_norm":
                            j = arg[0]
                            full(act, keys[0])
                            a.read(apply(c_sqs[:, 2 * j, :], bank(keys[0])[:, :], ACT.Sqrt, bias=eps[:, 0:1],
                                         scale=1.0 / 256), keys[0])
                        elif kind == "g_gate":
                            for t in range(2):
                                was_read(act, keys[t])
                            a.did(apply(g_d[:, :], g_b[:, :], ACT.Abs))
                            a.settle()
                            a.did(apply(g_d[:, :], g_d[:, :], ACT.Exp, scale=-1.0))
                            a.settle()
                            a.did(apply(g_d[:, :], g_d[:, :], ACT.Ln, bias=1.0), g_ln)
                        elif kind == "g_decay":
                            last = g_b[:, :].rearrange("p (n b) -> p n b", b=P)[:, :, P - 1]
                            act.wait_ge(g_diff, 1)
                            a.did(apply(g_d[:, :], g_d[:, :], ACT.Exp, scale=1.0 / 16), g_exp)
                            a.did(apply(g_dec[:, :, :].rearrange("p a b -> p (a b)"), last, ACT.Exp,
                                        scale=1.0 / 16), g_exp)
                            a.did(apply(g_qb[:, :], g_b[:, :], ACT.Exp, scale=1.0 / 16), g_exp)
                        elif kind == "g_ktok":
                            for t in range(2):
                                full(act, keys[t])
                                a.read(apply(g_kt[:, t, :], bank(keys[t])[:, 0:384], ACT.Copy), keys[t])
                        elif kind == "g_prep":
                            act.wait_ge(g_diff, arg[0] + 2)
                            a.did(apply(g_d[:, :], g_d[:, :], ACT.Exp, scale=1.0 / 16), g_exp)
                        elif kind == "g_out":
                            h = arg[0]
                            full(act, keys[0])
                            merged(act)
                            a.read(apply(g_o[:, h, :], bank(keys[0])[:, :], ACT.Copy), keys[0])
                            a.settle()
                            a.did(apply(g_sqs[:, h, :], g_o[:, h, :], ACT.Square), g_sq)
                        elif kind == "g_norm":
                            full(act, keys[0])
                            a.read(apply(g_att[:, arg[0], :], bank(keys[0])[:, :], ACT.Sqrt, bias=eps[:, 0:1],
                                         scale=1.0 / P), keys[0])
                        elif kind == "a_s":
                            p = arg[0]
                            st = a_st[:, p % 2, :]
                            act.wait_ge(a_max, p + 1)
                            act.wait_ge(g_done, 4)
                            if p >= 2:
                                full(act, ("a_pt", p - 2, 1))
                            for par in range(2):
                                for t in range(4):
                                    h = 2 * t + par
                                    ins = apply(a_p[:, p % 2, h * P:(h + 1) * P], bank(keys[par])[:, t * P:(t + 1) * P],
                                                ACT.Exp, bias=st[:, 8 + h:9 + h], scale=0.125,
                                                accum_out=st[:, 24 + h:25 + h])
                                a.read(ins, keys[par])
                            a.did(apply(st[:, 16:24], st[:, 16:24], ACT.Exp), a_exp)
                        elif kind == "a_pt":
                            p = arg[0]
                            if p >= 2:
                                full(act, ("a_pv", p - 2, 0))
                            full(act, keys[0])
                            a.read(apply(a_pt[:, p % 2, 0:512], bank(keys[0])[:, :], ACT.Copy), keys[0])
                        elif kind == "y_split":
                            act.wait_ge(m_done, 4)
                            act.wait_ge(c_done, 4)
                            full(act, ("g_out", 3, 0))
                            for k in (range(8) if arg[0] == 0 else range(8, N_EARLY)):
                                if k >= 8:
                                    act.wait_ge(g_done, k - 7)
                                a.did(apply(y_hi[:, Y_SLOT[k], :], yT[:, k, :], ACT.Copy), y_hi_ready)
                        elif kind == "a_pv":
                            p = arg[0]
                            was_read(act, keys[0])
                            tk = slice(p * P, (p + 1) * P)
                            a.did(apply(y_hi[:, 0:4, tk], yT[:, 12:16, tk], ACT.Copy), y_hi_ready)
                        for i in after:
                            split(i)

                @block.gpsimd
                def _(pool):
                    q = Line(pool, pool_order)

                    def split(i):
                        n = WIDTH.get(SPLITS[i], TILE_W)
                        pool.wait_ge(w_hi_ready, i + 1)
                        at = i % SPLIT_RING
                        q.did(pool.tensor_tensor(w_lo[:, at, 0:n], ring[:, i % RING, 0:n],
                                                 w_hi[:, at, 0:n].bitcast(F32), ALU.subtract), w_lo_ready)

                    for step in SCHEDULE:
                        kind, arg = step[0], step[1:]
                        keys = tiles_of(step)
                        q.settle()
                        for i in next_splits(step)[0] + (list(range(SPLIT_RING)) if kind == "modulate" else []):
                            split(i)
                        if kind == "norm":
                            for t in range(KT_IN):
                                pool.wait_ge(root, 2)
                                q.did(pool.tensor_tensor(hT[:, t, :], xT[:, t, :], scr_t[:, 1, :], ALU.mult), x_scaled)
                        elif kind == "rope":
                            i = ROPES[arg]
                            full(pool, keys[0])
                            w = scr_in[:, i % 2, 3:3 + SEQ]
                            q.did(pool.tensor_tensor(w, w, cos[:, :], ALU.mult), rope_cos)
                        elif kind == "m_qk":
                            h = arg[0]
                            pool.wait_ge(m_exp, h + 1)
                            w = m_w[:, h % 2, :].rearrange("p (a b) -> p a b", a=NC)
                            q.did(pool.tensor_tensor(w, w, mid_bcast(causal[:, :], NC), ALU.mult), m_masked)
                        elif kind == "m_state" and arg[0]:
                            p = arg[0]
                            carry = edge_e[:, p, 4:8]
                            was_read(pool, ("m_state", p - 1, 0))
                            was_read(pool, ("m_state", p - 1, 1))
                            q.did(pool.tensor_tensor(m_cs[:, p, :].rearrange("p (a b) -> p a b", a=4),
                                                     m_cs[:, p - 1, :].rearrange("p (a b) -> p a b", a=4),
                                                     bcast(carry, P), ALU.mult), m_decayed)
                            q.did(pool.tensor_tensor(m_ns[:, p, :], m_ns[:, p - 1, :], carry, ALU.mult), m_decayed)
                        elif kind == "c_x" and arg[0] < 3:
                            p = arg[0]
                            was_read(pool, keys[0])
                            q.did(pool.tensor_tensor(c_xdd[:, p, :].rearrange("p (a b) -> p a b", a=8),
                                                     c_xdt[:, p, :].rearrange("p (a b) -> p a b", a=8),
                                                     bcast(edge_e[:, p, 16:24], 64), ALU.mult), c_xdd_s)
                        elif kind == "c_state" and arg[0]:
                            p = arg[0]
                            was_read(pool, ("c_state", p - 1, 0))
                            q.did(pool.tensor_tensor(c_ss[:, p, :].rearrange("p (a b) -> p a b", a=8),
                                                     c_ss[:, p - 1, :].rearrange("p (a b) -> p a b", a=8),
                                                     bcast(edge_e[:, p, 8:16], 64), ALU.mult), c_decayed)
                        elif kind == "c_decay":
                            h = arg[0]
                            pool.wait_ge(c_exp, h + 1)
                            was_read(pool, ("c_cb", h // 4, 0))
                            q.did(pool.tensor_tensor(c_l[:, h % 4, :], c_l[:, h % 4, :], c_cb[:, h // 4, :], ALU.mult),
                                  c_l_s)
                        elif kind == "g_decay":
                            pool.wait_ge(c_done, 4)
                            q.did(pool.memset(g_s[:, :, :], 0.0), g_kd)
                            pool.wait_ge(g_exp, 3)
                            was_read(pool, ("proj", "gk", 1, 0))
                            kk = g_k[:, :, :].rearrange("p a b -> p (a b)")
                            qq = g_q[:, :, :].rearrange("p a b -> p (a b)")
                            q.did(pool.tensor_tensor(g_g[:, 0, :], kk, g_d[:, :], ALU.mult), g_kd)
                            q.did(pool.tensor_tensor(g_qb[:, :], qq, g_qb[:, :], ALU.mult), g_kd)
                        elif kind == "g_prep":
                            i = arg[0]
                            b = LEVELS[i]
                            pool.wait_ge(g_exp, 4 + i)
                            full(pool, ("g_level", i - 2, 1) if i >= 2 else ("g_ktok", 1))

                            def first(v):
                                return v.rearrange("p (n b) -> p n b", b=2 * b)[:, :, 0:b]

                            kk = g_k[:, :, :].rearrange("p a b -> p (a b)")
                            q.did(pool.tensor_tensor(first(g_g[:, i % 2, :]), first(kk), first(g_d[:, :]), ALU.mult),
                                  g_key)
                        elif kind == "a_s":
                            p = arg[0]
                            pool.wait_ge(a_rden, p + 1)
                            w = a_p[:, p % 2, :].rearrange("p (a b) -> p a b", a=8)
                            q.did(pool.tensor_tensor(w, w, bcast(a_st[:, p % 2, 32:40], P), ALU.mult), a_prob)
                        elif kind == "y_split":
                            for k in (range(8) if arg[0] == 0 else range(8, N_EARLY)):
                                pool.wait_ge(y_hi_ready, k + 1)
                                q.did(pool.tensor_tensor(y_lo[:, k, :], yT[:, k, :], y_hi[:, Y_SLOT[k], :].bitcast(F32),
                                                         ALU.subtract), y_ready)
                        elif kind == "a_pv":
                            p = arg[0]
                            tk = slice(p * P, (p + 1) * P)
                            pool.wait_ge(y_hi_ready, N_EARLY + p + 1)
                            q.did(pool.tensor_tensor(y_lo[:, 12:16, tk], yT[:, 12:16, tk],
                                                     y_hi[:, 0:4, tk].bitcast(F32), ALU.subtract), y_ready)
                        elif kind == "out2" and 0 < arg[0] < KT_IN - 1:
                            j = arg[0]
                            pool.wait_ge(squares, j + 1)
                            q.did(pool.tensor_tensor(hT[:, 0, :], hT[:, 0, :], hT[:, j, :], ALU.add), squares_sum)
                        for i in next_splits(step)[1]:
                            split(i)

                @block.vector
                def _(dve):
                    v = Line(dve, vec_order)

                    def col(name, i=0):
                        return cols[:, COL[name] + i:COL[name] + i + 1]

                    def chunks(ap):
                        return ap.rearrange("p (a b) -> p a b", a=NC)

                    dve.wait_ge(layer_in, 32)
                    v.did(dve.tensor_scalar(half_b, cols[:, COL["conv_b"]:COL["conv_b"] + 16], 0.5, None, ALU.mult))
                    v.did(dve.tensor_scalar(half_mg, cols[:, COL["m_g"]:COL["m_g"] + 4], 0.5, None, ALU.mult))
                    v.did(dve.tensor_scalar(neg_sinks, cols[:, COL["sinks"]:COL["sinks"] + 8], -1.0, None, ALU.mult))
                    dve.wait_ge(a_log_exp, 1)
                    v.did(dve.tensor_scalar(a_col, small[0:8, 29:30], -1.0, None, ALU.mult))
                    for step in SCHEDULE:
                        kind, arg = step[0], step[1:]
                        keys = tiles_of(step)
                        v.settle()
                        o = bank(keys[0]) if keys else None
                        if kind == "norm":
                            dve.wait_ge(root, 1)
                            v.count["root"] = 1
                            v.did(dve.reciprocal(scr_t[:, 1, :], scr_t[:, 0, :]), root)
                        elif kind == "ada":
                            j = arg[0]
                            dve.wait_ge(ada_w_in[j % ADA_SLOTS], 16 * (j // ADA_SLOTS + 1))
                            for i in range(KT_IN // 2):
                                for half in range(2):
                                    k = half * KT_IN // 2 + i
                                    w = ada_w[:, j % ADA_SLOTS, k * 256:(k + 1) * 256]
                                    acc = ada_sums(j, half)
                                    if i == 0:
                                        v.did(dve.tensor_scalar(acc, w, ccol[:, k:k + 1], None, ALU.mult))
                                    else:
                                        v.did(dve.scalar_tensor_tensor(acc, w, ccol[:, k:k + 1], acc, ALU.mult, ALU.add),
                                              ada_sum if k == KT_IN - 1 else None)
                                if i < KT_IN // 2 - 1:
                                    v.settle()
                        elif kind == "ada_col":
                            i = arg[0]
                            full(dve, keys[0])
                            v.read(dve.tensor_tensor(mod[:, 2 * i:2 * i + 2], o[:, 0:2],
                                                     cols[:, COL["b_ada"] + 2 * i:COL["b_ada"] + 2 * i + 2], ALU.add),
                                   keys[0])
                        elif kind == "modulate":
                            v.did(dve.scalar_tensor_tensor(factor[:, :], mod[:, 8:16], 1.0,
                                                           cols[:, COL["norm_g"]:COL["norm_g"] + 8], ALU.add, ALU.mult))
                            v.settle()
                            for t in range(KT_IN + 1):
                                if t < KT_IN:
                                    dve.wait_ge(x_scaled, t + 1)
                                    v.did(dve.tensor_scalar(hT[:, t, :], hT[:, t, :], factor[:, t:t + 1],
                                                            mod[:, t:t + 1], ALU.mult, ALU.add), h_mod)
                                if t:
                                    dve.wait_ge(h_hi_ready, t)
                                    v.did(dve.tensor_tensor(hT_lo[:, t - 1, :], hT[:, t - 1, :],
                                                            hT_hi[:, t - 1, :].bitcast(F32), ALU.subtract), h_ready)
                        elif kind == "proj" and arg[0] == "gate":
                            full(dve, keys[0])
                            v.read(dve.tensor_scalar(gate_x[:, :], o[:, :], col("gate_b"), None, ALU.add), keys[0])
                            v.settle()
                        elif kind == "proj" and arg in SILUS:
                            name, t = arg
                            u = SILUS[arg]
                            was_read(dve, keys[0])
                            acc = scr_acc[:, u % 2, :]
                            if arg in CONVS:
                                i, ch = CONVS[arg], CONV_TILE[arg]
                                src = scr_in[:, i % 2, :]
                                v.did(dve.tensor_scalar(acc, src[:, 0:SEQ], col("conv_w", 4 * ch),
                                                        half_b[:, ch:ch + 1], ALU.mult, ALU.add))
                                for k in range(1, 4):
                                    v.settle()
                                    v.did(dve.scalar_tensor_tensor(acc, src[:, k:k + SEQ], col("conv_w", 4 * ch + k),
                                                                   acc, ALU.mult, ALU.add),
                                          conv_acc if k == 3 else None)
                                dst = {"mq": m_q[:, t, :], "mk": m_k[:, t, :], "xs": c_x[:, t, :],
                                       "bc": r2[:, t, :]}[name]
                                dve.wait_ge(conv_tanh, i + 1)
                            else:
                                dst = yT[:, Y_TILE[Z_OF[name]] + t, :]
                            v.did(dve.scalar_tensor_tensor(dst, scr_t[:, u % 2, :], 1.0, acc, ALU.add, ALU.mult),
                                  silu_out)
                        elif kind == "rows":
                            dve.wait_ge(gate_ln, 1)
                            ln = scr_t[:, 1, :]
                            lf, b, da = scr_acc[32:36, 0, :], scr_acc[32:36, 1, :], scr_acc[0:8, 1, :]
                            ig = gate_x[R_I:R_I + 4, :]
                            mprev = small[32:36, 48:52]
                            v.did(dve.scalar_tensor_tensor(dtm[0:8, :], gate_x[R_DT:R_DT + 8, :], 0.0, ln[0:8, :],
                                                           ALU.max, ALU.add))
                            v.did(dve.scalar_tensor_tensor(lf, gate_x[R_F:R_F + 4, :], 0.0, ln[R_F:R_F + 4, :],
                                                           ALU.min, ALU.subtract))
                            v.did(dve.memset(mprev[:, 0:1], 0.0))
                            v.settle()
                            v.did(dve.tensor_tensor_scan(m_max, lf, ig, 0.0, ALU.add, ALU.max))
                            v.did(dve.tensor_tensor_scan(b, reset[32:36, :], lf, 0.0, ALU.mult, ALU.add))
                            v.did(dve.tensor_scalar(da, dtm[0:8, :], a_col, None, ALU.mult))
                            v.settle()
                            v.did(dve.tensor_tensor_scan(rows[T_ACS:T_ACS + 8, :], reset[0:8, :], da, 0.0,
                                                         ALU.mult, ALU.add))
                            v.did(dve.tensor_tensor(rows[T_C:T_C + 4, :], ig, b, ALU.subtract))
                            v.did(dve.tensor_tensor(rows[T_R:T_R + 4, :], b, m_max, ALU.subtract))
                            v.did(dve.tensor_copy(mprev[:, 1:4], chunks(m_max)[:, 0:3, P - 1]))
                            v.settle()
                            v.did(dve.tensor_tensor(chunks(rows[T_R2:T_R2 + 4, :]), chunks(rows[T_R:T_R + 4, :]),
                                                    bcast(mprev, P), ALU.add), rows_ready)
                        elif kind == "rope":
                            i = ROPES[arg]
                            w = scr_in[:, i % 2, 3:3 + SEQ]
                            dst = scr_t[:, 0, :] if i == 0 else a_q[:, i - 1, :]
                            full(dve, keys[0])
                            v.read(dve.tensor_tensor(dst, o[:, :], sin[:, :], ALU.mult), keys[0])
                            dve.wait_ge(rope_cos, i + 1)
                            v.settle()
                            if i:
                                v.did(dve.tensor_tensor(dst, dst, w, ALU.add), rope_out)
                            else:
                                for g in range(2):
                                    half = slice(64 * g, 64 * g + 64)
                                    v.did(dve.tensor_tensor(kdup[half, g, WIN:], dst[half, :], w[half, :], ALU.add))
                                v.settle()
                                v.did(dve.tensor_copy(kdup[64:128, 0, WIN:], kdup[0:64, 0, WIN:]))
                                v.did(dve.tensor_copy(kdup[0:64, 1, WIN:], kdup[64:128, 1, WIN:]), rope_out)
                        elif kind == "tok":
                            full(dve, keys[2])
                            was_read(dve, keys[1])
                            was_read(dve, keys[0])
                            e = chunks(bank(keys[2])[:, :])
                            v.did(dve.tensor_tensor(edge[:, :, 0:4], e[:, :, T_R:T_R + 4], tok[:, :, T_C:T_C + 4],
                                                    ALU.add))
                            v.did(dve.tensor_copy(edge[:, :, 4:8], e[:, :, T_R2:T_R2 + 4]))
                            v.did(dve.tensor_copy(edge[:, :, 8:16], e[:, :, T_ACS:T_ACS + 8]))
                            v.read(dve.tensor_tensor(edge[:, :, 16:24], e[:, :, T_ACS:T_ACS + 8],
                                                     tok[:, :, T_ACS:T_ACS + 8], ALU.subtract), keys[2])
                        elif kind == "mk_tok":
                            dve.wait_ge(edge_exp, 1)
                            for p in range(3):
                                full(dve, keys[p])
                                v.read(dve.tensor_tensor(chunks(m_kw[:, p, :]), chunks(bank(keys[p])[:, :]),
                                                         bcast(edge_e[:, p, 0:4], P), ALU.mult), keys[p])
                        elif kind == "m_qk":
                            h = arg[0]
                            w = m_w[:, h % 2, :]
                            full(dve, keys[1])
                            v.read(dve.tensor_tensor(chunks(w), chunks(bank(keys[1])[:, :]),
                                                     bcast(tok[:, :, T_C + h], P), ALU.add), keys[1])
                            v.settle()
                            v.did(dve.tensor_scalar(w, w, 0.0, None, ALU.min), m_exp_in)
                        elif kind == "m_decay":
                            h = arg[0]
                            dve.wait_ge(m_masked, h + 1)
                            full(dve, ("m_qk", h, 0))
                            v.read(dve.scalar_tensor_tensor(m_pt[:, h % 2, :], bank(("m_qk", h, 0))[:, :], P ** -0.5,
                                                            m_w[:, h % 2, :], ALU.mult, ALU.mult), ("m_qk", h, 0))
                            was_read(dve, keys[0])
                            v.did(dve.scalar_tensor_tensor(m_qw[:, h % 2, :], m_q[:, h, :], P ** -0.5,
                                                           m_qw[:, h % 2, :], ALU.mult, ALU.mult), m_query)
                        elif kind == "m_state":
                            p = arg[0]
                            if p:
                                dve.wait_ge(m_decayed, 2 * p)
                            for dst, key, n in ((m_cs, keys[0], 512), (m_ns, keys[1], 4)):
                                full(dve, key)
                                src = bank(key)[:, 0:n]
                                v.read(dve.tensor_tensor(dst[:, p, :], src, dst[:, p, :], ALU.add) if p else
                                       dve.tensor_copy(dst[:, p, :], src), key)
                        elif kind == "m_num":
                            h = arg[0]
                            was_read(dve, keys[1])
                            was_read(dve, ("m_decay", h, 1))
                            v.did(dve.tensor_tensor(m_ad[:, :], m_ad[:, :], m_em[:, h % 2, :], ALU.max))
                            v.settle()
                            v.did(dve.reciprocal(m_ad[:, :], m_ad[:, :]))
                            v.settle()
                            full(dve, keys[0])
                            v.read(dve.tensor_tensor(m_q[:, h, :], o[:, :], m_ad[:, :], ALU.mult), keys[0])
                            v.settle()
                            was_read(dve, ("proj", "mo", h, 0))
                            v.did(dve.scalar_tensor_tensor(m_q[:, h, :], m_o[:, h, :], 1.0, m_q[:, h, :],
                                                           ALU.add, ALU.mult), m_h)
                        elif kind == "m_norm":
                            h = arg[0]
                            was_read(dve, keys[0])
                            v.did(dve.reciprocal(m_k[:, h, :], m_k[:, h, :]))
                            v.settle()
                            v.did(dve.scalar_tensor_tensor(m_q[:, h, :], m_q[:, h, :], half_mg[:, h:h + 1],
                                                           m_k[:, h, :], ALU.mult, ALU.mult))
                            v.settle()
                            silu_done(dve, "mz", h)
                            v.did(dve.tensor_tensor(yT[:, h, :], m_q[:, h, :], yT[:, h, :], ALU.mult), m_done)
                        elif kind == "c_cb":
                            full(dve, keys[0])
                            v.read(dve.tensor_tensor(chunks(c_cb[:, arg[0], :]), chunks(o[:, :]),
                                                     mid_bcast(causal[:, :], NC), ALU.mult), keys[0])
                        elif kind == "c_x":
                            p = arg[0]
                            full(dve, keys[0])
                            v.read(dve.tensor_tensor(c_xdt[:, p, :].rearrange("p (a b) -> p a b", a=8),
                                                     o[:, :].rearrange("p (a b) -> p a b", a=8),
                                                     bcast(dt_tok[:, p, :], 64), ALU.mult), keys[0])
                        elif kind == "c_state":
                            p = arg[0]
                            full(dve, keys[0])
                            if p:
                                dve.wait_ge(c_decayed, p)
                            v.read(dve.tensor_tensor(c_ss[:, p, :], o[:, :], c_ss[:, p, :], ALU.add) if p else
                                   dve.tensor_copy(c_ss[:, p, :], o[:, :]), keys[0])
                        elif kind == "c_decay":
                            h = arg[0]
                            if h >= 4:
                                full(dve, ("c_y", (h - 4) // 2, 0))
                            full(dve, keys[0])
                            w = c_l[:, h % 4, :]
                            v.read(dve.tensor_tensor(chunks(w), chunks(o[:, :]), bcast(tok[:, :, T_ACS + h], P),
                                                     ALU.subtract), keys[0])
                            v.settle()
                            v.did(dve.tensor_scalar(w, w, 0.0, None, ALU.min), c_exp_in)
                        elif kind == "c_y":
                            t = arg[0]
                            full(dve, keys[0])
                            v.read(dve.scalar_tensor_tensor(c_tmp[:, :], c_x[:, t, :], col("ssd_d", t), o[:, :],
                                                            ALU.mult, ALU.add), keys[0])
                            was_read(dve, keys[2])
                            full(dve, keys[1])
                            v.read(dve.tensor_tensor(c_e2[:, P:], c_e2[:, P:], bank(keys[1])[:, P:], ALU.mult), keys[1])
                            v.settle()
                            v.did(dve.tensor_tensor(c_tmp[:, P:], c_tmp[:, P:], c_e2[:, P:], ALU.add))
                            v.settle()
                            silu_done(dve, "cz", t)
                            v.did(dve.tensor_tensor(yT[:, 4 + t, :], yT[:, 4 + t, :], c_tmp[:, :], ALU.mult), c_gated)
                        elif kind == "c_norm":
                            j = arg[0]
                            was_read(dve, keys[0])
                            w = c_sqs[:, 2 * j, :]
                            v.did(dve.reciprocal(w, w))
                            v.settle()
                            for t in (2 * j, 2 * j + 1):
                                v.did(dve.scalar_tensor_tensor(yT[:, 4 + t, :], yT[:, 4 + t, :], col("ssd_g", t), w,
                                                               ALU.mult, ALU.mult), c_done)
                        elif kind == "g_gate":
                            dve.wait_ge(c_done, 4)
                            for t in range(2):
                                full(dve, keys[t])
                                v.read(dve.tensor_scalar(g_b[:, t * SEQ:(t + 1) * SEQ], bank(keys[t])[:, :],
                                                         col("gla_b", t), None, ALU.add), keys[t])
                        elif kind == "g_scan":
                            dve.wait_ge(g_ln, 1)
                            v.did(dve.scalar_tensor_tensor(g_g[:, 0, :], g_b[:, :], 0.0, g_d[:, :],
                                                           ALU.min, ALU.subtract))
                            v.settle()
                            for t in range(2):
                                tk = slice(t * SEQ, (t + 1) * SEQ)
                                v.did(dve.tensor_tensor_scan(g_b[:, tk], reset[:, :], g_g[:, 0, tk], 0.0,
                                                             ALU.mult, ALU.add))
                            v.settle()
                            b = g_b[:, :].rearrange("p (n b) -> p n b", b=P)
                            v.did(dve.tensor_tensor(g_d[:, :].rearrange("p (n b) -> p n b", b=P),
                                                    bcast(b[:, :, P - 1], P), b, ALU.subtract), g_diff)
                        elif kind == "g_diag":
                            for h in range(4):
                                full(dve, keys[h])
                                v.read(dve.tensor_tensor(chunks(g_att[:, h, :]), chunks(bank(keys[h])[:, :]),
                                                         mid_bcast(ident[:, :], NC), ALU.mult), keys[h])
                        elif kind == "g_state":
                            p = arg[0]
                            full(dve, keys[0])
                            dve.wait_ge(g_kd, 1)
                            dve.wait_ge(g_exp, 2)
                            for h in range(4):
                                half, hd = slice(64 * (h % 2), 64 * (h % 2) + 64), slice(h * P, (h + 1) * P)
                                if p:
                                    ins = dve.scalar_tensor_tensor(g_s[half, p, hd], g_s[half, p - 1, hd],
                                                                   g_dec[half, h // 2, p:p + 1], o[half, hd],
                                                                   ALU.mult, ALU.add)
                                else:
                                    ins = dve.tensor_copy(g_s[half, p, hd], o[half, hd])
                                if h == 3:
                                    v.read(ins, keys[0])
                                else:
                                    v.did(ins)
                        elif kind == "g_prep":
                            i = arg[0]
                            b = LEVELS[i]
                            dve.wait_ge(g_kd, 2) if i == 0 else dve.wait_ge(g_key, i)
                            bb = g_b[:, :].rearrange("p (n b) -> p n b", b=2 * b)
                            d = g_d[:, :].rearrange("p (n b) -> p n b", b=2 * b)
                            mid = bcast(bb[:, :, b - 1], b)
                            v.did(dve.tensor_tensor(d[:, :, 0:b], mid, bb[:, :, 0:b], ALU.subtract))
                            v.did(dve.tensor_tensor(d[:, :, b:2 * b], bb[:, :, b:2 * b], mid, ALU.subtract), g_diff)
                            dve.wait_ge(g_exp, 4 + i)
                            full(dve, ("g_level", i - 2, 1) if i >= 2 else ("g_ktok", 1))

                            def second(x):
                                return x.rearrange("p (n b) -> p n b", b=2 * b)[:, :, b:2 * b]

                            qq = g_q[:, :, :].rearrange("p a b -> p (a b)")
                            v.did(dve.tensor_tensor(second(g_g[:, i % 2, :]), second(qq), second(g_d[:, :]), ALU.mult),
                                  g_query)
                        elif kind == "g_merge":
                            i = arg[0]
                            b = LEVELS[i]
                            mask = levelmask[:, i, :].rearrange("p (m b) -> p m b", b=b)
                            mask = mask.unsqueeze(1).broadcast_to([P, 2, 256 // b, b])
                            for par in range(2):
                                key = ("g_level", i, par)
                                full(dve, key)
                                dst = g_att[:, :, :].rearrange("p (t e) n -> p t e n", e=2)[:, :, par, :]
                                dst = dst.rearrange("p t (m b) -> p t m b", b=2 * b)[:, :, :, b:2 * b]
                                src = bank(key)[:, :].rearrange("p (t m b) -> p t m b", t=2, b=b)
                                v.read(dve.copy_predicated(dst, mask, src), key)
                        elif kind == "g_norm":
                            h = arg[0]
                            was_read(dve, keys[0])
                            w = g_att[:, h, :]
                            v.did(dve.reciprocal(w, w))
                            v.settle()
                            v.did(dve.scalar_tensor_tensor(w, g_o[:, h, :], col("gla_g"), w, ALU.mult, ALU.mult))
                            v.settle()
                            silu_done(dve, "gz", h)
                            v.did(dve.tensor_tensor(yT[:, 8 + h, :], w, yT[:, 8 + h, :], ALU.mult), g_done)
                        elif kind == "a_s":
                            p = arg[0]
                            st = a_st[:, p % 2, :]
                            mx = st[:, 0:8].rearrange("p (t e) -> p t e", e=2)
                            for par in range(2):
                                full(dve, keys[par])
                                v.did(dve.tensor_reduce(mx[:, :, par], chunks(bank(keys[par])[:, :]), AX_X, ALU.max))
                            v.settle()
                            v.did(dve.scalar_tensor_tensor(st[:, 8:16], st[:, 0:8], -0.125, neg_sinks,
                                                           ALU.mult, ALU.min))
                            v.settle()
                            v.did(dve.tensor_tensor(st[:, 16:24], cols[:, COL["sinks"]:COL["sinks"] + 8],
                                                    st[:, 8:16], ALU.add), a_max)
                            dve.wait_ge(a_exp, p + 1)
                            v.did(dve.tensor_tensor(st[:, 32:40], st[:, 16:24], st[:, 24:32], ALU.add))
                            v.settle()
                            v.did(dve.reciprocal(st[:, 32:40], st[:, 32:40]), a_rden)
                        elif kind == "a_pt":
                            p = arg[0]
                            full(dve, keys[1])
                            if p >= 2:
                                full(dve, ("a_pv", p - 2, 0))
                            v.read(dve.tensor_copy(a_pt[:, p % 2, 512:1024], bank(keys[1])[:, :]), keys[1])
                        elif kind == "a_pv":
                            p = arg[0]
                            full(dve, keys[0])
                            z = yT[:, 12:16, p * P:(p + 1) * P]
                            v.read(dve.tensor_tensor(z, chunks(o[:, :]), z, ALU.mult), keys[0])
                        elif kind in ("out1", "out2"):
                            j, key = arg[0], (kind, arg[0], 0)
                            full(dve, key)
                            dve.wait_ge(x_back, 16)
                            v.read(dve.scalar_tensor_tensor(xT[:, j, :], bank(key)[:, :], mod[:, 16 + j:17 + j],
                                                            xT[:, j, :], ALU.mult, ALU.add), key)

            numbers = sorted(s.num for s in layer)
            assert numbers == list(range(numbers[0], numbers[-1] + 1))
            nc.gpsimd.sem_clear(range(numbers[0], numbers[-1] + 1))
            nc.all_engine_barrier()

        with nc.Block() as block:
            @block.scalar
            def _(act):
                act.activation(scr_t[:, 0, :], sum_bank[:, :], ACT.Sqrt, bias=eps[:, 0:1], scale=1.0 / D_MODEL)\
                    .then_inc(root, 1)

            @block.vector
            def _(dve):
                dve.wait_ge(root, 1)
                dve.reciprocal(scr_t[:, 1, :], scr_t[:, 0, :]).then_inc(vec_order, 1)
                dve.wait_ge(vec_order, 1)
                for t in range(KT_IN):
                    dve.scalar_tensor_tensor(hT[:, t, :], xT[:, t, :], final_g[:, t:t + 1], scr_t[:, 1, :],
                                             ALU.mult, ALU.mult).then_inc(x_scaled, 1)

            @block.sync
            def _(sp):
                for t in range(KT_IN):
                    sp.wait_ge(x_scaled, t + 1)
                    sp.dma_start(out[:, t, :], hT[:, t, :]).then_inc(out_done, 16)
                sp.wait_ge(x_stored, 16 * KT_IN)
                sp.wait_ge(out_done, 16 * KT_IN)



def constants():
    c = np.zeros((P, 1410), np.float32)
    c[:, 0:128] = np.eye(P)
    c[:, 128:256] = np.triu(np.ones((P, P)))
    for head in (0, 64):
        for d in range(ROPE_DIM // 2):
            c[head + d + ROPE_DIM // 2, 256 + head + d] = -1.0
            c[head + d, 256 + head + d + ROPE_DIM // 2] = 1.0
    c[:, 384:896] = (np.arange(SEQ) % C != 0).astype(np.float32)
    inv = np.float32(ROPE_THETA) ** (-np.arange(0, ROPE_DIM, 2, dtype=np.float32) / np.float32(ROPE_DIM))
    for head in (0, 64):
        for d in range(ROPE_DIM):
            c[head + d, 896] = inv[d % (ROPE_DIM // 2)]
    for h in range(8):
        c[T_ACS + h, 898 + (h // 2) * P + 64 * (h % 2):898 + (h // 2) * P + 64 * (h % 2) + 64] = 1.0
    masks = np.zeros((P, len(LEVELS), C // 2), np.float32)
    s = np.arange(P)
    for i, b in enumerate(LEVELS):
        n = np.arange(P // (2 * b))
        m = (s[:, None] // (2 * b) == n[None, :]) & (s[:, None] % (2 * b) < b)
        masks[:, i, :] = np.repeat(m, b, axis=1)
    return c, masks


def feature_tiles(w):
    k, n = w.shape[0] // P, w.shape[1] // P
    return w.reshape(k, P, n, P).transpose(2, 1, 0, 3).reshape(n, P, k * P)


def pack_ada(w_ada):
    t = w_ada.reshape(DEPTH, KT_IN, P, 12, 256).transpose(0, 3, 2, 1, 4)
    return np.ascontiguousarray(t.reshape(DEPTH, 12, P, 2 * TILE_W))


def pack_weights(w_in, w_out):
    tiles = np.zeros((DEPTH, len(SPLITS), P, TILE_W), np.float32)
    names = {"xs": (IN_OFF["xbc"], 512), "bc": (IN_OFF["xbc"] + 512, 512)}
    for l in range(DEPTH):
        gates = np.zeros((D_MODEL, P), np.float32)
        for at, name, n in ((R_DT, "dt", 8), (R_I, "mi", 4), (R_F, "mf", 4), (R_LR, "lr", 16)):
            gates[:, at:at + n] = w_in[l, :, IN_OFF[name]:IN_OFF[name] + n]
        tiles[l, SPLIT_NO[("gate", 0)]] = feature_tiles(gates)[0]
        for name, n in (("ak", 1), ("av", 1), ("gq", 2), ("gk", 2), ("mq", 4), ("mk", 4), ("mo", 4), ("mz", 4),
                        ("xs", 4), ("bc", 4), ("cz", 4), ("gz", 4), ("aq", 4), ("az", 4)):
            at = names[name][0] if name in names else IN_OFF[name]
            for t, w in enumerate(feature_tiles(w_in[l, :, at:at + n * P])):
                tiles[l, SPLIT_NO[(name, t)]] = w
        for name in ("mv", "gv"):
            w = w_in[l, :, IN_OFF[name]:IN_OFF[name] + 512].reshape(4, 2, P, 512)
            for q in range(4):
                tiles[l, SPLIT_NO[(name, q)]] = w[q].transpose(1, 0, 2).reshape(P, TILE_W)
        order = np.concatenate([w_out[l, Y_ROW[b]:Y_ROW[b] + 512] for b in ORDER], axis=0)
        early = feature_tiles(order[0:N_EARLY * P])
        late = feature_tiles(order[N_EARLY * P:])
        for j in range(8):
            tiles[l, SPLIT_NO[("o1", j, 0)]] = early[j][:, 0:TILE_W]
            tiles[l, SPLIT_NO[("o1", j, 1)], :, 0:512] = early[j][:, TILE_W:]
        for j in range(4):
            tiles[l, SPLIT_NO[("o2", j)]] = late[2 * j:2 * j + 2].transpose(1, 0, 2).reshape(P, TILE_W)
    return tiles


def pack_columns(a):
    out = np.zeros((DEPTH, P, N_COLS), np.float32)

    def put(name, v):
        out[:, :, COL[name]:COL[name] + v.shape[2]] = v

    def per_feature(v):
        return v.reshape(DEPTH, -1, P).transpose(0, 2, 1)

    put("norm_g", per_feature(a["norm_g"]))
    put("b_ada", per_feature(a["b_ada"]))
    put("gla_b", per_feature(a["gla_b_gate"]))
    put("gla_g", per_feature(a["gla_norm_g"]))
    put("ssd_g", per_feature(a["ssd_norm_g"]))
    put("m_g", per_feature(a["mlstm_norm_g"]))
    put("conv_b", np.concatenate([per_feature(a["ssd_conv_b"]), per_feature(a["mlstm_conv_b"])], axis=2))
    for at, name in ((0, "ssd_conv_w"), (32, "mlstm_conv_w")):
        w = a[name].reshape(DEPTH, 4, 8, P).transpose(0, 3, 2, 1).reshape(DEPTH, P, 32)
        out[:, :, COL["conv_w"] + at:COL["conv_w"] + at + 32] = w
    put("ssd_d", per_feature(np.repeat(a["ssd_d"], 64, axis=1)))
    g = COL["gate_b"]
    out[:, R_DT:R_DT + 8, g] = a["ssd_dt_bias"]
    out[:, R_I:R_I + 4, g] = a["mlstm_i_bias"]
    out[:, R_F:R_F + 4, g] = a["mlstm_f_bias"]
    out[:, 0:8, COL["a_log"]] = a["ssd_a_log"]
    out[:, :, COL["sinks"]:COL["sinks"] + 8] = a["swa_sinks"][:, None, :]
    return out


def host_arrays(inputs):
    a = {k: np.asarray(v) for k, v in inputs.items()}
    consts, masks = constants()
    return {
        "xT": np.ascontiguousarray(a["x"][0].T.reshape(KT_IN, P, SEQ).transpose(1, 0, 2)),
        "c": np.ascontiguousarray(a["c"].reshape(KT_IN, P).T),
        "pos": np.ascontiguousarray(np.broadcast_to(a["positions"].astype(np.int32).reshape(1, SEQ), (P, SEQ))),
        "cols": pack_columns(a),
        "wgate": np.ascontiguousarray(a["gla_w_gate"]),
        "final": np.ascontiguousarray(a["final_g"].reshape(KT_IN, P).T),
        "ada": pack_ada(a["w_ada"]),
        "weights": pack_weights(a["w_in"], a["w_out"]),
        "consts": consts,
        "masks": masks,
    }


def program(nc, arrays):
    aps = [nc.dram_tensor(f"in_{k}", v.shape, mybir.dt.from_np(v.dtype), kind="ExternalInput").ap()
           for k, v in arrays.items()]
    out = nc.dram_tensor("out", (P, KT_IN, SEQ), F32, kind="ExternalOutput").ap()
    x_kept = nc.dram_tensor("x_kept", (P, KT_IN, SEQ), F32, kind="Internal").ap()
    build(nc, *aps, x_kept, out)


def kernel(**inputs):
    import concourse.bacc as bacc
    from concourse.bass_utils import run_bass_kernel_spmd

    arrays = host_arrays(inputs)
    nc = bacc.Bacc("TRN2", target_bir_lowering=False, num_devices=1)
    program(nc, arrays)
    r = run_bass_kernel_spmd(nc, [{f"in_{k}": v for k, v in arrays.items()}], core_ids=[0])
    y = r.results[0]["out"]
    return np.ascontiguousarray(y.transpose(1, 0, 2).reshape(D_MODEL, SEQ).T)[None]
```

```python
from contextlib import ExitStack

import numpy as np

import concourse.bass as bass
from concourse import mybir

F32 = mybir.dt.float32
F32R = mybir.dt.float32r
I32 = mybir.dt.int32
U8 = mybir.dt.uint8
ALU = mybir.AluOpType
ACT = mybir.ActivationFunctionType
AX_X = mybir.AxisListType.X

P = 128
D_MODEL = 1024
SEQ = 512
DEPTH = 2
EPS = 1e-6
KT_IN = D_MODEL // P
C = 128
NC = SEQ // C
NB = 8
WIN = 64
ROPE_THETA = 500000.0
ROPE_DIM = 16
POOL_SCALES = [5, 6, 7]
LEVELS = [64, 32, 16, 8, 4, 2, 1]

IN_SPLITS = [512, 128, 128, 512, 256, 256, 512, 512, 16, 1024, 8, 512, 512, 512, 512, 4, 4, 512, 512]
IN_NAMES = ["aq", "ak", "av", "az", "gq", "gk", "gv", "gz", "lr", "xbc", "dt", "cz",
            "mq", "mk", "mv", "mi", "mf", "mo", "mz"]
IN_OFF = dict(zip(IN_NAMES, np.cumsum([0] + IN_SPLITS[:-1]).tolist()))

ORDER = ["m", "c", "g", "a"]
Y_TILE = {"m": 0, "c": 4, "g": 8, "a": 12}
Y_ROW = {"a": 0, "g": 512, "c": 1024, "m": 1536}
N_EARLY = 12

R_DT, R_I, R_LR, R_F = 0, 32, 64, 96
T_C, T_R, T_R2, T_ACS = 0, 32, 64, 96

COL = {}
_n = 0
for _name, _w in [("norm_g", 8), ("b_ada", 24), ("gla_b", 2), ("gla_g", 1), ("ssd_g", 4), ("m_g", 4),
                  ("conv_b", 16), ("conv_w", 64), ("ssd_d", 4), ("gate_b", 1), ("a_log", 1), ("sinks", 8)]:
    COL[_name] = _n
    _n += _w
N_COLS = _n

TILE_W = 1024
RING = 3
SPLIT_RING = 3
ADA_NEXT, ADA_ALL = 8, 12
ADA_AFTER = [7, 8, 10, 11, 13, 14, 16, 17]


def between(steps, fill):
    out, n = [], 0
    for i, s in enumerate(steps):
        out.append(s)
        want = (i + 1) * len(fill) // len(steps)
        out += fill[n:want]
        n = want
    return out


def make_schedule():
    def proj(name, n=4):
        return [("proj", name, t) for t in range(n)]

    s = [("modulate",), ("proj", "gate", 0), ("rows",), ("proj", "ak", 0),
         ("proj", "av", 0), ("rope", "ak", 0), ("proj", "mq", 0), ("av",), ("rows_split",)]
    s += proj("mq")[1:] + proj("mk") + [("ada", j) for j in range(ADA_NEXT, ADA_ALL)] + [("vtok", "mv")]
    s += [("ada_col", j) for j in range(ADA_NEXT, ADA_ALL)]
    mo, mz, xs, bc, cz = (proj(n) for n in ("mo", "mz", "xs", "bc", "cz"))
    s += [("tok",), mo[0], ("edge",), ("mk_tok",), ("m_qk", 0), mo[1], ("m_state", 0), ("m_decay", 0), xs[0], ("m_state", 1), mo[2],
          ("m_qk", 1), xs[1], ("m_state", 2), ("m_decay", 1), mo[3], ("m_num", 0), xs[2], ("m_qk", 2), mz[0],
          ("m_decay", 2), xs[3], ("m_num", 1), mz[1], ("m_qk", 3), bc[0], ("m_decay", 3), ("m_square", 0), mz[2],
          ("m_num", 2), ("m_square", 1), bc[1], ("m_norm", 0), mz[3], ("m_num", 3), ("m_square", 2), bc[2],
          ("m_norm", 1), cz[0], ("m_square", 3), bc[3], ("m_norm", 2), cz[1], ("m_norm", 3), cz[2], cz[3]]
    gq, gk, gz, aq, az = proj("gq", 2), proj("gk", 2), proj("gz"), proj("aq"), proj("az")
    s += [("c_cb", 0), ("c_cb", 1), ("c_x", 0), ("c_x", 1), ("c_x", 2), ("c_x", 3), gq[0], ("c_b", 0), ("c_b", 1),
          ("c_decay", 0), ("c_decay", 1), gq[1], ("c_state", 0), ("c_state", 1), ("c_state", 2),
          ("c_decay", 2), ("c_decay", 3), gk[0], ("c_y", 0), ("c_decay", 4), ("c_decay", 5),
          ("c_decay", 6), ("c_y", 1), ("c_decay", 7), gk[1], ("c_y", 2), ("c_y", 3), ("c_square", 0),
          ("c_square", 1), gz[0], ("c_norm", 0), ("c_norm", 1), ("g_gate",), ("g_scan",), ("vtok", "gv"), ("g_decay",), ("g_diag",),
          gz[1], ("g_ktok",), ("g_prep", 0), gz[2], ("g_state", 0), ("g_state", 1), ("g_state", 2)]
    fill = [[gz[3]], [aq[0]], [("rope", "aq", 0), aq[1]], [("rope", "aq", 1), aq[2]], [("rope", "aq", 2), aq[3]],
            [("rope", "aq", 3), az[0]], []]
    for i in range(len(LEVELS)):
        s += ([("g_prep", i + 1)] if i + 1 < len(LEVELS) else []) + [("g_level", i)] + fill[i] + [("g_merge", i)]
    s += [az[1], az[2], ("g_out", 0), ("g_out", 1), ("g_out", 2), ("g_out", 3), ("g_norm", 0), ("g_norm", 1),
          ("y_split", 0), az[3], ("g_norm", 2), ("g_norm", 3), ("y_split", 1)]
    o1 = [[("outa", j), ("out1", j)] for j in range(8)]
    s += [("outa", 0), ("outa", 1), ("a_s", 0), ("out1", 0), ("outa", 2), ("a_s", 1), ("out1", 1), ("a_pt", 0),
          ("out1", 2)]
    s += [("a_s", 2), ("a_pv", 0), ("a_pt", 1)] + o1[3] + [("a_s", 3), ("a_pv", 1)] + o1[4] + [("a_pt", 2)] + o1[5]
    s += [("a_pv", 2), ("a_pt", 3)] + o1[6] + [("a_pv", 3)] + o1[7]
    s += [("out2", j) for j in range(8)] + [("square",)]
    out, n = [], 0
    for step in s:
        out.append(step)
        if step[0] in ("outa", "out1") or step[0] == "out2" and step[1] % 2:
            n += 1
            out += [("ada", j) for j in range(ADA_NEXT) if ADA_AFTER[j] == n]
            out += [("ada_col", j) for j in range(ADA_NEXT) if ADA_AFTER[j] + 2 == n]
    s = out
    return s


SCHEDULE = make_schedule()


def tiles_of(step):
    kind = step[0]
    one = {"square": 1, "ada": 0, "ada_col": 1, "proj": 1, "av": 1, "rope": 1, "m_qk": 2, "m_decay": 2, "m_state": 2, "m_num": 2,
           "c_cb": 1, "c_x": 1, "c_b": 1, "c_state": 1, "c_decay": 1, "c_norm": 1, "g_ktok": 2, "g_gate": 2,
           "g_state": 1, "g_level": 2, "g_out": 1, "a_s": 2, "a_pt": 2, "a_pv": 1, "out1": 0, "out2": 1,
           "tok": 2, "edge": 1, "mk_tok": 3, "vtok": 4, "m_norm": 1, "g_norm": 1, "g_diag": 4, "c_y": 3,
           "modulate": 0, "rows": 0, "y_split": 0, "g_prep": 0, "g_scan": 0, "rows_split": 0, "m_square": 0, "c_square": 0, "g_decay": 0, "g_merge": 0}
    if kind == "outa":
        return [("out1", step[1], 0)]
    return [step + (i,) for i in range(one[kind])]


WITH_LEVEL = dict(enumerate([("gz", 3), ("aq", 0), ("aq", 1), ("aq", 2), ("aq", 3), ("az", 0), ("az", 1)]))

TILE = {}
for _step in SCHEDULE:
    for _key in tiles_of(_step):
        TILE[_key] = (len(TILE) % NB, len(TILE) // NB)

def weights_of(step):
    kind, arg = step[0], step[1:]
    if kind == "proj":
        return [arg]
    if kind == "vtok":
        return [(arg[0], q) for q in range(4)]
    if kind in ("outa", "out1"):
        return [("o1", arg[0], int(kind == "out1"))]
    if kind == "out2" and arg[0] % 2 == 0:
        return [("o2", arg[0] // 2)]
    return []


SPLITS = [w for s in SCHEDULE for w in weights_of(s)]
SPLIT_NO = {w: i for i, w in enumerate(SPLITS)}
WIDTH = {("o1", j, 1): 512 for j in range(8)}

USED_BY = {}
_n = 0
for _w in SPLITS:
    if _w[0] in ("mv", "gv") and _w[1] < 3 or _w[0] == "o1" and _w[2] == 0:
        _n += 1
        USED_BY[_w] = _n
    else:
        USED_BY[_w] = {"mv": ("vtok", _w[0], 3), "gv": ("vtok", _w[0], 3), "o1": ("out1", _w[1], 0),
                       "o2": ("out2", 2 * _w[1] + 1, 0)}.get(_w[0], ("proj",) + _w + (0,))


def releases(step):
    if step[0] == "out2":
        return [("o2", step[1] // 2)] if step[1] % 2 else []
    return weights_of(step)


def next_splits(step):
    n = [SPLIT_NO[w] + SPLIT_RING for w in releases(step)]
    n = [i if i < len(SPLITS) else None for i in n]
    return [i for i in n[:-1] if i is not None], [i for i in n[-1:] if i is not None]


GATE_SLAB_BEFORE = {5: 8, 7: 9, 9: 10, 11: 11}
LAST_PROJ = max(i for i, w in enumerate(SPLITS) if w[0] not in ("o1", "o2"))
X_BACK_BEFORE = LAST_PROJ + SPLIT_RING + RING
NEXT_SLAB_BEFORE = {LAST_PROJ + (ADA_AFTER[j] if j < 2 else ADA_AFTER[j - 2] + 4): j for j in range(ADA_NEXT)}
Y_SLOT = [10, 11, 12, 13, 14, 15, 4, 5, 6, 7, 8, 9, 0, 1, 2, 3]


def order_of(kinds):
    seen = [s[1:] for s in SCHEDULE if s[0] == "proj" and s[1] in kinds]
    return {k: i for i, k in enumerate(seen)}


CONV_NAMES = ("mq", "mk", "xs", "bc")
SILUS = order_of(CONV_NAMES + ("mz", "cz", "gz", "az"))
CONVS = order_of(CONV_NAMES)
CONV_TILE = {("xs", t): t for t in range(4)} | {("bc", t): 4 + t for t in range(4)} \
    | {("mq", t): 8 + t for t in range(4)} | {("mk", t): 12 + t for t in range(4)}
Z_OF = {"mz": "m", "cz": "c", "gz": "g", "az": "a"}
ROPES = {("ak", 0): 0} | {("aq", t): 1 + t for t in range(4)}

TWO_PI = 2.0 * np.pi
PI_HI = 6.28125
PI_MID = float(np.float32(np.floor((TWO_PI - PI_HI) * 2 ** 21) / 2 ** 21))
PI_LO = float(np.float32(TWO_PI - PI_HI - PI_MID))
ROUND = 12582912.0
PI_CLIP = 3.1415925


def bcast(ap, n):
    shape = list(ap.shape)
    return ap.unsqueeze(len(shape)).broadcast_to(shape + [n])


def mid_bcast(ap, n):
    p, a = ap.shape
    return ap.unsqueeze(1).broadcast_to([p, n, a])


def build(nc, xT_in, c_in, pos_in, cols_in, wgate_in, final_in, ada_first_in, ada_next_in, ada_gate_in, b_first_in, weights, consts_in, masks_in, x_kept, out):
    ctx = ExitStack()
    with ctx:
        def sb(name, shape, dt=F32):
            return ctx.enter_context(nc.sbuf_tensor(name, shape, dt))

        at_x, at_h, at_y, at_r1, arena_size = 0, 4096, 8192, 16384, 30464
        arena_at = -(-nc.sbuf_base // 32) * 32
        sb("arena", [P, arena_size])
        assert nc.sbuf_base >= arena_at + 4 * arena_size

        def placed(name, at, shape, dt=F32):
            return nc.alloc_sbuf_tensor_at(name, shape, dt, offset=arena_at + 4 * at)

        xT = placed("xT", at_x, [P, KT_IN, SEQ])
        hT_hi = placed("hT_hi", at_x, [P, KT_IN, SEQ], F32R)
        hT = placed("hT", at_h, [P, KT_IN, SEQ])
        hT_lo = placed("hT_lo", at_h, [P, KT_IN, SEQ], F32R)
        yT = placed("yT", at_y, [P, 16, SEQ])
        y_lo = placed("y_lo", at_y, [P, 16, SEQ], F32R)
        r1 = placed("r1", at_r1, [P, 14080])
        y_hi = placed("y_hi", at_r1 + 4096, [P, 16, SEQ], F32R)
        ring = sb("ring", [P, RING, TILE_W])
        w_hi = sb("w_hi", [P, SPLIT_RING, TILE_W], F32R)
        w_lo = sb("w_lo", [P, SPLIT_RING, TILE_W], F32R)
        ident = sb("ident", [P, P])
        ones = sb("ones", [P, P])
        causal = sb("causal", [P, P])
        rot = sb("rot", [P, P])
        reset = sb("reset", [P, SEQ])
        invf = sb("invf", [P, 2])
        eps = sb("eps", [P, 1])
        levelmask = sb("levelmask", [P, len(LEVELS), 256], U8)
        cos = sb("cos", [P, SEQ])
        sin = sb("sin", [P, SEQ])
        neg = sb("neg", [1, WIN])
        cols = sb("cols", [P, N_COLS])
        ccol = sb("ccol", [P, KT_IN])
        mod = sb("mod", [P, 24])
        factor = sb("factor", [P, KT_IN])
        small = sb("small", [P, 64])
        half_b = small[:, 0:16]
        half_mg = small[:, 16:20]
        neg_sinks = small[:, 20:28]
        a_col = small[0:8, 28:29]
        final_g = small[:, 32:40]
        scr_in = sb("scr_in", [P, 2, SEQ + 4])
        scr_acc = sb("scr_acc", [P, 2, SEQ])
        scr_t = sb("scr_t", [P, 2, SEQ])
        gate_x = sb("gate_x", [P, SEQ])
        rows = sb("rows", [P, SEQ])
        split_r, split_m = sb("split_r", [P, SEQ], F32R), sb("split_m", [P, SEQ], F32R)
        sel = sb("sel", [P, 8], F32R)
        dtm = sb("dtm", [P, SEQ])
        tok = sb("tok", [P, NC, P])
        dt_tok = sb("dt_tok", [P, NC, 8])
        edge = sb("edge", [P, NC, 24])
        edge_e = sb("edge_e", [P, NC, 24])
        kdup = sb("kdup", [P, 2, WIN + SEQ])
        v_al = sb("v_al", [P, NC, P])
        v_off = sb("v_off", [P, NC, P])
        wgate = dtm[R_LR:R_LR + 16, 0:256]
        r2 = sb("r2", [P, 4, SEQ])

        def cut(at, *shape):
            n = int(np.prod(shape))
            v = r1[:, at:at + n]
            if len(shape) == 2:
                v = v.rearrange("p (a b) -> p a b", a=shape[0])
            if len(shape) == 3:
                v = v.rearrange("p (a b c) -> p a b c", a=shape[0], b=shape[1])
            return v

        banks = [ctx.enter_context(nc.psum_tensor(f"bank{i}", [P, 512], F32)) for i in range(NB)]

        m_q, m_k, m_v = cut(0, 4, SEQ), cut(2048, 4, SEQ), cut(4096, NC, 512)
        m_kw, m_cs = cut(6144, 3, 512), cut(7680, 3, 512)
        m_w, m_pt, m_qw = cut(9216, 2, SEQ), cut(10240, 2, SEQ), cut(11264, 2, SEQ)
        m_em, m_ad, m_ns = cut(12288, 2, SEQ), cut(13312, SEQ), cut(13824, 3, 4)
        m_max = dtm[32:36, :]
        av_t = cut(12288, SEQ)
        ada_gate = cut(4096, ADA_ALL - ADA_NEXT, 2048)
        ada_next = placed("ada_next", at_h, [P, 2, 2048])
        ada_first = [placed("ada_first", at_y, [P, 4, 2048])[:, i, :] for i in range(4)] \
            + [cut(4096 + i * 2048, 2048) for i in range(4)]

        ada_acc = cut(12288, 4, 256)

        def ada_slab(j):
            return ada_next[:, j % 2, :] if j < ADA_NEXT else ada_gate[:, j - ADA_NEXT, :]

        def two_sums(j):
            if j < ADA_NEXT:
                return ada_acc[:, 2 * (j % 2), :], ada_acc[:, 2 * (j % 2) + 1, :]
            return ada_slab(j)[:, 0:256], ada_slab(j)[:, TILE_W:TILE_W + 256]

        def ada_count(j):
            return (j if j < ADA_NEXT else j - ADA_ALL) + ADA_ALL - ADA_NEXT + 1

        col_bank = banks[(TILE[("square", 0)][0] + 1) % NB]
        sum_bank = banks[TILE[("square", 0)][0]]
        m_o = yT[:, 12:16, :]
        g_q, g_k, g_v = cut(0, 2, SEQ), cut(1024, 2, SEQ), cut(2048, NC, 512)
        g_o = cut(0, 4, SEQ)
        c_x = yT[:, 8:12, :]
        c_b, c_c = r2[:, 0:2, :], r2[:, 2:4, :]
        c_xdt, c_xdd = cut(4096, NC, 512), cut(6144, 3, 512)
        c_bt, c_cb = cut(7680, 2, 384), cut(8448, 2, SEQ)
        c_sqs = cut(6144, 4, SEQ)
        c_ss, c_l = cut(9472, 3, 512), cut(11008, 4, SEQ)
        c_e2, c_tmp = cut(13056, SEQ), cut(13568, SEQ)
        c_pairs = placed("c_pairs", at_r1 + 2048, [P, 4, P], F32R)
        g_att, g_b = cut(4096, 4, SEQ), cut(6144, 1024)
        g_g, g_d = cut(7168, 2, 1024), cut(9216, 1024)
        g_kt, g_s = cut(10240, 2, 384), cut(11008, 3, 512)
        g_qb, g_dec = cut(12544, 1024), cut(13568, 2, NC)
        g_sqs = cut(7168, 4, SEQ)
        a_q = r2
        a_p, a_pt, a_st = cut(0, 2, 1024), cut(2048, 2, 1024), cut(13600, 2, 40)

        masks_f = cut(2048, len(LEVELS), 64)

        layer = []

        def sem(name):
            s = ctx.enter_context(nc.semaphore(name))
            layer.append(s)
            return s

        bank_full = [sem(f"bank_full{i}") for i in range(NB)]
        bank_read = [sem(f"bank_read{i}") for i in range(NB)]
        w_in = [sem(f"w_in{i}") for i in range(RING)]
        row_hi, row_lo = sem("row_hi"), sem("row_lo")
        ada_gate_w = [sem(f"ada_gate_w{i}") for i in range(ADA_ALL - ADA_NEXT)]
        ada_next_w = [sem(f"ada_next_w{i}") for i in range(2)]
        w_hi_ready, w_lo_ready, w_used = sem("w_hi_ready"), sem("w_lo_ready"), sem("w_used")
        x_back, ada_sum = sem("x_back"), sem("ada_sum")
        y_hi_ready, y_ready = sem("y_hi_ready"), sem("y_ready")
        layer_in = sem("layer_in")
        vec_order, act_order, pool_order = sem("vec_order"), sem("act_order"), sem("pool_order")
        squares_sum = sem("squares_sum")
        squares, x_scaled, h_ready = sem("squares"), sem("x_scaled"), sem("h_ready")
        rstd, x_rstd, x_act, factor_ready = sem("rstd"), sem("x_rstd"), sem("x_act"), sem("factor_ready")
        sum_ready = sem("sum_ready")
        h_hi_ready, a_log_exp = sem("h_hi_ready"), sem("a_log_exp")
        conv_acc, conv_tanh, silu_out = sem("conv_acc"), sem("conv_tanh"), sem("silu_out")
        rope_cos, rope_out = sem("rope_cos"), sem("rope_out")
        gate_ln, rows_ready, edge_exp = sem("gate_ln"), sem("rows_ready"), sem("edge_exp")
        m_exp_in, m_exp, m_masked = sem("m_exp_in"), sem("m_exp"), sem("m_masked")
        m_query, m_decayed, m_h, m_sq, m_done = sem("m_query"), sem("m_decayed"), sem("m_h"), sem("m_sq"), sem("m_done")
        c_xdd_s, c_decayed, c_exp_in, c_exp = sem("c_xdd_s"), sem("c_decayed"), sem("c_exp_in"), sem("c_exp")
        c_pairs_ready, c_l_s, c_gated, c_sq, c_done = sem("c_pairs_ready"), sem("c_l_s"), sem("c_gated"), sem("c_sq"), sem("c_done")
        g_ln, g_diff, g_exp, g_kd = sem("g_ln"), sem("g_diff"), sem("g_exp"), sem("g_kd")
        g_key, g_query, g_sq, g_done = sem("g_key"), sem("g_query"), sem("g_sq"), sem("g_done")
        a_max, a_exp, a_rden, a_prob = sem("a_max"), sem("a_exp"), sem("a_rden"), sem("a_prob")
        once = ctx.enter_context(nc.semaphore("once"))
        once_pos = ctx.enter_context(nc.semaphore("once_pos"))
        once_rows = ctx.enter_context(nc.semaphore("once_rows"))
        once_slab = ctx.enter_context(nc.semaphore("once_slab"))
        once_x, once_sq = ctx.enter_context(nc.semaphore("once_x")), ctx.enter_context(nc.semaphore("once_sq"))
        once_ada = [ctx.enter_context(nc.semaphore(f"once_ada{j}")) for j in range(ADA_NEXT)]
        once_sum, once_col = ctx.enter_context(nc.semaphore("once_sum")), ctx.enter_context(nc.semaphore("once_col"))
        once_ones = ctx.enter_context(nc.semaphore("once_ones"))
        x_stored = ctx.enter_context(nc.semaphore("x_stored"))
        once_d = ctx.enter_context(nc.semaphore("once_d"))
        once_v = ctx.enter_context(nc.semaphore("once_v"))
        once_ang = ctx.enter_context(nc.semaphore("once_ang"))
        once_a = ctx.enter_context(nc.semaphore("once_a"))
        out_done = ctx.enter_context(nc.semaphore("out_done"))

        row_parts = [("R", split_r[32:36, :], split_r[0:4, :], rows[T_R:T_R + 4, :]),
                     ("R2", split_r[64:68, :], split_r[96:100, :], rows[T_R2:T_R2 + 4, :]),
                     ("maximum", split_m[32:36, :], split_m[0:4, :], m_max),
                     ("ACS", split_m[96:104, :], split_m[64:72, :], rows[T_ACS:T_ACS + 8, :])]

        def square_of(j):
            return r2[:, 1 + (j - 1) % 3 if j else 0, :]

        def bank(key):
            return banks[TILE[key][0]]

        def full(eng, key):
            b, n = TILE[key]
            eng.wait_ge(bank_full[b], n + 1)

        def was_read(eng, key):
            b, n = TILE[key]
            eng.wait_ge(bank_read[b], n + 1)

        def used(eng, w):
            by = USED_BY[w]
            if isinstance(by, tuple):
                full(eng, by)
            else:
                eng.wait_ge(w_used, by)

        def silu_done(eng, name, t):
            eng.wait_ge(silu_out, SILUS[(name, t)] + 1)

        def merged(eng):
            for par in range(2):
                was_read(eng, ("g_level", len(LEVELS) - 1, par))

        def vacant(eng, key):
            b, n = TILE[key]
            if n:
                eng.wait_ge(bank_read[b], n)

        class Line:

            def __init__(self, eng, own):
                self.eng, self.own, self.count, self.last = eng, own, {}, None

            def sum_slab(self, dve, w, acc, signal):
                for i in range(KT_IN // 2):
                    for half in range(2):
                        k = half * KT_IN // 2 + i
                        w_k = w[:, k * 256:(k + 1) * 256]
                        if i == 0:
                            self.did(dve.tensor_scalar(acc[half], w_k, ccol[:, k:k + 1], None, ALU.mult))
                        else:
                            self.did(dve.scalar_tensor_tensor(acc[half], w_k, ccol[:, k:k + 1], acc[half],
                                                              ALU.mult, ALU.add))
                    self.settle()
                self.did(dve.tensor_tensor(acc[0], acc[0], acc[1], ALU.add), signal)

            def did(self, ins, signal=None):
                s = self.own if signal is None else signal
                ins.then_inc(s, 1)
                self.count[s.name] = self.count.get(s.name, 0) + 1
                self.last = (s, self.count[s.name])

            def read(self, ins, key):
                b, n = TILE[key]
                ins.then_inc(bank_read[b], 1)
                self.last = (bank_read[b], n + 1)

            def settle(self):
                if self.last:
                    self.eng.wait_ge(*self.last)

        with nc.Block() as block:
            @block.sync
            def _(sp):
                for dst, src in ((scr_t[:, 1, :].bitcast(I32), pos_in), (invf[:, :], consts_in[:, 896:898]),
                                 (ccol[:, :], c_in)):
                    sp.dma_start(dst, src).then_inc(once_pos, 16)
                sp.dma_start(xT[:, :, :], xT_in).then_inc(once_x, 16)
                for j in range(ADA_NEXT):
                    sp.dma_start(ada_first[j], ada_first_in[j]).then_inc(once_ada[j], 16)
                loads = [(small[:, 0:16], b_first_in), (small[:, 40:48], consts_in[:, 898:906]), (final_g, final_in),
                         (ident[:, :], consts_in[:, 0:128]), (causal[:, :], consts_in[:, 128:256]),
                         (rot[:, :], consts_in[:, 256:384]), (reset[:, :], consts_in[:, 384:896]),
                         (masks_f, masks_in)]
                for dst, src in loads:
                    sp.dma_start(dst, src).then_inc(once, 16)
                sp.wait_ge(once_x, 16)
                for t in range(KT_IN):
                    sp.dma_start(x_kept[:, t, :], xT[:, t, :]).then_inc(x_stored, 16)
                sp.wait_ge(once, 16 * len(loads))
                sp.sem_inc(once_v, 1)

            @block.tensor
            def _(pe):
                pe.wait_ge(once_ones, 1)
                for t in range(KT_IN):
                    pe.wait_ge(once_sq, t + 1)
                    pe.matmul(sum_bank[:, :], ones[:, :], hT[:, t, :], start=(t == 0), stop=(t == KT_IN - 1))\
                        .then_inc(once_sum, 1)
                for j in range(ADA_NEXT):
                    pe.wait_ge(once_slab, j + 1)
                    for t in range(2):
                        pe.matmul(col_bank[:, 2 * j + t:2 * j + t + 1], ada_first[j][:, t * P:(t + 1) * P], ones[:, 0:1],
                                  start=True, stop=True).then_inc(once_col, 1)

            @block.gpsimd
            def _(pool):
                pool.memset(ones[:, :], 1.0).then_inc(once_ones, 1)
                pool.memset(eps[:, :], EPS).then_inc(once_ones, 1)
                pool.memset(neg[:, :], -1.0e30)
                pool.memset(scr_in[:, :, :], 0.0)
                pool.memset(rows[:, :], 0.0).then_inc(once_rows, 1)
                pool.wait_ge(once_rows, 1)
                pool.tensor_copy(split_r[:, :], rows[:, :])
                pool.tensor_copy(split_m[:, :], rows[:, :])
                pool.memset(kdup[:, :, :], 0.0)
                pool.memset(v_off[:, :, :], 0.0)

            @block.vector
            def _(dve):
                v = Line(dve, once_d)
                dve.wait_ge(once_pos, 48)
                ang, r = scr_acc[:, 0, :], scr_t[:, 0, :]
                v.did(dve.tensor_copy(r, scr_t[:, 1, :].bitcast(I32)))
                v.settle()
                v.did(dve.tensor_scalar(ang, r, invf[:, 0:1], None, ALU.mult))
                v.settle()
                both = ((0.0, r1[:, 0:512], r1[:, 1024:1536]), (0.25, r1[:, 512:1024], r1[:, 1536:2048]))
                for quarter, dst, k in both:
                    v.did(dve.tensor_scalar(k, ang, 1.0 / TWO_PI, quarter, ALU.mult, ALU.add))
                for x in (ROUND, -ROUND):
                    v.settle()
                    for quarter, dst, k in both:
                        v.did(dve.tensor_scalar(k, k, x, None, ALU.add))
                for part in (PI_HI, PI_MID, PI_LO):
                    v.settle()
                    for quarter, dst, k in both:
                        v.did(dve.scalar_tensor_tensor(dst, k, -part, ang if part == PI_HI else dst,
                                                       ALU.mult, ALU.add))
                v.settle()
                for quarter, dst, k in both:
                    v.did(dve.tensor_scalar(dst, dst, quarter * TWO_PI, PI_CLIP, ALU.add, ALU.min))
                v.settle()
                for quarter, dst, k in both:
                    v.did(dve.tensor_scalar(dst, dst, -PI_CLIP, None, ALU.max))
                v.settle()
                dve.sem_inc(once_ang, 1)
                dve.wait_ge(once_a, 3 + KT_IN)
                for j in range(ADA_NEXT):
                    dve.wait_ge(once_ada[j], 16)
                    v.sum_slab(dve, ada_first[j], (ada_first[j][:, 0:256], ada_first[j][:, TILE_W:TILE_W + 256]), once_slab)
                dve.wait_ge(once_v, 1)
                v.did(dve.tensor_copy(levelmask[:, :, :].rearrange("p i (c b) -> p i c b", c=NC),
                                      masks_f.unsqueeze(2).broadcast_to([P, len(LEVELS), NC, 64])))
                dve.wait_ge(once_col, 2 * ADA_NEXT)
                v.did(dve.tensor_copy(sel[:, :], small[:, 40:48]))
                v.did(dve.tensor_tensor(mod[:, 0:16], col_bank[:, 0:16], small[:, 0:16], ALU.add))

            @block.scalar
            def _(act):
                act.wait_ge(once_pos, 48)
                th = small[:, 52:60]
                act.activation(th, ccol[:, :], ACT.Tanh, scale=0.5).then_inc(once_a, 1)
                act.wait_ge(once_a, 1)
                act.activation(th, th, ACT.Copy, bias=1.0).then_inc(once_a, 1)
                act.wait_ge(once_a, 2)
                for t in range(KT_IN):
                    act.activation(ccol[:, t:t + 1], ccol[:, t:t + 1], ACT.Copy, scale=th[:, t:t + 1])\
                        .then_inc(once_a, 1)
                act.wait_ge(once_a, 2 + KT_IN)
                act.activation(ccol[:, :], ccol[:, :], ACT.Copy, scale=0.5).then_inc(once_a, 1)
                act.wait_ge(once_x, 16)
                for t in range(KT_IN):
                    act.activation(hT[:, t, :], xT[:, t, :], ACT.Square).then_inc(once_sq, 1)
                act.wait_ge(once_ang, 1)
                act.activation(sin[:, :], r1[:, 0:512], ACT.Sin)
                act.activation(cos[:, :], r1[:, 512:1024], ACT.Sin)
                act.wait_ge(once_ones, 2)
                act.wait_ge(once_sum, KT_IN)
                act.activation(scr_t[:, 0, :], sum_bank[:, :], ACT.Sqrt, bias=eps[:, 0:1], scale=1.0 / D_MODEL)

        with nc.Fori(0, DEPTH) as l:
            with nc.Block() as block:
                @block.sync
                def _(sp):
                    sp.dma_start(cols[:, :], cols_in[bass.ds(l, 1)].rearrange("a p n -> (a p) n"))\
                        .then_inc(layer_in, 16)
                    sp.dma_start(wgate, wgate_in[bass.ds(l, 1)].rearrange("a p n -> (a p) n"))\
                        .then_inc(layer_in, 16)

                    for i, w in enumerate(SPLITS):
                        if i in GATE_SLAB_BEFORE:
                            j = GATE_SLAB_BEFORE[i] - ADA_NEXT
                            sp.dma_start(ada_gate[:, j, :], ada_gate_in[bass.ds(l, 1), j].rearrange("a p n -> (a p) n"))\
                                .then_inc(ada_gate_w[j], 16)
                        if i in NEXT_SLAB_BEFORE:
                            j = NEXT_SLAB_BEFORE[i]
                            if j >= 2:
                                sp.wait_ge(ada_sum, ada_count(j - 2))
                            sp.dma_start(ada_next[:, j % 2, :],
                                         ada_next_in[bass.ds(l, 1), j].rearrange("a p n -> (a p) n"))\
                                .then_inc(ada_next_w[j % 2], 16)
                        if i == X_BACK_BEFORE:
                            sp.wait_ge(x_stored, 16 * KT_IN)
                            used(sp, SPLITS[LAST_PROJ])
                            sp.sem_clear(x_stored)
                            sp.dma_start(xT[:, :, :], x_kept).then_inc(x_back, 16)
                        if i >= RING:
                            sp.wait_ge(w_lo_ready, i - RING + 1)
                        n = WIDTH.get(w, TILE_W)
                        src = weights[bass.ds(l, 1), i, :, 0:n].rearrange("a p n -> (a p) n")
                        sp.dma_start(ring[:, i % RING, 0:n], src).then_inc(w_in[i % RING], 16)
                    for j in range(KT_IN):
                        was_read(sp, ("out2", j, 0))
                        sp.dma_start(x_kept[:, j, :], xT[:, j, :]).then_inc(x_stored, 16)

                @block.tensor
                def _(pe):
                    def end(mm, key):
                        mm.then_inc(bank_full[TILE[key][0]], 1)

                    def split_tile(w):
                        i = SPLIT_NO[w]
                        pe.wait_ge(w_lo_ready, i + 1)
                        return [t[:, i % SPLIT_RING, :] for t in (w_hi, w_lo)]

                    def everywhere(o, halves, at, h):
                        return pe.matmul(o[:, :], sel[at:at + 64, h:h + 1].broadcast_to([64, P]),
                                         halves[at:at + 64, :], start=True, stop=True)

                    def product(o, a, b, start, stop):
                        pe.matmul(o, a[0], b[0], start=start, stop=False)
                        pe.matmul(o, a[0], b[1], start=False, stop=False)
                        return pe.matmul(o, a[1], b[0], start=False, stop=stop)

                    for step in SCHEDULE:
                        kind, arg = step[0], step[1:]
                        keys = tiles_of(step)
                        for key in keys[:1]:
                            vacant(pe, key)
                        o = bank(keys[0]) if keys else None
                        if kind == "square":
                            pe.wait_ge(squares_sum, KT_IN - 2)
                            pe.matmul(sum_bank[:, :], ones[:, :], r2[:, 0, :], start=True, stop=False)
                            pe.wait_ge(squares, KT_IN)
                            pe.matmul(sum_bank[:, :], ones[:, :], square_of(KT_IN - 1), start=False, stop=True)\
                                .then_inc(sum_ready, 1)
                        elif kind == "ada_col":
                            pe.wait_ge(ada_sum, ada_count(arg[0]))
                            for t in range(2):
                                mm = pe.matmul(o[:, t:t + 1], two_sums(arg[0])[0][:, t * P:(t + 1) * P], ones[:, 0:1],
                                               start=True, stop=True)
                            end(mm, keys[0])
                        elif kind == "proj" and arg not in WITH_LEVEL.values():
                            w = split_tile(arg)
                            for k in range(KT_IN):
                                if arg[0] == "gate":
                                    pe.wait_ge(h_ready, k + 1)
                                mm = product(o[:, :], [x[:, k * P:(k + 1) * P] for x in w],
                                             [x[:, k, :] for x in (hT_hi, hT_lo)], k == 0, k == KT_IN - 1)
                            end(mm, keys[0])
                        elif kind == "rope":
                            i = ROPES[arg]
                            was_read(pe, ("proj",) + arg + (0,))
                            end(pe.matmul(o[:, :], rot[:, :], scr_in[:, i % 2, 3:3 + SEQ], start=True, stop=True), keys[0])
                        elif kind == "av":
                            was_read(pe, ("proj", "av", 0, 0))
                            for p in range(NC):
                                mm = pe.transpose(o[:, p * P:(p + 1) * P], av_t[:, p * P:(p + 1) * P], ident[:, :])
                            end(mm, keys[0])
                        elif kind == "vtok":
                            for q in range(4):
                                w = split_tile((arg[0], q))
                                for p in range(NC):
                                    if q == 0 and p:
                                        vacant(pe, keys[p])
                                    for k in range(2):
                                        mm = product(bank(keys[p])[:, :],
                                                     [x[:, 2 * q + k, p * P:(p + 1) * P] for x in (hT_hi, hT_lo)],
                                                     [x[:, k * 512:(k + 1) * 512] for x in w],
                                                     q == 0 and k == 0, q == 3 and k == 1)
                                    if q == 3:
                                        end(mm, keys[p])
                                if q < 3:
                                    mm.then_inc(w_used, 1)
                        elif kind == "tok":
                            pe.wait_ge(rows_ready, 1)
                            for p in range(NC):
                                mm = pe.transpose(o[:, p * P:(p + 1) * P], rows[:, p * P:(p + 1) * P], ident[:, :])
                            end(mm, keys[0])
                            vacant(pe, keys[1])
                            for p in range(NC):
                                mm = pe.transpose(bank(keys[1])[:, p * 8:(p + 1) * 8], dtm[0:8, p * P:(p + 1) * P],
                                                  ident[0:8, 0:8])
                            end(mm, keys[1])
                        elif kind == "edge":
                            was_read(pe, ("tok", 0))
                            end(pe.matmul(o[:, :], ident[:, P - 1:P].broadcast_to([P, P]),
                                          tok[:, :, :].rearrange("p a b -> p (a b)"), start=True, stop=True), keys[0])
                        elif kind == "mk_tok":
                            silu_done(pe, "mk", 3)
                            for p in range(3):
                                if p:
                                    vacant(pe, keys[p])
                                for h in range(4):
                                    mm = pe.transpose(bank(keys[p])[:, h * P:(h + 1) * P],
                                                      m_k[:, h, p * P:(p + 1) * P], ident[:, :])
                                end(mm, keys[p])
                        elif kind == "m_qk":
                            h = arg[0]
                            silu_done(pe, "mk", 3)
                            for p in range(NC):
                                tk = slice(p * P, (p + 1) * P)
                                mm = pe.matmul(o[:, tk], m_k[:, h, tk], m_q[:, h, tk], start=True, stop=True)
                            end(mm, keys[0])
                            vacant(pe, keys[1])
                            pe.wait_ge(row_lo, 4)
                            end(everywhere(bank(keys[1]), split_r, 0, h), keys[1])
                        elif kind == "m_decay":
                            h = arg[0]
                            end(everywhere(o, split_r, 64, h), keys[0])
                            vacant(pe, keys[1])
                            end(everywhere(bank(keys[1]), split_m, 0, h), keys[1])
                        elif kind == "m_state":
                            p = arg[0]
                            was_read(pe, ("mk_tok", p))
                            was_read(pe, ("vtok", "mv", p))
                            for h in range(4):
                                hd = slice(h * P, (h + 1) * P)
                                mm = pe.matmul(o[:, hd], m_kw[:, p, hd], m_v[:, p, hd], start=True, stop=True)
                            end(mm, keys[0])
                            vacant(pe, keys[1])
                            for h in range(4):
                                hd = slice(h * P, (h + 1) * P)
                                mm = pe.matmul(bank(keys[1])[:, h:h + 1], m_kw[:, p, hd], ones[:, 0:1],
                                               start=True, stop=True)
                            end(mm, keys[1])
                        elif kind == "m_num":
                            h = arg[0]
                            hd = slice(h * P, (h + 1) * P)
                            was_read(pe, ("m_qk", h, 0))
                            pe.wait_ge(m_query, h + 1)
                            was_read(pe, ("m_state", 2, 0))
                            was_read(pe, ("m_state", 2, 1))
                            was_read(pe, ("vtok", "mv", 3))
                            for p in range(NC):
                                tk = slice(p * P, (p + 1) * P)
                                mm = pe.matmul(o[:, tk], m_v[:, p, hd], m_pt[:, h % 2, tk], start=True, stop=(p == 0))
                                if p:
                                    mm = pe.matmul(o[:, tk], m_cs[:, p - 1, hd], m_qw[:, h % 2, tk],
                                                   start=False, stop=True)
                            end(mm, keys[0])
                            vacant(pe, keys[1])
                            d = bank(keys[1])
                            pe.matmul(d[:, :], ones[:, :], m_pt[:, h % 2, :], start=True, stop=False)
                            for p in range(1, NC):
                                tk = slice(p * P, (p + 1) * P)
                                mm = pe.matmul(d[:, tk], m_ns[:, p - 1, h:h + 1].broadcast_to([P, P]), m_qw[:, h % 2, tk],
                                               start=False, stop=(p == NC - 1))
                            end(mm, keys[1])
                        elif kind == "m_norm":
                            pe.wait_ge(m_sq, arg[0] + 1)
                            end(pe.matmul(o[:, :], ones[:, :], m_k[:, arg[0], :], start=True, stop=True), keys[0])
                        elif kind == "c_cb":
                            g = arg[0]
                            silu_done(pe, "bc", 3)
                            for p in range(NC):
                                tk = slice(p * P, (p + 1) * P)
                                mm = pe.matmul(o[:, tk], c_b[:, g, tk], c_c[:, g, tk], start=True, stop=True)
                            end(mm, keys[0])
                        elif kind == "c_x":
                            p = arg[0]
                            for t in range(4):
                                mm = pe.transpose(o[:, t * P:(t + 1) * P], c_x[:, t, p * P:(p + 1) * P], ident[:, :])
                            end(mm, keys[0])
                        elif kind == "c_b":
                            g = arg[0]
                            for p in range(3):
                                mm = pe.transpose(o[:, p * P:(p + 1) * P], c_b[:, g, p * P:(p + 1) * P], ident[:, :])
                            end(mm, keys[0])
                        elif kind == "c_state":
                            p = arg[0]
                            pe.wait_ge(c_xdd_s, p + 1)
                            was_read(pe, ("c_b", 1, 0))
                            was_read(pe, ("c_b", 0, 0))
                            for g in range(2):
                                mm = pe.matmul(o[:, g * 256:(g + 1) * 256], c_bt[:, g, p * P:(p + 1) * P],
                                               c_xdd[:, p, g * 256:(g + 1) * 256], start=True, stop=True)
                            end(mm, keys[0])
                        elif kind == "c_decay":
                            h = arg[0]
                            end(everywhere(o, split_m, 64, h), keys[0])
                        elif kind == "c_y":
                            t = arg[0]
                            g = t // 2
                            vacant(pe, keys[2])
                            pe.wait_ge(c_pairs_ready, 1)
                            end(pe.matmul(bank(keys[2])[:, :], c_pairs[64:128, t, :],
                                          split_m[64:128, :], start=True, stop=True), keys[2])
                            for h in (2 * t, 2 * t + 1):
                                pe.wait_ge(c_l_s, h + 1)
                                lo = WIN * (h % 2)
                                for p in range(NC):
                                    if h == 0:
                                        was_read(pe, ("c_x", p, 0))
                                    tk = slice(p * P, (p + 1) * P)
                                    mm = pe.matmul(o[lo:lo + WIN, tk], c_xdt[:, p, h * 64:(h + 1) * 64],
                                                   c_l[:, h % 4, tk], start=True, stop=True)
                            end(mm, keys[0])
                            vacant(pe, keys[1])
                            was_read(pe, ("c_state", 2, 0))
                            for p in range(1, NC):
                                tk = slice(p * P, (p + 1) * P)
                                mm = pe.matmul(bank(keys[1])[:, tk], c_ss[:, p - 1, t * P:(t + 1) * P],
                                               c_c[:, g, tk], start=True, stop=True)
                            end(mm, keys[1])
                        elif kind == "c_norm":
                            for j in range(2):
                                pe.wait_ge(c_sq, 2 * arg[0] + j + 1)
                                mm = pe.matmul(o[:, :], ones[:, :], c_sqs[:, 2 * arg[0] + j, :],
                                               start=(j == 0), stop=(j == 1))
                            end(mm, keys[0])
                        elif kind == "g_gate":
                            for t in range(2):
                                if t:
                                    vacant(pe, keys[t])
                                pe.wait_ge(layer_in, 32)
                                end(pe.matmul(bank(keys[t])[:, :], wgate[:, t * P:(t + 1) * P],
                                              gate_x[R_LR:R_LR + 16, :], start=True, stop=True), keys[t])
                        elif kind == "g_ktok":
                            pe.wait_ge(g_kd, 2)
                            for t in range(2):
                                if t:
                                    vacant(pe, keys[t])
                                for p in range(3):
                                    mm = pe.transpose(bank(keys[t])[:, p * P:(p + 1) * P],
                                                      g_g[:, 0, t * SEQ + p * P:t * SEQ + (p + 1) * P], ident[:, :])
                                end(mm, keys[t])
                        elif kind == "g_state":
                            p = arg[0]
                            for t in range(2):
                                was_read(pe, ("g_ktok", t))
                            for q in range(4):
                                was_read(pe, ("vtok", "gv", q))
                            for h in range(4):
                                mm = pe.matmul(o[:, h * P:(h + 1) * P], g_kt[:, h // 2, p * P:(p + 1) * P],
                                               g_v[:, p, h * P:(h + 1) * P], start=True, stop=True)
                            end(mm, keys[0])
                        elif kind == "g_diag":
                            for t in range(2):
                                was_read(pe, ("proj", "gq", t, 0))
                                was_read(pe, ("proj", "gk", t, 0))
                            for h in range(4):
                                if h:
                                    vacant(pe, keys[h])
                                lo = 64 * (h % 2)
                                for p in range(NC):
                                    tk = slice(p * P, (p + 1) * P)
                                    mm = pe.matmul(bank(keys[h])[:, tk], g_k[lo:lo + 64, h // 2, tk],
                                                   g_q[lo:lo + 64, h // 2, tk], start=True, stop=True)
                                end(mm, keys[h])
                        elif kind == "g_level":
                            i = arg[0]
                            b = LEVELS[i]
                            pe.wait_ge(g_key, i + 1)
                            pe.wait_ge(g_query, i + 1)
                            vacant(pe, keys[1])
                            proj = ("proj",) + WITH_LEVEL[i] + (0,)
                            w = split_tile(WITH_LEVEL[i])
                            vacant(pe, proj)
                            for t in range(2):
                                for p in range(NC):
                                    at = t * SEQ + p * P
                                    for par in range(2):
                                        lo = 64 * par
                                        src = g_g[lo:lo + 64, i % 2, at:at + P]
                                        second = src.rearrange("p (n b) -> p n b", b=2 * b)[:, :, b:2 * b]
                                        mm = pe.matmul(bank(keys[par])[:, (t * NC + p) * 64:(t * NC + p + 1) * 64],
                                                       src, second, start=True, stop=True)
                                        if (t, p) == (1, NC - 1):
                                            end(mm, keys[par])
                                    k = t * NC + p
                                    mm = product(bank(proj)[:, :], [x[:, k * P:(k + 1) * P] for x in w],
                                                 [x[:, k, :] for x in (hT_hi, hT_lo)], k == 0, k == KT_IN - 1)
                            end(mm, proj)
                        elif kind == "g_out":
                            h = arg[0]
                            hd = slice(h * P, (h + 1) * P)
                            merged(pe)
                            was_read(pe, ("g_state", 2, 0))
                            pe.wait_ge(g_kd, 3)
                            for p in range(NC):
                                tk = slice(p * P, (p + 1) * P)
                                mm = pe.matmul(o[:, tk], g_v[:, p, hd], g_att[:, h, tk], start=True, stop=(p == 0))
                                if p:
                                    mm = pe.matmul(o[:, tk], g_s[:, p - 1, hd], g_qb[:, (h // 2) * SEQ + p * P:(h // 2) * SEQ + (p + 1) * P],
                                                   start=False, stop=True)
                            end(mm, keys[0])
                        elif kind == "g_norm":
                            pe.wait_ge(g_sq, arg[0] + 1)
                            end(pe.matmul(o[:, :], ones[:, :], g_sqs[:, arg[0], :], start=True, stop=True), keys[0])
                        elif kind == "a_s":
                            p = arg[0]
                            pe.wait_ge(rope_out, 5)
                            for par in range(2):
                                if par:
                                    vacant(pe, keys[par])
                                s = bank(keys[par])
                                lo = 64 * par
                                for e in range(2):
                                    q0 = (2 * p + e) * WIN
                                    for t in range(4):
                                        mm = pe.matmul(s[64 * e:64 * e + 64, t * P:(t + 1) * P],
                                                       a_q[lo:lo + 64, t, q0:q0 + WIN],
                                                       kdup[lo:lo + 64, t // 2, q0:q0 + 2 * WIN],
                                                       start=True, stop=not (p == 0 and e == 0))
                                        if p == 0 and e == 0:
                                            mm = pe.matmul(s[0:64, t * P:t * P + WIN], ones[0:1, 0:64],
                                                           neg[0:1, 0:WIN], start=False, stop=True)
                                end(mm, keys[par])
                        elif kind == "a_pt":
                            p = arg[0]
                            pe.wait_ge(a_prob, p + 1)
                            for g in range(2):
                                if g:
                                    vacant(pe, keys[g])
                                for j in range(4):
                                    h = 4 * g + j
                                    mm = pe.transpose(bank(keys[g])[:, j * P:(j + 1) * P],
                                                      a_p[:, p % 2, h * P:(h + 1) * P], ident[:, :])
                                end(mm, keys[g])
                        elif kind == "a_pv":
                            p = arg[0]
                            for g in range(2):
                                was_read(pe, ("a_pt", p, g))
                            was_read(pe, ("av", 0))
                            for hp in range(2):
                                for g in range(2):
                                    for e in range(2):
                                        v = (v_al if e else v_off)[:, p, g * 64:(g + 1) * 64]
                                        pr = a_pt[:, p % 2, :].rearrange("p (h q) -> p h q", h=8)
                                        for j in range(2):
                                            t = 2 * g + j
                                            mm = pe.matmul(o[64 * hp:64 * hp + 64, t * P + 64 * e:t * P + 64 * e + 64],
                                                           v, pr[:, 2 * t + hp, 64 * e:64 * e + 64],
                                                           start=True, stop=True)
                            end(mm, keys[0])
                        elif kind in ("outa", "out1"):
                            j, i = arg[0], int(kind == "out1")
                            key = ("out1", j, 0)
                            w = split_tile(("o1", j, i))
                            for k in range(8 * i, 8 if i == 0 else N_EARLY):
                                if j == 0:
                                    pe.wait_ge(y_ready, k + 1)
                                at = (k - 8 * i) * P
                                mm = product(bank(key)[:, :], [x[:, at:at + P] for x in w],
                                             [y_hi[:, Y_SLOT[k], :], y_lo[:, k, :]], k == 0, k == N_EARLY - 1)
                            if i == 0:
                                mm.then_inc(w_used, 1)
                            else:
                                end(mm, key)
                        elif kind == "out2":
                            j = arg[0]
                            pe.wait_ge(y_ready, N_EARLY + NC)
                            w = split_tile(("o2", j // 2))
                            for k in range(4):
                                at = ((j % 2) * 4 + k) * P
                                mm = product(o[:, :], [x[:, at:at + P] for x in w],
                                             [y_hi[:, Y_SLOT[N_EARLY + k], :], y_lo[:, N_EARLY + k, :]], k == 0, k == 3)
                            end(mm, keys[0])

                @block.scalar
                def _(act):
                    a = Line(act, act_order)

                    def apply(out, in_, func, **kw):
                        return act.activation(out, in_, func, **kw)

                    def split(i):
                        n = WIDTH.get(SPLITS[i], TILE_W)
                        act.wait_ge(w_in[i % RING], 16 * (i // RING + 1))
                        if i >= SPLIT_RING:
                            used(act, SPLITS[i - SPLIT_RING])
                        a.did(apply(w_hi[:, i % SPLIT_RING, 0:n], ring[:, i % RING, 0:n], ACT.Copy), w_hi_ready)

                    act.wait_ge(layer_in, 32)
                    a.did(apply(small[0:8, 29:30], cols[0:8, COL["a_log"]:COL["a_log"] + 1], ACT.Exp), a_log_exp)
                    for step in SCHEDULE:
                        kind, arg = step[0], step[1:]
                        keys = tiles_of(step)
                        within, after = next_splits(step)
                        for i in within:
                            split(i)
                        a.settle()
                        if kind == "square":
                            act.wait_ge(sum_ready, 1)
                            a.did(apply(scr_t[:, 0, :], sum_bank[:, :], ACT.Sqrt, bias=eps[:, 0:1],
                                        scale=1.0 / D_MODEL))
                        elif kind == "out2":
                            j = arg[0]
                            was_read(act, keys[0])
                            if j >= 4:
                                act.wait_ge(squares_sum, j - 3)
                            a.did(apply(square_of(j), xT[:, j, :], ACT.Square), squares)
                            if j == KT_IN - 2:
                                a.did(apply(small[:, 60:61], eps[:, :], ACT.Sqrt))
                        elif kind == "modulate":
                            act.wait_ge(x_stored, 16 * KT_IN)
                            for t in range(KT_IN):
                                if t in POOL_SCALES:
                                    act.wait_ge(x_rstd, t - POOL_SCALES[0] + 1)
                                    act.wait_ge(factor_ready, 1)
                                    a.did(apply(hT[:, t, :], hT[:, t, :], ACT.Copy, scale=factor[:, t:t + 1]), x_act)
                                    a.settle()
                                else:
                                    act.wait_ge(x_scaled, t + 1)
                                a.did(apply(hT_hi[:, t, :], hT[:, t, :], ACT.Identity, bias=mod[:, t:t + 1]),
                                      h_hi_ready)
                                if t < SPLIT_RING:
                                    split(t)
                        elif kind == "proj":
                            name, t = arg
                            o, key = bank(keys[0]), keys[0]
                            if name != "gate":
                                full(act, key)
                            if name == "gate":
                                pass
                            elif name == "av":
                                a.read(apply(av_t, o[:, :], ACT.Copy), key)
                            elif name in ("ak", "aq"):
                                i = ROPES[arg]
                                if i == 1:
                                    silu_done(act, "bc", 3)
                                if i >= 2:
                                    act.wait_ge(rope_out, i - 1)
                                a.read(apply(scr_in[:, i % 2, 3:3 + SEQ], o[:, :], ACT.Copy), key)
                            elif arg in CONVS:
                                i, u = CONVS[arg], SILUS[arg]
                                if i == 0:
                                    act.wait_ge(rope_out, 1)
                                if i >= 2:
                                    act.wait_ge(conv_acc, i - 1)
                                a.read(apply(scr_in[:, i % 2, 3:3 + SEQ], o[:, :], ACT.Copy, scale=0.5), key)
                                for n in after:
                                    split(n)
                                after = []
                                act.wait_ge(conv_acc, i + 1)
                                if u >= 2:
                                    act.wait_ge(silu_out, u - 1)
                                a.did(apply(scr_t[:, u % 2, :], scr_acc[:, u % 2, :], ACT.Tanh), conv_tanh)
                            elif arg in SILUS:
                                u = SILUS[arg]
                                act.wait_ge(silu_out, u - 1)
                                a.did(apply(scr_acc[:, u % 2, :], o[:, :], ACT.Copy, scale=0.5))
                                a.read(apply(scr_t[:, u % 2, :], o[:, :], ACT.Tanh, scale=0.5), key)
                            elif name == "mo":
                                a.read(apply(m_o[:, t, :], o[:, :], ACT.Tanh, scale=0.5), key)
                            else:
                                act.wait_ge(m_done, 4)
                                dst, scale = {"gq": (g_q, 0.125), "gk": (g_k, 1.0)}[name]
                                a.read(apply(dst[:, t, :], o[:, :], ACT.Copy, scale=scale), key)
                        elif kind == "rows":
                            was_read(act, ("proj", "gate", 0, 0))
                            w = scr_t[:, 1, :]
                            act.wait_ge(x_scaled, POOL_SCALES[0])
                            a.did(apply(w, gate_x[:, :], ACT.Abs))
                            a.settle()
                            a.did(apply(w, w, ACT.Exp, scale=-1.0))
                            a.settle()
                            a.did(apply(w, w, ACT.Ln, bias=1.0), gate_ln)
                        elif kind == "av":
                            full(act, keys[0])
                            o = bank(keys[0])
                            a.did(apply(v_al[:, :, :], o[:, :].rearrange("p (a b) -> p a b", a=NC), ACT.Copy))
                            a.did(apply(v_off[64:128, :, :], o[0:64, :].rearrange("p (a b) -> p a b", a=NC), ACT.Copy))
                            a.read(apply(v_off[0:64, 1:NC, :], o[64:128, 0:384].rearrange("p (a b) -> p a b", a=3),
                                         ACT.Copy), keys[0])
                        elif kind == "vtok":
                            if arg[0] == "gv":
                                act.wait_ge(m_done, 4)
                            else:
                                full(act, ("ada_col", ADA_ALL - 1, 0))
                            for p in range(NC):
                                full(act, keys[p])
                                dst = m_v if arg[0] == "mv" else g_v
                                a.read(apply(dst[:, p, :], bank(keys[p])[:, :], ACT.Copy), keys[p])
                        elif kind == "tok":
                            full(act, keys[0])
                            a.read(apply(tok[:, :, :].rearrange("p a b -> p (a b)"), bank(keys[0])[:, :], ACT.Copy),
                                   keys[0])
                            full(act, keys[1])
                            a.read(apply(dt_tok[:, :, :].rearrange("p a b -> p (a b)"), bank(keys[1])[:, 0:32],
                                         ACT.Copy), keys[1])
                        elif kind == "edge":
                            was_read(act, keys[0])
                            a.did(apply(edge_e[:, :, :], edge[:, :, :], ACT.Exp), edge_exp)
                        elif kind == "m_qk":
                            h = arg[0]
                            act.wait_ge(m_exp_in, h + 1)
                            a.did(apply(m_w[:, h % 2, :], m_w[:, h % 2, :], ACT.Exp), m_exp)
                        elif kind == "m_decay":
                            h = arg[0]
                            if h >= 2:
                                full(act, ("m_num", h - 2, 1))
                                act.wait_ge(m_h, h - 1)
                            full(act, keys[0])
                            a.read(apply(m_qw[:, h % 2, :], bank(keys[0])[:, :], ACT.Exp), keys[0])
                            full(act, keys[1])
                            a.read(apply(m_em[:, h % 2, :], bank(keys[1])[:, :], ACT.Exp, scale=-1.0), keys[1])
                        elif kind == "m_num":
                            h = arg[0]
                            if h:
                                act.wait_ge(m_h, h)
                            full(act, keys[1])
                            a.read(apply(m_ad[:, :], bank(keys[1])[:, :], ACT.Abs), keys[1])
                        elif kind == "m_square":
                            h = arg[0]
                            act.wait_ge(m_h, h + 1)
                            a.did(apply(m_k[:, h, :], m_q[:, h, :], ACT.Square), m_sq)
                        elif kind == "m_norm":
                            h = arg[0]
                            full(act, keys[0])
                            a.read(apply(m_k[:, h, :], bank(keys[0])[:, :], ACT.Sqrt, bias=eps[:, 0:1],
                                         scale=0.25 / P), keys[0])
                        elif kind == "c_b":
                            full(act, keys[0])
                            act.wait_ge(m_done, 4)
                            a.read(apply(c_bt[:, arg[0], :], bank(keys[0])[:, 0:384], ACT.Copy), keys[0])
                        elif kind == "c_decay":
                            h = arg[0]
                            act.wait_ge(c_exp_in, h + 1)
                            a.did(apply(c_l[:, h % 4, :], c_l[:, h % 4, :], ACT.Exp), c_exp)
                        elif kind == "c_y":
                            t = arg[0]
                            if t:
                                act.wait_ge(c_gated, t)
                            full(act, keys[2])
                            a.read(apply(c_e2[:, :], bank(keys[2])[:, :], ACT.Exp), keys[2])
                        elif kind == "c_square":
                            j = arg[0]
                            full(act, ("c_state", 2, 0))
                            for t in (2 * j, 2 * j + 1):
                                act.wait_ge(c_gated, t + 1)
                                a.did(apply(c_sqs[:, t, :], yT[:, 4 + t, :], ACT.Square), c_sq)
                        elif kind == "c_norm":
                            j = arg[0]
                            full(act, keys[0])
                            a.read(apply(c_sqs[:, 2 * j, :], bank(keys[0])[:, :], ACT.Sqrt, bias=eps[:, 0:1],
                                         scale=1.0 / 256), keys[0])
                        elif kind == "g_gate":
                            for t in range(2):
                                was_read(act, keys[t])
                            a.did(apply(g_d[:, :], g_b[:, :], ACT.Abs))
                            a.settle()
                            a.did(apply(g_d[:, :], g_d[:, :], ACT.Exp, scale=-1.0))
                            a.settle()
                            a.did(apply(g_d[:, :], g_d[:, :], ACT.Ln, bias=1.0), g_ln)
                        elif kind == "g_decay":
                            last = g_b[:, :].rearrange("p (n b) -> p n b", b=P)[:, :, P - 1]
                            act.wait_ge(g_diff, 1)
                            a.did(apply(g_d[:, :], g_d[:, :], ACT.Exp, scale=1.0 / 16), g_exp)
                            a.did(apply(g_dec[:, :, :].rearrange("p a b -> p (a b)"), last, ACT.Exp,
                                        scale=1.0 / 16), g_exp)
                            a.did(apply(g_qb[:, :], g_b[:, :], ACT.Exp, scale=1.0 / 16), g_exp)
                        elif kind == "g_ktok":
                            for t in range(2):
                                full(act, keys[t])
                                a.read(apply(g_kt[:, t, :], bank(keys[t])[:, 0:384], ACT.Copy), keys[t])
                        elif kind == "g_prep":
                            act.wait_ge(g_diff, arg[0] + 2)
                            a.did(apply(g_d[:, :], g_d[:, :], ACT.Exp, scale=1.0 / 16), g_exp)
                        elif kind == "g_out":
                            h = arg[0]
                            full(act, keys[0])
                            merged(act)
                            a.read(apply(g_o[:, h, :], bank(keys[0])[:, :], ACT.Copy), keys[0])
                            a.settle()
                            a.did(apply(g_sqs[:, h, :], g_o[:, h, :], ACT.Square), g_sq)
                        elif kind == "g_norm":
                            full(act, keys[0])
                            a.read(apply(g_att[:, arg[0], :], bank(keys[0])[:, :], ACT.Sqrt, bias=eps[:, 0:1],
                                         scale=1.0 / P), keys[0])
                        elif kind == "a_s":
                            p = arg[0]
                            st = a_st[:, p % 2, :]
                            act.wait_ge(a_max, p + 1)
                            act.wait_ge(g_done, 4)
                            if p >= 2:
                                full(act, ("a_pt", p - 2, 1))
                            for par in range(2):
                                for t in range(4):
                                    h = 2 * t + par
                                    ins = apply(a_p[:, p % 2, h * P:(h + 1) * P], bank(keys[par])[:, t * P:(t + 1) * P],
                                                ACT.Exp, bias=st[:, 8 + h:9 + h], scale=0.125,
                                                accum_out=st[:, 24 + h:25 + h])
                                a.read(ins, keys[par])
                            a.did(apply(st[:, 16:24], st[:, 16:24], ACT.Exp), a_exp)
                        elif kind == "a_pt":
                            p = arg[0]
                            if p >= 2:
                                full(act, ("a_pv", p - 2, 0))
                            full(act, keys[0])
                            a.read(apply(a_pt[:, p % 2, 0:512], bank(keys[0])[:, :], ACT.Copy), keys[0])
                        elif kind == "rows_split":
                            act.wait_ge(rows_ready, 1)
                            for _, hi, _, row in row_parts:
                                a.did(apply(hi, row, ACT.Copy), row_hi)
                        elif kind == "y_split":
                            act.wait_ge(m_done, 4)
                            act.wait_ge(c_done, 4)
                            full(act, ("g_out", 3, 0))
                            for k in (range(8) if arg[0] == 0 else range(8, N_EARLY)):
                                if k >= 8:
                                    act.wait_ge(g_done, k - 7)
                                a.did(apply(y_hi[:, Y_SLOT[k], :], yT[:, k, :], ACT.Copy), y_hi_ready)
                        elif kind == "a_pv":
                            p = arg[0]
                            was_read(act, keys[0])
                            tk = slice(p * P, (p + 1) * P)
                            a.did(apply(y_hi[:, 0:4, tk], yT[:, 12:16, tk], ACT.Copy), y_hi_ready)
                        for i in after:
                            split(i)

                @block.gpsimd
                def _(pool):
                    q = Line(pool, pool_order)

                    def split(i):
                        n = WIDTH.get(SPLITS[i], TILE_W)
                        pool.wait_ge(w_hi_ready, i + 1)
                        at = i % SPLIT_RING
                        q.did(pool.tensor_tensor(w_lo[:, at, 0:n], ring[:, i % RING, 0:n],
                                                 w_hi[:, at, 0:n].bitcast(F32), ALU.subtract), w_lo_ready)

                    for step in SCHEDULE:
                        kind, arg = step[0], step[1:]
                        keys = tiles_of(step)
                        q.settle()
                        if kind == "modulate":
                            pool.wait_ge(rstd, 1)
                            for t in POOL_SCALES:
                                q.did(pool.tensor_tensor(hT[:, t, :], xT[:, t, :], scr_t[:, 1, :], ALU.mult), x_rstd)
                        for i in next_splits(step)[0] + (list(range(SPLIT_RING)) if kind == "modulate" else []):
                            split(i)
                        if kind == "rope":
                            i = ROPES[arg]
                            full(pool, keys[0])
                            w = scr_in[:, i % 2, 3:3 + SEQ]
                            q.did(pool.tensor_tensor(w, w, cos[:, :], ALU.mult), rope_cos)
                        elif kind == "m_qk":
                            h = arg[0]
                            pool.wait_ge(m_exp, h + 1)
                            w = m_w[:, h % 2, :].rearrange("p (a b) -> p a b", a=NC)
                            q.did(pool.tensor_tensor(w, w, mid_bcast(causal[:, :], NC), ALU.mult), m_masked)
                        elif kind == "m_state" and arg[0]:
                            p = arg[0]
                            carry = edge_e[:, p, 4:8]
                            was_read(pool, ("m_state", p - 1, 0))
                            was_read(pool, ("m_state", p - 1, 1))
                            q.did(pool.tensor_tensor(m_cs[:, p, :].rearrange("p (a b) -> p a b", a=4),
                                                     m_cs[:, p - 1, :].rearrange("p (a b) -> p a b", a=4),
                                                     bcast(carry, P), ALU.mult), m_decayed)
                            q.did(pool.tensor_tensor(m_ns[:, p, :], m_ns[:, p - 1, :], carry, ALU.mult), m_decayed)
                        elif step == ("c_cb", 0):
                            pool.wait_ge(m_done, 4)
                            q.did(pool.tensor_copy(c_pairs[64:128, :, :].rearrange("p t (e n) -> p (t e) n", e=2),
                                                   bcast(sel[64:128, :].bitcast(F32), 64)), c_pairs_ready)
                        elif kind == "c_x" and arg[0] < 3:
                            p = arg[0]
                            was_read(pool, keys[0])
                            q.did(pool.tensor_tensor(c_xdd[:, p, :].rearrange("p (a b) -> p a b", a=8),
                                                     c_xdt[:, p, :].rearrange("p (a b) -> p a b", a=8),
                                                     bcast(edge_e[:, p, 16:24], 64), ALU.mult), c_xdd_s)
                        elif kind == "c_state" and arg[0]:
                            p = arg[0]
                            was_read(pool, ("c_state", p - 1, 0))
                            q.did(pool.tensor_tensor(c_ss[:, p, :].rearrange("p (a b) -> p a b", a=8),
                                                     c_ss[:, p - 1, :].rearrange("p (a b) -> p a b", a=8),
                                                     bcast(edge_e[:, p, 8:16], 64), ALU.mult), c_decayed)
                        elif kind == "c_decay":
                            h = arg[0]
                            pool.wait_ge(c_exp, h + 1)
                            was_read(pool, ("c_cb", h // 4, 0))
                            q.did(pool.tensor_tensor(c_l[:, h % 4, :], c_l[:, h % 4, :], c_cb[:, h // 4, :], ALU.mult),
                                  c_l_s)
                        elif kind == "g_decay":
                            pool.wait_ge(c_done, 4)
                            q.did(pool.memset(g_s[:, :, :], 0.0), g_kd)
                            pool.wait_ge(g_exp, 3)
                            was_read(pool, ("proj", "gk", 1, 0))
                            kk = g_k[:, :, :].rearrange("p a b -> p (a b)")
                            qq = g_q[:, :, :].rearrange("p a b -> p (a b)")
                            q.did(pool.tensor_tensor(g_g[:, 0, :], kk, g_d[:, :], ALU.mult), g_kd)
                            q.did(pool.tensor_tensor(g_qb[:, :], qq, g_qb[:, :], ALU.mult), g_kd)
                        elif kind == "g_prep":
                            i = arg[0]
                            b = LEVELS[i]
                            pool.wait_ge(g_exp, 4 + i)
                            full(pool, ("g_level", i - 2, 1) if i >= 2 else ("g_ktok", 1))

                            def first(v):
                                return v.rearrange("p (n b) -> p n b", b=2 * b)[:, :, 0:b]

                            kk = g_k[:, :, :].rearrange("p a b -> p (a b)")
                            q.did(pool.tensor_tensor(first(g_g[:, i % 2, :]), first(kk), first(g_d[:, :]), ALU.mult),
                                  g_key)
                        elif kind == "a_s":
                            p = arg[0]
                            pool.wait_ge(a_rden, p + 1)
                            w = a_p[:, p % 2, :].rearrange("p (a b) -> p a b", a=8)
                            q.did(pool.tensor_tensor(w, w, bcast(a_st[:, p % 2, 32:40], P), ALU.mult), a_prob)
                        elif kind == "rows_split":
                            for i, (_, hi, lo, row) in enumerate(row_parts):
                                pool.wait_ge(row_hi, i + 1)
                                q.did(pool.tensor_tensor(lo, row, hi.bitcast(F32), ALU.subtract), row_lo)
                        elif kind == "y_split":
                            for k in (range(8) if arg[0] == 0 else range(8, N_EARLY)):
                                pool.wait_ge(y_hi_ready, k + 1)
                                q.did(pool.tensor_tensor(y_lo[:, k, :], yT[:, k, :], y_hi[:, Y_SLOT[k], :].bitcast(F32),
                                                         ALU.subtract), y_ready)
                        elif kind == "a_pv":
                            p = arg[0]
                            tk = slice(p * P, (p + 1) * P)
                            pool.wait_ge(y_hi_ready, N_EARLY + p + 1)
                            q.did(pool.tensor_tensor(y_lo[:, 12:16, tk], yT[:, 12:16, tk],
                                                     y_hi[:, 0:4, tk].bitcast(F32), ALU.subtract), y_ready)
                        elif kind == "out2" and 0 < arg[0] < KT_IN - 1:
                            j = arg[0]
                            pool.wait_ge(squares, j + 1)
                            q.did(pool.tensor_tensor(r2[:, 0, :], r2[:, 0, :], square_of(j), ALU.add), squares_sum)
                        for i in next_splits(step)[1]:
                            split(i)

                @block.vector
                def _(dve):
                    v = Line(dve, vec_order)

                    def col(name, i=0):
                        return cols[:, COL[name] + i:COL[name] + i + 1]

                    def chunks(ap):
                        return ap.rearrange("p (a b) -> p a b", a=NC)

                    v.did(dve.reciprocal(scr_t[:, 1, :], scr_t[:, 0, :]), rstd)
                    dve.wait_ge(layer_in, 32)
                    for step in SCHEDULE:
                        kind, arg = step[0], step[1:]
                        keys = tiles_of(step)
                        v.settle()
                        o = bank(keys[0]) if keys else None
                        if kind == "ada":
                            j = arg[0]
                            if j < ADA_NEXT:
                                dve.wait_ge(ada_next_w[j % 2], 16 * (j // 2 + 1))
                            else:
                                dve.wait_ge(ada_gate_w[j - ADA_NEXT], 16)
                            if 2 <= j < ADA_NEXT:
                                full(dve, ("ada_col", j - 2, 0))
                            v.sum_slab(dve, ada_slab(j), two_sums(j), ada_sum)
                        elif kind == "ada_col":
                            i = arg[0]
                            full(dve, keys[0])
                            v.read(dve.tensor_tensor(mod[:, 2 * i:2 * i + 2], o[:, 0:2],
                                                     cols[:, COL["b_ada"] + 2 * i:COL["b_ada"] + 2 * i + 2], ALU.add),
                                   keys[0])
                        elif kind == "modulate":
                            v.did(dve.scalar_tensor_tensor(factor[:, :], mod[:, 8:16], 1.0,
                                                           cols[:, COL["norm_g"]:COL["norm_g"] + 8], ALU.add, ALU.mult),
                                  factor_ready)
                            v.settle()
                            for t in range(KT_IN + 1):
                                if t < POOL_SCALES[0]:
                                    v.did(dve.scalar_tensor_tensor(hT[:, t, :], xT[:, t, :], factor[:, t:t + 1],
                                                                   scr_t[:, 1, :], ALU.mult, ALU.mult), x_scaled)
                                if t:
                                    dve.wait_ge(h_hi_ready, t)
                                    v.did(dve.scalar_tensor_tensor(hT_lo[:, t - 1, :], hT[:, t - 1, :], mod[:, t - 1:t],
                                                                   hT_hi[:, t - 1, :].bitcast(F32),
                                                                   ALU.add, ALU.subtract), h_ready)
                            v.did(dve.tensor_scalar(half_b, cols[:, COL["conv_b"]:COL["conv_b"] + 16], 0.5, None, ALU.mult))
                            v.did(dve.tensor_scalar(half_mg, cols[:, COL["m_g"]:COL["m_g"] + 4], 0.5, None, ALU.mult))
                            v.did(dve.tensor_scalar(neg_sinks, cols[:, COL["sinks"]:COL["sinks"] + 8], -1.0, None, ALU.mult))
                            dve.wait_ge(a_log_exp, 1)
                            v.did(dve.tensor_scalar(a_col, small[0:8, 29:30], -1.0, None, ALU.mult))
                        elif kind == "proj" and arg[0] == "gate":
                            full(dve, keys[0])
                            v.read(dve.tensor_scalar(gate_x[:, :], o[:, :], col("gate_b"), None, ALU.add), keys[0])
                            v.settle()
                        elif kind == "proj" and arg in SILUS:
                            name, t = arg
                            u = SILUS[arg]
                            was_read(dve, keys[0])
                            acc = scr_acc[:, u % 2, :]
                            if arg in CONVS:
                                i, ch = CONVS[arg], CONV_TILE[arg]
                                src = scr_in[:, i % 2, :]
                                v.did(dve.tensor_scalar(acc, src[:, 0:SEQ], col("conv_w", 4 * ch),
                                                        half_b[:, ch:ch + 1], ALU.mult, ALU.add))
                                for k in range(1, 4):
                                    v.settle()
                                    v.did(dve.scalar_tensor_tensor(acc, src[:, k:k + SEQ], col("conv_w", 4 * ch + k),
                                                                   acc, ALU.mult, ALU.add),
                                          conv_acc if k == 3 else None)
                                dst = {"mq": m_q[:, t, :], "mk": m_k[:, t, :], "xs": c_x[:, t, :],
                                       "bc": r2[:, t, :]}[name]
                                dve.wait_ge(conv_tanh, i + 1)
                            else:
                                dst = yT[:, Y_TILE[Z_OF[name]] + t, :]
                            v.did(dve.scalar_tensor_tensor(dst, scr_t[:, u % 2, :], 1.0, acc, ALU.add, ALU.mult),
                                  silu_out)
                        elif kind == "rows":
                            dve.wait_ge(gate_ln, 1)
                            ln = scr_t[:, 1, :]
                            lf, b, da = scr_acc[32:36, 0, :], scr_acc[32:36, 1, :], scr_acc[0:8, 1, :]
                            ig = gate_x[R_I:R_I + 4, :]
                            mprev = small[32:36, 48:52]
                            v.did(dve.scalar_tensor_tensor(dtm[0:8, :], gate_x[R_DT:R_DT + 8, :], 0.0, ln[0:8, :],
                                                           ALU.max, ALU.add))
                            v.did(dve.scalar_tensor_tensor(lf, gate_x[R_F:R_F + 4, :], 0.0, ln[R_F:R_F + 4, :],
                                                           ALU.min, ALU.subtract))
                            v.did(dve.memset(mprev[:, 0:1], 0.0))
                            v.settle()
                            v.did(dve.tensor_tensor_scan(m_max, lf, ig, 0.0, ALU.add, ALU.max))
                            v.did(dve.tensor_tensor_scan(b, reset[32:36, :], lf, 0.0, ALU.mult, ALU.add))
                            v.did(dve.tensor_scalar(da, dtm[0:8, :], a_col, None, ALU.mult))
                            v.settle()
                            v.did(dve.tensor_tensor_scan(rows[T_ACS:T_ACS + 8, :], reset[0:8, :], da, 0.0,
                                                         ALU.mult, ALU.add))
                            v.did(dve.tensor_tensor(rows[T_C:T_C + 4, :], ig, b, ALU.subtract))
                            v.did(dve.tensor_tensor(rows[T_R:T_R + 4, :], b, m_max, ALU.subtract))
                            v.did(dve.tensor_copy(mprev[:, 1:4], chunks(m_max)[:, 0:3, P - 1]))
                            v.settle()
                            v.did(dve.tensor_tensor(chunks(rows[T_R2:T_R2 + 4, :]), chunks(rows[T_R:T_R + 4, :]),
                                                    bcast(mprev, P), ALU.add), rows_ready)
                        elif kind == "rope":
                            i = ROPES[arg]
                            w = scr_in[:, i % 2, 3:3 + SEQ]
                            dst = scr_t[:, 0, :] if i == 0 else a_q[:, i - 1, :]
                            full(dve, keys[0])
                            v.read(dve.tensor_tensor(dst, o[:, :], sin[:, :], ALU.mult), keys[0])
                            dve.wait_ge(rope_cos, i + 1)
                            v.settle()
                            if i:
                                v.did(dve.tensor_tensor(dst, dst, w, ALU.add), rope_out)
                            else:
                                for g in range(2):
                                    half = slice(64 * g, 64 * g + 64)
                                    v.did(dve.tensor_tensor(kdup[half, g, WIN:], dst[half, :], w[half, :], ALU.add))
                                v.settle()
                                v.did(dve.tensor_copy(kdup[64:128, 0, WIN:], kdup[0:64, 0, WIN:]))
                                v.did(dve.tensor_copy(kdup[0:64, 1, WIN:], kdup[64:128, 1, WIN:]), rope_out)
                        elif kind == "edge":
                            full(dve, keys[0])
                            was_read(dve, ("tok", 1))
                            was_read(dve, ("tok", 0))
                            e = chunks(o[:, :])
                            v.did(dve.tensor_tensor(edge[:, :, 0:4], e[:, :, T_R:T_R + 4], tok[:, :, T_C:T_C + 4],
                                                    ALU.add))
                            v.did(dve.tensor_copy(edge[:, :, 4:8], e[:, :, T_R2:T_R2 + 4]))
                            v.did(dve.tensor_copy(edge[:, :, 8:16], e[:, :, T_ACS:T_ACS + 8]))
                            v.read(dve.tensor_tensor(edge[:, :, 16:24], e[:, :, T_ACS:T_ACS + 8],
                                                     tok[:, :, T_ACS:T_ACS + 8], ALU.subtract), keys[0])
                        elif kind == "mk_tok":
                            dve.wait_ge(edge_exp, 1)
                            for p in range(3):
                                full(dve, keys[p])
                                v.read(dve.tensor_tensor(chunks(m_kw[:, p, :]), chunks(bank(keys[p])[:, :]),
                                                         bcast(edge_e[:, p, 0:4], P), ALU.mult), keys[p])
                        elif kind == "m_qk":
                            h = arg[0]
                            w = m_w[:, h % 2, :]
                            full(dve, keys[1])
                            v.read(dve.tensor_tensor(chunks(w), chunks(bank(keys[1])[:, :]),
                                                     bcast(tok[:, :, T_C + h], P), ALU.add), keys[1])
                            v.settle()
                            v.did(dve.tensor_scalar(w, w, 0.0, None, ALU.min), m_exp_in)
                        elif kind == "m_decay":
                            h = arg[0]
                            dve.wait_ge(m_masked, h + 1)
                            full(dve, ("m_qk", h, 0))
                            v.read(dve.scalar_tensor_tensor(m_pt[:, h % 2, :], bank(("m_qk", h, 0))[:, :], P ** -0.5,
                                                            m_w[:, h % 2, :], ALU.mult, ALU.mult), ("m_qk", h, 0))
                            was_read(dve, keys[0])
                            v.did(dve.scalar_tensor_tensor(m_qw[:, h % 2, :], m_q[:, h, :], P ** -0.5,
                                                           m_qw[:, h % 2, :], ALU.mult, ALU.mult), m_query)
                        elif kind == "m_state":
                            p = arg[0]
                            if p:
                                dve.wait_ge(m_decayed, 2 * p)
                            for dst, key, n in ((m_cs, keys[0], 512), (m_ns, keys[1], 4)):
                                full(dve, key)
                                src = bank(key)[:, 0:n]
                                v.read(dve.tensor_tensor(dst[:, p, :], src, dst[:, p, :], ALU.add) if p else
                                       dve.tensor_copy(dst[:, p, :], src), key)
                        elif kind == "m_num":
                            h = arg[0]
                            was_read(dve, keys[1])
                            was_read(dve, ("m_decay", h, 1))
                            v.did(dve.tensor_tensor(m_ad[:, :], m_ad[:, :], m_em[:, h % 2, :], ALU.max))
                            v.settle()
                            v.did(dve.reciprocal(m_ad[:, :], m_ad[:, :]))
                            v.settle()
                            full(dve, keys[0])
                            v.read(dve.tensor_tensor(m_q[:, h, :], o[:, :], m_ad[:, :], ALU.mult), keys[0])
                            v.settle()
                            was_read(dve, ("proj", "mo", h, 0))
                            v.did(dve.scalar_tensor_tensor(m_q[:, h, :], m_o[:, h, :], 1.0, m_q[:, h, :],
                                                           ALU.add, ALU.mult), m_h)
                        elif kind == "m_norm":
                            h = arg[0]
                            was_read(dve, keys[0])
                            v.did(dve.reciprocal(m_k[:, h, :], m_k[:, h, :]))
                            v.settle()
                            v.did(dve.scalar_tensor_tensor(m_q[:, h, :], m_q[:, h, :], half_mg[:, h:h + 1],
                                                           m_k[:, h, :], ALU.mult, ALU.mult))
                            v.settle()
                            silu_done(dve, "mz", h)
                            v.did(dve.tensor_tensor(yT[:, h, :], m_q[:, h, :], yT[:, h, :], ALU.mult), m_done)
                        elif kind == "c_cb":
                            full(dve, keys[0])
                            v.read(dve.tensor_tensor(chunks(c_cb[:, arg[0], :]), chunks(o[:, :]),
                                                     mid_bcast(causal[:, :], NC), ALU.mult), keys[0])
                        elif kind == "c_x":
                            p = arg[0]
                            full(dve, keys[0])
                            v.read(dve.tensor_tensor(c_xdt[:, p, :].rearrange("p (a b) -> p a b", a=8),
                                                     o[:, :].rearrange("p (a b) -> p a b", a=8),
                                                     bcast(dt_tok[:, p, :], 64), ALU.mult), keys[0])
                        elif kind == "c_state":
                            p = arg[0]
                            full(dve, keys[0])
                            if p:
                                dve.wait_ge(c_decayed, p)
                            v.read(dve.tensor_tensor(c_ss[:, p, :], o[:, :], c_ss[:, p, :], ALU.add) if p else
                                   dve.tensor_copy(c_ss[:, p, :], o[:, :]), keys[0])
                        elif kind == "c_decay":
                            h = arg[0]
                            if h >= 4:
                                full(dve, ("c_y", (h - 4) // 2, 0))
                            full(dve, keys[0])
                            w = c_l[:, h % 4, :]
                            v.read(dve.tensor_tensor(chunks(w), chunks(o[:, :]), bcast(tok[:, :, T_ACS + h], P),
                                                     ALU.subtract), keys[0])
                            v.settle()
                            v.did(dve.tensor_scalar(w, w, 0.0, None, ALU.min), c_exp_in)
                        elif kind == "c_y":
                            t = arg[0]
                            full(dve, keys[0])
                            v.read(dve.scalar_tensor_tensor(c_tmp[:, :], c_x[:, t, :], col("ssd_d", t), o[:, :],
                                                            ALU.mult, ALU.add), keys[0])
                            was_read(dve, keys[2])
                            full(dve, keys[1])
                            v.read(dve.tensor_tensor(c_e2[:, P:], c_e2[:, P:], bank(keys[1])[:, P:], ALU.mult), keys[1])
                            v.settle()
                            v.did(dve.tensor_tensor(c_tmp[:, P:], c_tmp[:, P:], c_e2[:, P:], ALU.add))
                            v.settle()
                            silu_done(dve, "cz", t)
                            v.did(dve.tensor_tensor(yT[:, 4 + t, :], yT[:, 4 + t, :], c_tmp[:, :], ALU.mult), c_gated)
                        elif kind == "c_norm":
                            j = arg[0]
                            was_read(dve, keys[0])
                            w = c_sqs[:, 2 * j, :]
                            v.did(dve.reciprocal(w, w))
                            v.settle()
                            for t in (2 * j, 2 * j + 1):
                                v.did(dve.scalar_tensor_tensor(yT[:, 4 + t, :], yT[:, 4 + t, :], col("ssd_g", t), w,
                                                               ALU.mult, ALU.mult), c_done)
                        elif kind == "g_gate":
                            dve.wait_ge(c_done, 4)
                            for t in range(2):
                                full(dve, keys[t])
                                v.read(dve.tensor_scalar(g_b[:, t * SEQ:(t + 1) * SEQ], bank(keys[t])[:, :],
                                                         col("gla_b", t), None, ALU.add), keys[t])
                        elif kind == "g_scan":
                            dve.wait_ge(g_ln, 1)
                            v.did(dve.scalar_tensor_tensor(g_g[:, 0, :], g_b[:, :], 0.0, g_d[:, :],
                                                           ALU.min, ALU.subtract))
                            v.settle()
                            for t in range(2):
                                tk = slice(t * SEQ, (t + 1) * SEQ)
                                v.did(dve.tensor_tensor_scan(g_b[:, tk], reset[:, :], g_g[:, 0, tk], 0.0,
                                                             ALU.mult, ALU.add))
                            v.settle()
                            b = g_b[:, :].rearrange("p (n b) -> p n b", b=P)
                            v.did(dve.tensor_tensor(g_d[:, :].rearrange("p (n b) -> p n b", b=P),
                                                    bcast(b[:, :, P - 1], P), b, ALU.subtract), g_diff)
                        elif kind == "g_diag":
                            for h in range(4):
                                full(dve, keys[h])
                                v.read(dve.tensor_tensor(chunks(g_att[:, h, :]), chunks(bank(keys[h])[:, :]),
                                                         mid_bcast(ident[:, :], NC), ALU.mult), keys[h])
                        elif kind == "g_state":
                            p = arg[0]
                            full(dve, keys[0])
                            dve.wait_ge(g_kd, 1)
                            dve.wait_ge(g_exp, 2)
                            for h in range(4):
                                half, hd = slice(64 * (h % 2), 64 * (h % 2) + 64), slice(h * P, (h + 1) * P)
                                if p:
                                    ins = dve.scalar_tensor_tensor(g_s[half, p, hd], g_s[half, p - 1, hd],
                                                                   g_dec[half, h // 2, p:p + 1], o[half, hd],
                                                                   ALU.mult, ALU.add)
                                else:
                                    ins = dve.tensor_copy(g_s[half, p, hd], o[half, hd])
                                if h == 3:
                                    v.read(ins, keys[0])
                                else:
                                    v.did(ins)
                        elif kind == "g_prep":
                            i = arg[0]
                            b = LEVELS[i]
                            dve.wait_ge(g_kd, 2) if i == 0 else dve.wait_ge(g_key, i)
                            bb = g_b[:, :].rearrange("p (n b) -> p n b", b=2 * b)
                            d = g_d[:, :].rearrange("p (n b) -> p n b", b=2 * b)
                            mid = bcast(bb[:, :, b - 1], b)
                            v.did(dve.tensor_tensor(d[:, :, 0:b], mid, bb[:, :, 0:b], ALU.subtract))
                            v.did(dve.tensor_tensor(d[:, :, b:2 * b], bb[:, :, b:2 * b], mid, ALU.subtract), g_diff)
                            dve.wait_ge(g_exp, 4 + i)
                            full(dve, ("g_level", i - 2, 1) if i >= 2 else ("g_ktok", 1))

                            def second(x):
                                return x.rearrange("p (n b) -> p n b", b=2 * b)[:, :, b:2 * b]

                            qq = g_q[:, :, :].rearrange("p a b -> p (a b)")
                            v.did(dve.tensor_tensor(second(g_g[:, i % 2, :]), second(qq), second(g_d[:, :]), ALU.mult),
                                  g_query)
                        elif kind == "g_merge":
                            i = arg[0]
                            b = LEVELS[i]
                            mask = levelmask[:, i, :].rearrange("p (m b) -> p m b", b=b)
                            mask = mask.unsqueeze(1).broadcast_to([P, 2, 256 // b, b])
                            for par in range(2):
                                key = ("g_level", i, par)
                                full(dve, key)
                                dst = g_att[:, :, :].rearrange("p (t e) n -> p t e n", e=2)[:, :, par, :]
                                dst = dst.rearrange("p t (m b) -> p t m b", b=2 * b)[:, :, :, b:2 * b]
                                src = bank(key)[:, :].rearrange("p (t m b) -> p t m b", t=2, b=b)
                                v.read(dve.copy_predicated(dst, mask, src), key)
                        elif kind == "g_norm":
                            h = arg[0]
                            was_read(dve, keys[0])
                            w = g_att[:, h, :]
                            v.did(dve.reciprocal(w, w))
                            v.settle()
                            v.did(dve.scalar_tensor_tensor(w, g_o[:, h, :], col("gla_g"), w, ALU.mult, ALU.mult))
                            v.settle()
                            silu_done(dve, "gz", h)
                            v.did(dve.tensor_tensor(yT[:, 8 + h, :], w, yT[:, 8 + h, :], ALU.mult), g_done)
                        elif kind == "a_s":
                            p = arg[0]
                            st = a_st[:, p % 2, :]
                            mx = st[:, 0:8].rearrange("p (t e) -> p t e", e=2)
                            for par in range(2):
                                full(dve, keys[par])
                                v.did(dve.tensor_reduce(mx[:, :, par], chunks(bank(keys[par])[:, :]), AX_X, ALU.max))
                            v.settle()
                            v.did(dve.scalar_tensor_tensor(st[:, 8:16], st[:, 0:8], -0.125, neg_sinks,
                                                           ALU.mult, ALU.min))
                            v.settle()
                            v.did(dve.tensor_tensor(st[:, 16:24], cols[:, COL["sinks"]:COL["sinks"] + 8],
                                                    st[:, 8:16], ALU.add), a_max)
                            dve.wait_ge(a_exp, p + 1)
                            v.did(dve.tensor_tensor(st[:, 32:40], st[:, 16:24], st[:, 24:32], ALU.add))
                            v.settle()
                            v.did(dve.reciprocal(st[:, 32:40], st[:, 32:40]), a_rden)
                        elif kind == "a_pt":
                            p = arg[0]
                            full(dve, keys[1])
                            if p >= 2:
                                full(dve, ("a_pv", p - 2, 0))
                            v.read(dve.tensor_copy(a_pt[:, p % 2, 512:1024], bank(keys[1])[:, :]), keys[1])
                        elif kind == "a_pv":
                            p = arg[0]
                            full(dve, keys[0])
                            z = yT[:, 12:16, p * P:(p + 1) * P]
                            v.read(dve.tensor_tensor(z, chunks(o[:, :]), z, ALU.mult), keys[0])
                        elif kind in ("out1", "out2"):
                            j, key = arg[0], (kind, arg[0], 0)
                            full(dve, key)
                            dve.wait_ge(x_back, 16)
                            v.read(dve.scalar_tensor_tensor(xT[:, j, :], bank(key)[:, :], mod[:, 16 + j:17 + j],
                                                            xT[:, j, :], ALU.mult, ALU.add), key)

            numbers = sorted(s.num for s in layer)
            assert numbers == list(range(numbers[0], numbers[-1] + 1))
            nc.gpsimd.sem_clear(range(numbers[0], numbers[-1] + 1))
            nc.all_engine_barrier()

        with nc.Block() as block:
            @block.vector
            def _(dve):
                dve.reciprocal(scr_t[:, 1, :], scr_t[:, 0, :]).then_inc(vec_order, 1)
                dve.wait_ge(vec_order, 1)
                for t in range(KT_IN):
                    dve.scalar_tensor_tensor(hT[:, t, :], xT[:, t, :], final_g[:, t:t + 1], scr_t[:, 1, :],
                                             ALU.mult, ALU.mult).then_inc(x_scaled, 1)

            @block.sync
            def _(sp):
                for t in range(KT_IN):
                    sp.wait_ge(x_scaled, t + 1)
                    sp.dma_start(out[:, t, :], hT[:, t, :]).then_inc(out_done, 16)
                sp.wait_ge(x_stored, 16 * KT_IN)
                sp.wait_ge(out_done, 16 * KT_IN)



def constants():
    c = np.zeros((P, 906), np.float32)
    c[:, 898:906] = np.arange(P)[:, None] % 32 == np.arange(8)[None, :]
    c[:, 0:128] = np.eye(P)
    c[:, 128:256] = np.triu(np.ones((P, P)))
    for head in (0, 64):
        for d in range(ROPE_DIM // 2):
            c[head + d + ROPE_DIM // 2, 256 + head + d] = -1.0
            c[head + d, 256 + head + d + ROPE_DIM // 2] = 1.0
    c[:, 384:896] = (np.arange(SEQ) % C != 0).astype(np.float32)
    inv = np.float32(ROPE_THETA) ** (-np.arange(0, ROPE_DIM, 2, dtype=np.float32) / np.float32(ROPE_DIM))
    for head in (0, 64):
        for d in range(ROPE_DIM):
            c[head + d, 896] = inv[d % (ROPE_DIM // 2)]
    masks = np.zeros((P, len(LEVELS), C // 2), np.float32)
    s = np.arange(P)
    for i, b in enumerate(LEVELS):
        n = np.arange(P // (2 * b))
        m = (s[:, None] // (2 * b) == n[None, :]) & (s[:, None] % (2 * b) < b)
        masks[:, i, :] = np.repeat(m, b, axis=1)
    return c, masks


def feature_tiles(w):
    k, n = w.shape[0] // P, w.shape[1] // P
    return w.reshape(k, P, n, P).transpose(2, 1, 0, 3).reshape(n, P, k * P)


def pack_ada(w_ada):
    t = w_ada.reshape(DEPTH, KT_IN, P, ADA_ALL, 256).transpose(0, 3, 2, 1, 4).reshape(DEPTH, ADA_ALL, P, 2 * TILE_W)
    return (np.ascontiguousarray(t[0, :ADA_NEXT]),
            np.ascontiguousarray(np.concatenate([t[1:, :ADA_NEXT], np.zeros_like(t[:1, :ADA_NEXT])])),
            np.ascontiguousarray(t[:, ADA_NEXT:]))


def pack_weights(w_in, w_out):
    tiles = np.zeros((DEPTH, len(SPLITS), P, TILE_W), np.float32)
    names = {"xs": (IN_OFF["xbc"], 512), "bc": (IN_OFF["xbc"] + 512, 512)}
    for l in range(DEPTH):
        gates = np.zeros((D_MODEL, P), np.float32)
        for at, name, n in ((R_DT, "dt", 8), (R_I, "mi", 4), (R_F, "mf", 4), (R_LR, "lr", 16)):
            gates[:, at:at + n] = w_in[l, :, IN_OFF[name]:IN_OFF[name] + n]
        tiles[l, SPLIT_NO[("gate", 0)]] = feature_tiles(gates)[0]
        for name, n in (("ak", 1), ("av", 1), ("gq", 2), ("gk", 2), ("mq", 4), ("mk", 4), ("mo", 4), ("mz", 4),
                        ("xs", 4), ("bc", 4), ("cz", 4), ("gz", 4), ("aq", 4), ("az", 4)):
            at = names[name][0] if name in names else IN_OFF[name]
            for t, w in enumerate(feature_tiles(w_in[l, :, at:at + n * P])):
                tiles[l, SPLIT_NO[(name, t)]] = w
        for name in ("mv", "gv"):
            w = w_in[l, :, IN_OFF[name]:IN_OFF[name] + 512].reshape(4, 2, P, 512)
            for q in range(4):
                tiles[l, SPLIT_NO[(name, q)]] = w[q].transpose(1, 0, 2).reshape(P, TILE_W)
        order = np.concatenate([w_out[l, Y_ROW[b]:Y_ROW[b] + 512] for b in ORDER], axis=0)
        early = feature_tiles(order[0:N_EARLY * P])
        late = feature_tiles(order[N_EARLY * P:])
        for j in range(8):
            tiles[l, SPLIT_NO[("o1", j, 0)]] = early[j][:, 0:TILE_W]
            tiles[l, SPLIT_NO[("o1", j, 1)], :, 0:512] = early[j][:, TILE_W:]
        for j in range(4):
            tiles[l, SPLIT_NO[("o2", j)]] = late[2 * j:2 * j + 2].transpose(1, 0, 2).reshape(P, TILE_W)
    return tiles


def pack_columns(a):
    out = np.zeros((DEPTH, P, N_COLS), np.float32)

    def put(name, v):
        out[:, :, COL[name]:COL[name] + v.shape[2]] = v

    def per_feature(v):
        return v.reshape(DEPTH, -1, P).transpose(0, 2, 1)

    put("norm_g", per_feature(a["norm_g"]))
    put("b_ada", per_feature(a["b_ada"]))
    out[:-1, :, COL["b_ada"]:COL["b_ada"] + 16] = out[1:, :, COL["b_ada"]:COL["b_ada"] + 16]
    put("gla_b", per_feature(a["gla_b_gate"]))
    put("gla_g", per_feature(a["gla_norm_g"]))
    put("ssd_g", per_feature(a["ssd_norm_g"]))
    put("m_g", per_feature(a["mlstm_norm_g"]))
    put("conv_b", np.concatenate([per_feature(a["ssd_conv_b"]), per_feature(a["mlstm_conv_b"])], axis=2))
    for at, name in ((0, "ssd_conv_w"), (32, "mlstm_conv_w")):
        w = a[name].reshape(DEPTH, 4, 8, P).transpose(0, 3, 2, 1).reshape(DEPTH, P, 32)
        out[:, :, COL["conv_w"] + at:COL["conv_w"] + at + 32] = w
    put("ssd_d", per_feature(np.repeat(a["ssd_d"], 64, axis=1)))
    g = COL["gate_b"]
    out[:, R_DT:R_DT + 8, g] = a["ssd_dt_bias"]
    out[:, R_I:R_I + 4, g] = a["mlstm_i_bias"]
    out[:, R_F:R_F + 4, g] = a["mlstm_f_bias"]
    out[:, 0:8, COL["a_log"]] = a["ssd_a_log"]
    out[:, :, COL["sinks"]:COL["sinks"] + 8] = a["swa_sinks"][:, None, :]
    return out


def host_arrays(inputs):
    a = {k: np.asarray(v) for k, v in inputs.items()}
    consts, masks = constants()
    ada_first, ada_next, ada_gate = pack_ada(a["w_ada"])
    return {
        "xT": np.ascontiguousarray(a["x"][0].T.reshape(KT_IN, P, SEQ).transpose(1, 0, 2)),
        "c": np.ascontiguousarray(a["c"].reshape(KT_IN, P).T),
        "pos": np.ascontiguousarray(np.broadcast_to(a["positions"].reshape(1, SEQ), (P, SEQ))),
        "cols": pack_columns(a),
        "wgate": np.ascontiguousarray(a["gla_w_gate"]),
        "final": np.ascontiguousarray(a["final_g"].reshape(KT_IN, P).T),
        "ada_first": ada_first,
        "ada_next": ada_next,
        "ada_gate": ada_gate,
        "b_first": np.ascontiguousarray(a["b_ada"][0].reshape(24, P).T[:, 0:16]),
        "weights": pack_weights(a["w_in"], a["w_out"]),
        "consts": consts,
        "masks": masks,
    }


def program(nc, arrays):
    aps = [nc.dram_tensor(f"in_{k}", v.shape, mybir.dt.from_np(v.dtype), kind="ExternalInput").ap()
           for k, v in arrays.items()]
    out = nc.dram_tensor("out", (P, KT_IN, SEQ), F32, kind="ExternalOutput").ap()
    x_kept = nc.dram_tensor("x_kept", (P, KT_IN, SEQ), F32, kind="Internal").ap()
    build(nc, *aps, x_kept, out)


def kernel(**inputs):
    import concourse.bacc as bacc
    from concourse.bass_utils import run_bass_kernel_spmd

    arrays = host_arrays(inputs)
    nc = bacc.Bacc("TRN2", target_bir_lowering=False, num_devices=1)
    program(nc, arrays)
    r = run_bass_kernel_spmd(nc, [{f"in_{k}": v for k, v in arrays.items()}], core_ids=[0])
    y = r.results[0]["out"]
    return np.ascontiguousarray(y.transpose(1, 0, 2).reshape(D_MODEL, SEQ).T)[None]
```
